# Optimizing a Trainium2 kernel written in Bass

```python
import jax, jax.numpy as jnp
from jax import lax
import numpy as np
import math

D_MODEL = 1024
BATCH = 1
SEQ = 256
DEPTH = 2

CHUNK = 64
HG_HEADS = 4
HG_DK = 128
HG_W = HG_HEADS * HG_DK
RET_HEADS = 4
RET_DK = 128
RET_DV = 256
RET_QK = RET_HEADS * RET_DK
RET_V = RET_HEADS * RET_DV
ML_HEADS = 4
ML_DK = 128
ML_DV = 256
ML_QK = ML_HEADS * ML_DK
ML_V = ML_HEADS * ML_DV
CONV_W = 4
D_FF = 4 * D_MODEL
EPS = 1e-6
GATE_CAP = 15.0
ROPE_BASE = 10000.0
N_EVEN = (DEPTH + 1) // 2
N_ODD = DEPTH // 2
EVEN_IN = 4 * HG_W + 2 * RET_QK + 2 * RET_V
EVEN_OUT = HG_W + RET_V
ODD_IN = 2 * ML_QK + 2 * ML_V + 2 * ML_HEADS


def rmsnorm(x, g):
    xf = x.astype(jnp.float32)
    y = xf * lax.rsqrt(jnp.mean(xf * xf, axis=-1, keepdims=True) + EPS)
    return (y * g.astype(jnp.float32)).astype(x.dtype)

def head_rmsnorm(o, g, n_heads):
    b, s, w = o.shape
    return rmsnorm(o.reshape(b, s, n_heads, w // n_heads), g).reshape(b, s, w)

def to_chunks(x, n_heads):
    b, s, w = x.shape
    return x.reshape(b, s // CHUNK, CHUNK, n_heads, w // n_heads).transpose(1, 0, 3, 2, 4)

def gate_chunks(g):
    b, s, h = g.shape
    return g.reshape(b, s // CHUNK, CHUNK, h).transpose(1, 0, 3, 2)

def from_chunks(x):
    nc, b, h, c, d = x.shape
    return x.transpose(1, 0, 3, 2, 4).reshape(b, nc * c, h * d)

def rope(x, n_heads):
    b, s, w = x.shape
    dk = w // n_heads
    half = dk // 2
    xh = x.reshape(b, s, n_heads, dk)
    inv_freq = ROPE_BASE ** (-jnp.arange(half, dtype=jnp.float32) / half)
    ang = jnp.arange(s, dtype=jnp.float32)[:, None] * inv_freq[None, :]
    cos = jnp.cos(ang)[None, :, None, :]
    sin = jnp.sin(ang)[None, :, None, :]
    x1, x2 = xh[..., :half], xh[..., half:]
    return jnp.concatenate([x1 * cos - x2 * sin, x2 * cos + x1 * sin], axis=-1).reshape(b, s, w)

def hgrn2_scan(q, k, logf, v):
    nc, b, h, c, dk = q.shape
    dv = v.shape[-1]
    mask = jnp.tril(jnp.ones((c, c), dtype=bool))

    def step(state, inp):
        qc, kc, lfc, vc = inp
        bcum = jnp.cumsum(lfc, axis=2)
        diff = bcum[:, :, :, None, :] - bcum[:, :, None, :, :]
        decay = jnp.exp(jnp.where(mask[:, :, None], diff, -jnp.inf))
        scores = jnp.einsum('bhtd,bhsd,bhtsd->bhts', qc, kc, decay)
        out = jnp.einsum('bhts,bhsv->bhtv', scores, vc) \
            + jnp.einsum('bhtd,bhdv->bhtv', qc * jnp.exp(bcum), state)
        blast = bcum[:, :, -1, :]
        state = jnp.exp(blast)[..., None] * state \
            + jnp.einsum('bhsd,bhsv->bhdv', kc * jnp.exp(blast[:, :, None, :] - bcum), vc)
        return state, out

    init = jnp.zeros((b, h, dk, dv), jnp.float32)
    _, out = lax.scan(step, init, (q, k, logf, v))
    return out

def retention_scan(q, k, v):
    nc, b, h, c, dk = q.shape
    dv = v.shape[-1]
    mask = jnp.tril(jnp.ones((c, c), dtype=bool))
    lg = jnp.log1p(-jnp.exp2(-5.0 - jnp.arange(h, dtype=jnp.float32)))
    j = jnp.arange(c, dtype=jnp.float32)
    decay = jnp.where(mask, jnp.exp(lg[:, None, None] * (j[:, None] - j[None, :])), 0.0)
    q_decay = jnp.exp(lg[:, None] * (j + 1.0))[:, :, None]
    k_decay = jnp.exp(lg[:, None] * (c - 1.0 - j))[:, :, None]
    chunk_decay = jnp.exp(lg * c)[:, None, None]

    def step(state, inp):
        qc, kc, vc = inp
        scores = jnp.einsum('bhtd,bhsd->bhts', qc, kc) * decay
        out = jnp.einsum('bhts,bhsv->bhtv', scores, vc) \
            + jnp.einsum('bhtd,bhdv->bhtv', qc * q_decay, state)
        state = chunk_decay * state + jnp.einsum('bhsd,bhsv->bhdv', kc * k_decay, vc)
        return state, out

    init = jnp.zeros((b, h, dk, dv), jnp.float32)
    _, out = lax.scan(step, init, (q, k, v))
    return out

def mlstm_scan(q, k, v, lf, ig):
    nc, b, h, c, dk = q.shape
    dv = v.shape[-1]
    mask = jnp.tril(jnp.ones((c, c), dtype=bool))

    def step(carry, inp):
        cm, n, m = carry
        qc, kc, vc, lfc, igc = inp
        bcum = jnp.cumsum(lfc, axis=-1)
        logw = jnp.where(mask, bcum[..., :, None] - bcum[..., None, :] + igc[..., None, :], -jnp.inf)
        inter = bcum + m[..., None]
        m_row = jnp.maximum(inter, jnp.max(logw, axis=-1))
        w_intra = jnp.exp(logw - m_row[..., None])
        w_inter = jnp.exp(inter - m_row)
        scores = jnp.einsum('bhtd,bhsd->bhts', qc, kc) * w_intra
        num = jnp.einsum('bhts,bhsv->bhtv', scores, vc) \
            + w_inter[..., None] * jnp.einsum('bhtd,bhdv->bhtv', qc, cm)
        den = jnp.sum(scores, axis=-1) + w_inter * jnp.einsum('bhtd,bhd->bht', qc, n)
        out = num / jnp.maximum(jnp.abs(den), jnp.exp(-m_row))[..., None]
        blast = bcum[..., -1]
        logw_end = blast[..., None] - bcum + igc
        m_new = jnp.maximum(blast + m, jnp.max(logw_end, axis=-1))
        carry_scale = jnp.exp(blast + m - m_new)
        kw = kc * jnp.exp(logw_end - m_new[..., None])[..., None]
        cm = carry_scale[..., None, None] * cm + jnp.einsum('bhsd,bhsv->bhdv', kw, vc)
        n = carry_scale[..., None] * n + jnp.sum(kw, axis=2)
        return (cm, n, m_new), out

    init = (jnp.zeros((b, h, dk, dv), jnp.float32),
            jnp.zeros((b, h, dk), jnp.float32),
            jnp.zeros((b, h), jnp.float32))
    _, out = lax.scan(step, init, (q, k, v, lf, ig))
    return out

def causal_conv_silu(x, w, bias):
    s = x.shape[1]
    xp = jnp.pad(x, ((0, 0), (CONV_W - 1, 0), (0, 0)))
    y = sum(w[j].astype(jnp.float32) * xp[:, j:j + s, :] for j in range(CONV_W))
    return jax.nn.silu(y + bias.astype(jnp.float32))

def soft_cap(z):
    return GATE_CAP * jnp.tanh(z / GATE_CAP)

def even_mixer(h, w_in, lb, hg_norm_g, ret_norm_g, w_out):
    p = (h @ w_in).astype(jnp.float32)
    splits = [HG_W, 2 * HG_W, 3 * HG_W, 4 * HG_W, 4 * HG_W + RET_QK,
              4 * HG_W + 2 * RET_QK, 4 * HG_W + 2 * RET_QK + RET_V]
    hq, hf, hi, hgate, rq, rk, rv, rgate = jnp.split(p, splits, axis=-1)
    f = lb + (1.0 - lb) * jax.nn.sigmoid(hf)
    o_hg = from_chunks(hgrn2_scan(to_chunks(jax.nn.silu(hq), HG_HEADS), to_chunks(1.0 - f, HG_HEADS),
                                  to_chunks(jnp.log(f), HG_HEADS), to_chunks(hi, HG_HEADS)))
    o_hg = head_rmsnorm(o_hg, hg_norm_g, HG_HEADS) * jax.nn.silu(hgate)
    rq = rope(rq, RET_HEADS)
    rk = rope(rk, RET_HEADS) * RET_DK ** -0.5
    o_ret = from_chunks(retention_scan(to_chunks(rq, RET_HEADS), to_chunks(rk, RET_HEADS),
                                       to_chunks(rv, RET_HEADS)))
    o_ret = head_rmsnorm(o_ret, ret_norm_g, RET_HEADS) * jax.nn.silu(rgate)
    y = jnp.concatenate([o_hg, o_ret], axis=-1).astype(h.dtype)
    return y @ w_out

def odd_mixer(h, w_in, conv_w, conv_b, gate_b, ml_norm_g, w_out):
    p = (h @ w_in).astype(jnp.float32)
    splits = [2 * ML_QK, 2 * ML_QK + ML_V, 2 * ML_QK + 2 * ML_V, 2 * ML_QK + 2 * ML_V + ML_HEADS]
    qk, v, og, ig_pre, fg_pre = jnp.split(p, splits, axis=-1)
    qk = causal_conv_silu(qk, conv_w, conv_b)
    q, k = jnp.split(qk, 2, axis=-1)
    k = k * ML_DK ** -0.5
    gb = gate_b.astype(jnp.float32)
    ig = soft_cap(ig_pre + gb[0])
    lf = jax.nn.log_sigmoid(soft_cap(fg_pre + gb[1]))
    out = from_chunks(mlstm_scan(to_chunks(q, ML_HEADS), to_chunks(k, ML_HEADS), to_chunks(v, ML_HEADS),
                                 gate_chunks(lf), gate_chunks(ig)))
    y = (jax.nn.sigmoid(og) * head_rmsnorm(out, ml_norm_g, ML_HEADS)).astype(h.dtype)
    return y @ w_out

def sq_relu_mlp(h, w1, w2):
    return jnp.square(jax.nn.relu(h @ w1)) @ w2

def first_inputs(seed: int = 0) -> dict:
    key = jax.random.key(seed)
    ks = jax.random.split(key, 16)
    f32 = jnp.float32

    def nrm(k, shape, fan_in):
        return jax.random.normal(k, shape, f32) * fan_in ** -0.5

    x = jax.random.normal(ks[0], (BATCH, SEQ, D_MODEL), f32)
    norm_g = 1.0 + 0.05 * jax.random.normal(ks[1], (DEPTH, 4, D_MODEL), f32)
    hg_lower_bound = 0.5 * jax.random.normal(ks[2], (DEPTH + 1, HG_W), f32)
    ev_w_in = nrm(ks[3], (N_EVEN, D_MODEL, EVEN_IN), D_MODEL)
    ev_hg_norm_g = 1.0 + 0.05 * jax.random.normal(ks[4], (N_EVEN, HG_DK), f32)
    ev_ret_norm_g = 1.0 + 0.05 * jax.random.normal(ks[5], (N_EVEN, RET_DV), f32)
    ev_w_out = nrm(ks[6], (N_EVEN, EVEN_OUT, D_MODEL), EVEN_OUT)
    od_w_in = nrm(ks[7], (N_ODD, D_MODEL, ODD_IN), D_MODEL)
    od_conv_w = nrm(ks[8], (N_ODD, CONV_W, 2 * ML_QK), CONV_W)
    od_conv_b = 0.02 * jax.random.normal(ks[9], (N_ODD, 2 * ML_QK), f32)
    kg1, kg2 = jax.random.split(ks[10])
    i_bias = 0.1 * jax.random.normal(kg1, (N_ODD, ML_HEADS), f32)
    f_bias = jnp.linspace(3.0, 6.0, ML_HEADS, dtype=f32)[None, :] + 0.1 * jax.random.normal(kg2, (N_ODD, ML_HEADS), f32)
    od_gate_b = jnp.stack([i_bias, f_bias], axis=1)
    od_ml_norm_g = 1.0 + 0.05 * jax.random.normal(ks[11], (N_ODD, ML_DV), f32)
    od_w_out = nrm(ks[12], (N_ODD, ML_V, D_MODEL), ML_V)
    mlp_w1 = nrm(ks[13], (DEPTH, D_MODEL, D_FF), D_MODEL)
    mlp_w2 = nrm(ks[14], (DEPTH, D_FF, D_MODEL), D_FF)
    return {'x': x, 'norm_g': norm_g, 'hg_lower_bound': hg_lower_bound,
            'ev_w_in': ev_w_in, 'ev_hg_norm_g': ev_hg_norm_g, 'ev_ret_norm_g': ev_ret_norm_g,
            'ev_w_out': ev_w_out, 'od_w_in': od_w_in, 'od_conv_w': od_conv_w, 'od_conv_b': od_conv_b,
            'od_gate_b': od_gate_b, 'od_ml_norm_g': od_ml_norm_g, 'od_w_out': od_w_out,
            'mlp_w1': mlp_w1, 'mlp_w2': mlp_w2}

def first_block(x, norm_g, hg_lower_bound, ev_w_in, ev_hg_norm_g, ev_ret_norm_g, ev_w_out,
              od_w_in, od_conv_w, od_conv_b, od_gate_b, od_ml_norm_g, od_w_out, mlp_w1, mlp_w2):
    lower_bounds = jnp.cumsum(jax.nn.softmax(hg_lower_bound.astype(jnp.float32), axis=0), axis=0)
    for l in range(DEPTH):
        g = norm_g[l]
        h = rmsnorm(x, g[0])
        if l % 2 == 0:
            e = l // 2
            y = even_mixer(h, ev_w_in[e], lower_bounds[l], ev_hg_norm_g[e], ev_ret_norm_g[e], ev_w_out[e])
        else:
            o = l // 2
            y = odd_mixer(h, od_w_in[o], od_conv_w[o], od_conv_b[o], od_gate_b[o], od_ml_norm_g[o], od_w_out[o])
        x = x + rmsnorm(y, g[1])
        h = rmsnorm(x, g[2])
        x = x + rmsnorm(sq_relu_mlp(h, mlp_w1[l], mlp_w2[l]), g[3])
    return x


DEPTH_2 = 1

N_HEADS = 8
HEAD_DIM = 128
ATTN_WIDTH = N_HEADS * HEAD_DIM
CONV_WIDTH = 1024
CONV_K = 3
MOBA_BLOCK = 256
MOBA_TOPK = 3
Q_CHUNK = 8
N_BUCKETS = 32
MAX_DISTANCE = 128
IN_WIDTHS = (ATTN_WIDTH, ATTN_WIDTH, ATTN_WIDTH, ATTN_WIDTH,
             CONV_WIDTH, CONV_WIDTH, CONV_WIDTH, CONV_WIDTH,
             D_MODEL, D_MODEL)
IN_COLS = sum(IN_WIDTHS)
IN_OFFSETS = tuple(int(o) for o in np.cumsum(IN_WIDTHS)[:-1])


def rmsnorm_2(x, g):
    x32 = x.astype(jnp.float32)
    y = x32 * lax.rsqrt(jnp.mean(x32 * x32, axis=-1, keepdims=True) + EPS)
    return (y * g.astype(jnp.float32)).astype(x.dtype)

def t5_bucket(dist):
    n = jnp.maximum(dist, 0)
    max_exact = N_BUCKETS // 2
    nf = jnp.maximum(n, 1).astype(jnp.float32)
    large = max_exact + (jnp.log(nf / max_exact) / math.log(MAX_DISTANCE / max_exact)
                         * (N_BUCKETS - max_exact)).astype(jnp.int32)
    large = jnp.minimum(large, N_BUCKETS - 1)
    return jnp.where(n < max_exact, n, large)

def moba_attention(q, k, v, rel_bias):
    bsz, n_h, seq, hd = q.shape
    s_pad = -(-seq // MOBA_BLOCK) * MOBA_BLOCK
    padw = ((0, 0), (0, 0), (0, s_pad - seq), (0, 0))
    q32 = jnp.pad(q.astype(jnp.float32), padw) * (hd ** -0.5)
    nb = s_pad // MOBA_BLOCK
    kb = jnp.pad(k.astype(jnp.float32), padw).reshape(bsz, n_h, nb, MOBA_BLOCK, hd)
    vb = jnp.pad(v.astype(jnp.float32), padw).reshape(bsz, n_h, nb, MOBA_BLOCK, hd)
    bias_hb = rel_bias.astype(jnp.float32).T
    n_sel = min(MOBA_TOPK, nb - 1)
    n_chunks = s_pad // Q_CHUNK
    q_ch = q32.reshape(bsz, n_h, n_chunks, Q_CHUNK, hd).transpose(2, 0, 1, 3, 4)
    starts = jnp.arange(n_chunks, dtype=jnp.int32) * Q_CHUNK

    if n_sel > 0:
        k_mean = kb.mean(axis=3)
        scores = jnp.einsum('bhsd,bhnd->bhsn', q32, k_mean)
        q_blk = jnp.arange(s_pad) // MOBA_BLOCK
        fully_past = jnp.arange(nb)[None, :] < q_blk[:, None]
        scores = jnp.where(fully_past, scores, -jnp.inf)
        _, sel = lax.top_k(scores, n_sel)
        sel = sel.astype(jnp.int32)
    else:
        sel = jnp.zeros((bsz, n_h, s_pad, 0), jnp.int32)
    sel_ch = sel.reshape(bsz, n_h, n_chunks, Q_CHUNK, n_sel).transpose(2, 0, 1, 3, 4)

    b_idx = jnp.arange(bsz)[:, None, None, None]
    h_idx = jnp.arange(n_h)[None, :, None, None]
    offs = jnp.arange(MOBA_BLOCK, dtype=jnp.int32)

    def chunk(args):
        qc, selc, c0 = args
        qpos = c0 + jnp.arange(Q_CHUNK, dtype=jnp.int32)
        own = c0 // MOBA_BLOCK
        k_own = kb[:, :, own]
        v_own = vb[:, :, own]
        dist_own = qpos[:, None] - (own * MOBA_BLOCK + offs)[None, :]
        lg_own = jnp.einsum('bhqd,bhkd->bhqk', qc, k_own) + bias_hb[:, t5_bucket(dist_own)]
        lg_own = jnp.where(dist_own >= 0, lg_own, -jnp.inf)
        k_sel = kb[b_idx, h_idx, selc]
        v_sel = vb[b_idx, h_idx, selc]
        dist_sel = qpos[:, None, None] - (selc[..., None] * MOBA_BLOCK + offs)
        lg_sel = (jnp.einsum('bhqd,bhqnkd->bhqnk', qc, k_sel)
                  + bias_hb[h_idx[..., None], t5_bucket(dist_sel)])
        lg_sel = jnp.where((selc < own)[..., None], lg_sel, -jnp.inf)
        logits = jnp.concatenate(
            [lg_sel.reshape(bsz, n_h, Q_CHUNK, n_sel * MOBA_BLOCK), lg_own], axis=-1)
        p = jax.nn.softmax(logits, axis=-1)
        p_sel = p[..., :n_sel * MOBA_BLOCK].reshape(bsz, n_h, Q_CHUNK, n_sel, MOBA_BLOCK)
        p_own = p[..., n_sel * MOBA_BLOCK:]
        return (jnp.einsum('bhqnk,bhqnkd->bhqd', p_sel, v_sel)
                + jnp.einsum('bhqk,bhkd->bhqd', p_own, v_own))

    out = lax.map(chunk, (q_ch, sel_ch, starts))
    out = out.transpose(1, 2, 0, 3, 4).reshape(bsz, n_h, s_pad, hd)[:, :, :seq]
    return out.astype(q.dtype)

def short_conv(cb, cc, cx, conv_w):
    u = cc * cx
    y = lax.conv_general_dilated(
        u, conv_w[:, None, :].astype(u.dtype), window_strides=(1,),
        padding=[(CONV_K - 1, 0)], dimension_numbers=('NWC', 'WIO', 'NWC'),
        feature_group_count=CONV_WIDTH)
    return cb * y

def split_heads(t):
    b, s, _ = t.shape
    return t.reshape(b, s, N_HEADS, HEAD_DIM).transpose(0, 2, 1, 3)

def hybrid_layer(x, c, norm_g, w_ada, b_ada, w_in, conv_w, w_o_attn, w_o_conv, w_out, rel_bias):
    bsz, seq, _ = x.shape
    mod = jax.nn.silu(c) @ w_ada + b_ada
    shift, scale, gate = jnp.split(mod, 3, axis=-1)
    h = rmsnorm_2(x, norm_g) * (1 + scale[:, None, :]) + shift[:, None, :]
    proj = h @ w_in
    q, k, v, g_attn, cb, cc, cx, g_conv, m_attn, m_conv = jnp.split(proj, IN_OFFSETS, axis=-1)
    attn = moba_attention(split_heads(q), split_heads(k), split_heads(v), rel_bias)
    attn = attn.transpose(0, 2, 1, 3).reshape(bsz, seq, ATTN_WIDTH)
    y_attn = (attn * jax.nn.silu(g_attn)) @ w_o_attn
    y_conv = (short_conv(cb, cc, cx, conv_w) * jax.nn.silu(g_conv)) @ w_o_conv
    merged = jax.nn.sigmoid(m_attn) * y_attn + jax.nn.sigmoid(m_conv) * y_conv
    return x + gate[:, None, :] * (merged @ w_out)

def second_inputs(seed: int = 0) -> dict:
    key = jax.random.key(seed)
    ks = jax.random.split(key, 13)
    nrm = jax.random.normal
    f32 = jnp.float32
    return {
        "x": nrm(ks[0], (BATCH, SEQ, D_MODEL), f32),
        "c": nrm(ks[1], (BATCH, D_MODEL), f32),
        "norm_g": 1.0 + 0.05 * nrm(ks[2], (DEPTH_2, D_MODEL), f32),
        "w_ada": 0.5 * D_MODEL ** -0.5 * nrm(ks[3], (DEPTH_2, D_MODEL, 3 * D_MODEL), f32),
        "b_ada": 0.1 * nrm(ks[4], (DEPTH_2, 3 * D_MODEL), f32),
        "w_in": D_MODEL ** -0.5 * nrm(ks[5], (DEPTH_2, D_MODEL, IN_COLS), f32),
        "conv_w": CONV_K ** -0.5 * nrm(ks[6], (DEPTH_2, CONV_K, CONV_WIDTH), f32),
        "w_o_attn": ATTN_WIDTH ** -0.5 * nrm(ks[7], (DEPTH_2, ATTN_WIDTH, D_MODEL), f32),
        "w_o_conv": CONV_WIDTH ** -0.5 * nrm(ks[8], (DEPTH_2, CONV_WIDTH, D_MODEL), f32),
        "w_out": D_MODEL ** -0.5 * nrm(ks[9], (DEPTH_2, D_MODEL, D_MODEL), f32),
        "rel_bias": 0.5 * nrm(ks[10], (N_BUCKETS, N_HEADS), f32),
        "final_g": 1.0 + 0.05 * nrm(ks[11], (D_MODEL,), f32),
    }

def second_block(x, c, norm_g, w_ada, b_ada, w_in, conv_w, w_o_attn, w_o_conv, w_out, rel_bias, final_g):
    for layer in range(DEPTH_2):
        x = hybrid_layer(x, c, norm_g[layer], w_ada[layer], b_ada[layer], w_in[layer],
                         conv_w[layer], w_o_attn[layer], w_o_conv[layer], w_out[layer], rel_bias)
    return rmsnorm_2(x, final_g)


def setup_inputs(seed=0):
    out = dict(first_inputs(seed))
    for name, value in second_inputs(seed + 1).items():
        if name != "x":
            out[name + "_2"] = value
    return out


def reference(
    x, norm_g, hg_lower_bound, ev_w_in, ev_hg_norm_g, ev_ret_norm_g, ev_w_out, od_w_in,
    od_conv_w, od_conv_b, od_gate_b, od_ml_norm_g, od_w_out, mlp_w1, mlp_w2, c_2, norm_g_2,
    w_ada_2, b_ada_2, w_in_2, conv_w_2, w_o_attn_2, w_o_conv_2, w_out_2, rel_bias_2, final_g_2,
):
    x = first_block(
        x, norm_g, hg_lower_bound, ev_w_in, ev_hg_norm_g, ev_ret_norm_g, ev_w_out, od_w_in,
        od_conv_w, od_conv_b, od_gate_b, od_ml_norm_g, od_w_out, mlp_w1, mlp_w2,
    )
    return second_block(
        x, c_2, norm_g_2, w_ada_2, b_ada_2, w_in_2, conv_w_2, w_o_attn_2, w_o_conv_2, w_out_2,
        rel_bias_2, final_g_2,
    )


_drawn_inputs = setup_inputs


def setup_inputs(seed=0):
    import zlib

    import numpy as np

    out = dict(_drawn_inputs(seed))
    spreads = {}
    factors = {'hg_lower_bound': 2.934,
     'od_conv_b': 7.458,
     'norm_g_2': 8.0,
     'rel_bias_2': 64.0,
     'w_o_attn_2': 3.774}
    for name, (base, spread) in spreads.items():
        noise = np.random.default_rng([zlib.crc32(name.encode()), seed]).standard_normal(out[name].shape)
        drawn = base * np.exp(spread * noise) if base else spread * noise
        out[name] = __import__('jax').numpy.asarray(drawn.astype(out[name].dtype))
    for name, factor in factors.items():
        out[name] = (out[name] * factor).astype(out[name].dtype)
    return out
```

```python
from contextlib import ExitStack

import numpy as np

import concourse.bass as bass
from concourse import mybir

F32 = mybir.dt.float32
F32R = mybir.dt.float32r
U8 = mybir.dt.uint8
ALU = mybir.AluOpType
ACT = mybir.ActivationFunctionType
AX_X = mybir.AxisListType.X

P = 128
D = 1024
SEQ = 256
KT = D // P
TT = SEQ // P
CHUNK = 64
HEADS = 4
DK = 128
RET_DV = 256
FF = 4096
ATT_HEADS = 8
EPS = 1e-6
CAP = 15.0
QK_SCALE = float(np.float32(128.0) ** -0.5)
MASKED = 1e30

UCOLS = 256
UELEMS = KT * UCOLS
RING = 4
AHEAD = 3

T_COS, T_SIN = 0, 256
T_RET = 512
T_RESET = 1536
T_CAUSAL = 1792
T_UPPER = 2048
T_IDENT = 2176
T_ONEHOT = 2304
T_MASKS = 2560
T_END = 3584
LEVELS = (64, 32, 16, 8, 4, 2, 1)

R_NORM = 0
R_LOWER = 64
R_HG, R_RET = 76, 77
R_CONVW, R_CONVB = 79, 111
R_ML = 119
ROWS1 = 121
R2_C, R2_NORM, R2_BADA, R2_CONVW, R2_FINAL = 0, 8, 16, 40, 64
ROWS2 = 72


def shape_tables():
    f32 = np.float32
    tbl = np.zeros((P, T_END), f32)
    half = P // 2
    inv = (f32(10000.0) ** (-np.arange(half, dtype=f32) / f32(half))).astype(f32)
    ang = (np.arange(SEQ, dtype=f32)[:, None] * inv[None, :]).astype(f32)
    cos, sin = np.cos(ang).T, np.sin(ang).T
    tbl[:half, T_COS:T_COS + SEQ] = cos
    tbl[half:, T_COS:T_COS + SEQ] = cos
    tbl[:half, T_SIN:T_SIN + SEQ] = sin
    tbl[half:, T_SIN:T_SIN + SEQ] = -sin
    s = np.arange(P, dtype=np.float64)[:, None]
    t = np.arange(SEQ, dtype=np.float64)[None, :]
    for h in range(HEADS):
        log_g = np.log1p(-np.exp2(-5.0 - h))
        dec = np.where(t >= s, np.exp(log_g * np.maximum(t - s, 0.0)), 0.0)
        tbl[:, T_RET + h * SEQ:T_RET + (h + 1) * SEQ] = dec * float(DK) ** -0.5
    tbl[:, T_RESET:T_RESET + SEQ] = (np.arange(SEQ) % CHUNK != 0)[None, :]
    tbl[:, T_CAUSAL:T_CAUSAL + SEQ] = np.where(t >= s, 0.0, MASKED)
    tbl[:, T_UPPER:T_UPPER + P] = t[:, :P] >= s
    tbl[:, T_IDENT:T_IDENT + P] = np.eye(P)
    n = np.arange(SEQ)
    large = 16 + (np.log(np.maximum(n, 1).astype(f32) / f32(16)) / f32(np.log(8.0)) * f32(16)).astype(np.int32)
    bucket = np.where(n < 16, n, np.minimum(large, 31))
    tbl[:32, T_ONEHOT:T_ONEHOT + SEQ] = np.arange(32)[:, None] == bucket[None, :]
    masks = np.zeros((P, len(LEVELS) + 1, P), f32)
    i = np.arange(P)
    for n_level, m in enumerate(LEVELS):
        same = (i[:, None] // (2 * m)) == (i[None, :] // (2 * m))
        masks[:, n_level] = same & (i[:, None] % (2 * m) < m) & (i[None, :] % (2 * m) >= m)
    masks[:, len(LEVELS)] = np.eye(P)
    tbl[:, T_MASKS:T_END] = masks.reshape(P, -1)
    return tbl


def weight_units():
    A, B = "A", "B"
    us = []

    def cols(w, c0, n, role):
        us.extend((A, w, c0 + UCOLS * i, role, i) for i in range(n // UCOLS))

    def rows(w, n, role):
        us.extend((B, w, 2 * P * i, role, i) for i in range(n // (2 * P)))

    cols("ev_w_in", 512, 512, "hf")
    cols("ev_w_in", 0, 512, "hq")
    cols("ev_w_in", 1024, 512, "hi")
    cols("ev_w_in", 2048, 512, "rq")
    cols("ev_w_in", 2560, 512, "rk")
    cols("ev_w_in", 3072, 1024, "rv")
    cols("ev_w_in", 1536, 512, "hgate")
    cols("ev_w_in", 4096, 1024, "rgate")
    cols("w_ada", 0, 3072, "ada")
    rows("ev_w_out", 1536, "out0")
    mlp(us, 0)
    cols("od_w_in", 0, 1024, "mqk")
    cols("od_w_in", 1024, 1024, "mv")
    cols("od_w_in", 2048, 1024, "mog")
    rows("od_w_out", 1024, "out2")
    mlp(us, 1)
    cols("w_in", 0, 1024, "aq")
    cols("w_in", 1024, 1024, "ak")
    cols("w_in", 2048, 1024, "av")
    cols("w_in", 3072, 1024, "ag")
    for c in range(4):
        for role, c0 in (("cc", 5120), ("cx", 6144), ("cb", 4096), ("cg", 7168)):
            us.append((A, "w_in", c0 + UCOLS * c, role, c))
    rows("w_o_conv", 1024, "out4")
    cols("w_in", 9216, 1024, "mc")
    cols("w_in", 8192, 1024, "ma")
    rows("w_o_attn", 1024, "out5")
    rows("w_out", 1024, "out6")
    return us


def mlp(us, layer):
    for j in range(9):
        if j < 8:
            us.extend(("A", f"mlp_w1_{layer}", 512 * j + UCOLS * i, f"up{layer}", 2 * j + i) for i in range(2))
        if j >= 1:
            us.extend(("B", f"mlp_w2_{layer}", 512 * (j - 1) + 2 * P * i, f"out{2 * layer + 1}", 2 * (j - 1) + i)
                      for i in range(2))


UNITS = weight_units()
NU = len(UNITS)
A_OF = {}
for _u, _it in enumerate(UNITS):
    if _it[0] == "A":
        A_OF[_u] = len(A_OF)
EVAC = {"hf": "act", "hq": "act", "hi": "act", "rq": "dve", "rk": "dve", "rv": "act", "hgate": "act",
        "rgate": "act", "ada": "dve", "up0": "dve", "up1": "dve", "mqk": "dve", "mv": "act", "mog": "act",
        "aq": "act", "ak": "act", "av": "act", "ag": "act", "cc": "act", "cx": "dve", "cb": "dve",
        "cg": "act", "mc": "act", "ma": "act"}
FORM = {r: "F" for r in EVAC} | {"hi": "T", "rv": "T", "mv": "T", "av": "T", "ada": "mod"}
EVAC_UNITS = {e: [u for u in A_OF if EVAC[UNITS[u][3]] == e] for e in ("act", "dve")}
A_UNITS = list(A_OF)
PHASE = {f"out{p}": p for p in range(7)}
PHASE_KT = (12, 32, 8, 32, 8, 8, 8)


def at(role, i=0):
    return next(u for u, it in enumerate(UNITS) if it[3] == role and it[4] == i)


def last_of(role):
    return max(u for u, it in enumerate(UNITS) if it[3] == role)


def build(nc, a, out):
    ctx = ExitStack()
    with ctx:
        cursor = [(nc.sbuf_base + 63) // 64 * 64]

        def place(name, shape, dt, at_byte=None):
            size = int(np.prod(shape[1:])) * (1 if dt == U8 else 4)
            if at_byte is None:
                at_byte = cursor[0]
                cursor[0] += (size + 31) // 32 * 32
            return nc.alloc_sbuf_tensor_at(name, list(shape), dt, offset=at_byte)

        raw = place("raw", (P, RING, UELEMS), F32)
        wh = place("wh", (P, RING, UELEMS), F32R)
        wl = place("wl", (P, RING, UELEMS), F32R)
        xT = place("xT", (P, KT, SEQ), F32)
        hh = place("hh", (P, KT, SEQ), F32R)
        hl = place("hl", (P, KT, SEQ), F32R)
        y_at = cursor[0]
        yh = place("yh", (P, 12, SEQ), F32R)
        yl = place("yl", (P, 12, SEQ), F32R)
        scr1 = place("scr1", (P, 4, 512), F32, y_at + 4096)
        scr2 = place("scr2", (P, 4, 512), F32, y_at + 12288 + 4096)
        work = place("work", (P, KT, SEQ), F32)
        arena = place("arena", (P, 11264), F32)
        tables = place("tables", (P, 1792), F32)
        masks_at = cursor[0]
        masks = place("masks", (P, 8, P), U8)
        bias = place("bias", (P, ATT_HEADS, SEQ), F32, masks_at - 7168)
        ident = place("ident", (P, P), F32)
        col1 = place("col1", (P, ROWS1), F32)
        col2 = place("col2", (P, ROWS2), F32)
        wg = place("wg", (P, KT, 8), F32)
        modp = place("modp", (P, 24, 2), F32)
        mod = place("mod", (P, 24), F32)
        csp = place("csp", (P, KT, 2), F32R)
        cf = place("cf", (P, KT), F32)
        ones = place("ones", (P, 1), F32)
        eps = place("eps", (P, 1), F32)
        sd = place("sd", (P, 16), F32)
        rs = place("rs", (P, 16), F32)
        lb = place("lb", (P, 3, HEADS), F32)
        lbs = place("lbs", (P, 4, HEADS), F32)
        gz = place("gz", (P, 2, 8), F32)
        gzb = place("gzb", (P, 8), F32)
        gcap = place("gcap", (P, 2, 8), F32)
        glf = place("glf", (P, 2, 4), F32)
        gB = place("gB", (P, 2, 4), F32)
        gg = place("gg", (P, 2, 4), F32)
        gm = place("gm", (P, 2, 4), F32)
        gden = place("gden", (P, 2, 4), F32)
        gdi = place("gdi", (P, 2, 4), F32)
        gc = place("gc", (P, 8), F32)
        gs = place("gs", (P, KT), F32)
        mx = place("mx", (P, 2, 2), F32)
        sm = place("sm", (P, 2, 2), F32)
        assert cursor[0] <= nc.sbuf_usable_end, (cursor[0], nc.sbuf_usable_end)

        PS = [ctx.enter_context(nc.psum_tensor(f"bank{i}", [P, 512], F32)) for i in range(8)]
        scratch_dram = nc.dram_tensor("bias_scratch", (ATT_HEADS, 384), F32, kind="Internal").ap()

        names = (
            "raw0 raw1 raw2 raw3 hi lo_dve lo_pool used evac_act evac_dve "
            "d_x d_small d_tables d_causal d_wg d_u d_bias d_out "
            "const masks cols colsT xin xcopy step_dve "
            "xsq xstat xsd xrs xbc h h_part hh hl ysq ystat ysd yrs ybc ybs t x_new x_last acc "
            "low lowe c_act c_split f lf k_hg b diff e q k smm pred hout hev hsq hst hsd hrs hbc "
            "rope rmm rdec rout rev rst rsd rrs rbc y_src yh yl_pool yl_dve sq "
            "gmm gz gcap gsp gbm g gT M Mb fls fl warg w msc ms mout mev mst mvar msd mc mbc qk "
            "u asc lg mxn gle aexp p tr pt aout aout_v mcm merged acc_free4 acc_free5 fin_mm fin"
        ).split()
        S = {n: ctx.enter_context(nc.semaphore("s_" + n)) for n in names}
        raw_sem = [S["raw0"], S["raw1"], S["raw2"], S["raw3"]]
        block = ctx.enter_context(nc.Block())

        wf = work[:, :, :].rearrange("p k t -> p (k t)")
        ar = arena[:, :]

        def view(lo, *dims):
            v = ar[:, lo:lo + int(np.prod(dims))]
            if len(dims) == 1:
                return v
            if len(dims) == 2:
                return v.rearrange("p (a b) -> p a b", a=dims[0])
            return v.rearrange("p (a b c) -> p a b c", a=dims[0], b=dims[1])

        x_in = view(8192, TT, D)
        rows1, rows2 = ar[:, 10240:10368], ar[:, 10368:10496]
        rel_in, onehot = ar[0:32, 10496:10504], ar[0:32, 10512:10768]
        u_row = ar[0:ATT_HEADS, 10768:11152]
        g_qk = view(0, HEADS, 2, SEQ)
        g_b = view(2048, HEADS * SEQ)
        g_v = view(3072, TT, 512)
        g_gate = view(4096, HEADS * SEQ)
        r_qk = view(5120, HEADS, 2, SEQ)
        r_v = view(7168, TT, D)
        r_gate = view(9216, KT, SEQ)
        g_o, g_sq = view(0, HEADS * SEQ), view(1024, HEADS * SEQ)
        g_lf = scr1[:, 0:2, :].rearrange("p a b -> p (a b)")
        cosT, sinT = tables[:, 0:SEQ], tables[:, SEQ:2 * SEQ]
        ret_dec = tables[:, T_RET:T_RET + HEADS * SEQ].rearrange("p (h t) -> p h t", h=HEADS)
        reset = tables[:, T_RESET:T_RESET + SEQ]
        m_qk = view(0, 2 * HEADS, SEQ)
        m_v = view(2048, TT, D)
        m_og = view(4096, KT, SEQ)
        m_w = view(6144, HEADS, 384)
        m_s = view(7680, HEADS, 384)
        m_o = view(9216, KT, SEQ)
        m_sq = view(0, HEADS, 512)
        causal, upper = tables[:, 0:SEQ], tables[:, SEQ:SEQ + P]
        gT, MT = wf[0:HEADS, 0:SEQ], wf[0:HEADS, SEQ:2 * SEQ]
        a_q, a_k = view(0, KT, SEQ), view(2048, KT, SEQ)
        a_v, a_g = view(4096, TT, D), view(6144, KT, SEQ)
        c_y = view(8192, KT, SEQ)
        c_u, c_t = view(10240, 512), view(10752, 512)
        o_ma, o_mc = view(0, KT, SEQ), view(2048, KT, SEQ)
        y_conv = c_y
        fin_t = view(0, TT, D)
        ybs = ar[:, 0:SEQ]
        items = [(half, lv) for half in range(2) for lv in range(9)]

        PRENORM = {at("hf"): 0, at("up0"): 1, at("mqk"): 2, at("up1"): 3, at("aq"): 4}

        def item_unit(i):
            return at("hi") + (2 * i) // 3

        def decays_to(i):
            return sum(lv != 7 for _, lv in items[:i + 1])

        def a_unit(h):
            return at("cc") - 1 + (3 * h) // 2

        def acc_group(g):
            return PS[4 + g // 2][:, (g % 2) * SEQ:(g % 2 + 1) * SEQ]

        def y_pairs_before(p, mlp_too):
            return sum(PHASE_KT[q] // 2 for q in range(p) if mlp_too or q not in (1, 3))

        def y_source(p, i):
            if p == 0:
                return view(512 * i, 512) if i < 2 else view(9216 + 512 * (i - 2), 512)
            base = {2: 4096, 4: 8192, 5: 6144, 6: 0}[p]
            return view(base + 512 * i, 512)

        def wait_acc(eng, p, b):
            if b < 3:
                eng.wait_ge(S["acc"], 7 * p + 2 * b + 2)
            else:
                wait_used(eng, last_of(f"out{p}"))

        def flat2(t, i):
            return t[:, 2 * i:2 * i + 2, :].rearrange("p k t -> p (k t)")

        def evac_value(u):
            return EVAC_UNITS[EVAC[UNITS[u][3]]].index(u) + 1

        def wait_evac(eng, u):
            eng.wait_ge(S["evac_act"] if EVAC[UNITS[u][3]] == "act" else S["evac_dve"], evac_value(u))

        def wait_used(eng, u):
            eng.wait_ge(S["used"], u + 1)

        def unit_src(u):
            kind, w, c0, _, _ = UNITS[u]
            src = a[w]
            if kind == "A":
                return src[:, c0:c0 + UCOLS].rearrange("(k p) c -> p k c", p=P)
            return src[c0:c0 + 2 * P, :].rearrange("(k p) c -> p k c", p=P)

        def slot(t, u, kind):
            return t[:, u % RING, :].rearrange("p (k c) -> p k c", k=KT if kind == "A" else 2)

        def bank(u):
            return PS[A_OF[u] % 2]

        @block.sync
        def _(eng):
            eng.dma_start(x_in, a["x"].rearrange("(t p) d -> p t d", p=P)).then_inc(S["d_x"], 16)
            for u in range(NU):
                if u == at("mqk"):
                    eng.wait_ge(S["y_src"], 6)
                    eng.dma_start(tables[:, 0:384], a["tbl"][:, T_CAUSAL:T_CAUSAL + 384]).then_inc(S["d_causal"], 16)
                if u == at("aq"):
                    eng.wait_ge(S["warg"], HEADS)
                    eng.wait_ge(S["gbm"], 1)
                    eng.wait_ge(S["d_u"], 16)
                    src = scratch_dram
                    eng.dma_start(bias[:, :, :], bass.AP(tensor=src.tensor, offset=src.offset,
                                                         ap=[[1, P], [384, ATT_HEADS], [1, SEQ]])).then_inc(S["d_bias"], 16)
                if u >= RING:
                    v = u - RING
                    eng.wait_ge(S["lo_dve"] if v % 2 == 0 else S["lo_pool"], v // 2 + 1)
                eng.dma_start(slot(raw, u, UNITS[u][0]), unit_src(u)).then_inc(raw_sem[u % RING], 16)
            eng.wait_ge(S["fin"], 4)
            eng.dma_start(out.rearrange("(t p) d -> p t d", p=P), fin_t).then_inc(S["d_out"], 16)
            eng.wait_ge(S["d_out"], 16)

        @block.tensor
        def _(eng):
            def mm(o, l, r, start, stop):
                return eng.matmul(o, l, r, start=start, stop=stop, skip_group_check=True)

            def a_forward(u):
                role, i = UNITS[u][3:]
                w_hi, w_lo, o = slot(wh, u, "A"), slot(wl, u, "A"), bank(u)
                norm = PRENORM.get(u)
                for g in range(2):
                    for k in range(KT):
                        if norm is not None and g == 0:
                            eng.wait_ge(S["hl"], KT * norm + k + 1)
                        first, last = k == 0, k == KT - 1
                        if FORM[role] == "F":
                            c = slice(g * P, (g + 1) * P)
                            dst = o[:, g * SEQ:(g + 1) * SEQ]
                            mm(dst, w_hi[:, k, c], hh[:, k, :], first, False)
                            mm(dst, w_hi[:, k, c], hl[:, k, :], False, False)
                            m = mm(dst, w_lo[:, k, c], hh[:, k, :], False, last)
                        elif FORM[role] == "T":
                            c = slice(g * P, (g + 1) * P)
                            dst = o[:, g * UCOLS:(g + 1) * UCOLS]
                            mm(dst, hh[:, k, c], w_hi[:, k, :], first, False)
                            mm(dst, hh[:, k, c], w_lo[:, k, :], False, False)
                            m = mm(dst, hl[:, k, c], w_hi[:, k, :], False, last)
                        else:
                            c = slice(g * P, (g + 1) * P)
                            dst = o[:, 2 * g:2 * g + 2]
                            mm(dst, w_hi[:, k, c], csp[:, k, :], first, False)
                            m = mm(dst, w_lo[:, k, c], csp[:, k, :], False, last)
                m.then_inc(S["used"], 1)

            def b_forward(u):
                role, i = UNITS[u][3:]
                p = PHASE[role]
                w_hi, w_lo = slot(wh, u, "B"), slot(wl, u, "B")
                kt = 2 * i if p not in (1, 3) else 2 * (i % 4)
                end = i == PHASE_KT[p] // 2 - 1
                for g in range(KT):
                    c = slice(g * P, (g + 1) * P)
                    dst = acc_group(g)
                    for k in range(2):
                        mm(dst, w_hi[:, k, c], yh[:, kt + k, :], i == 0 and k == 0 and g % 2 == 0, False)
                        mm(dst, w_hi[:, k, c], yl[:, kt + k, :], False, False)
                        m = mm(dst, w_lo[:, k, c], yh[:, kt + k, :], False, end and k == 1)
                    if end and g < KT - 1:
                        m.then_inc(S["acc"], 1)
                m.then_inc(S["used"], 1)

            def column_sums(stat_col, tile, g, first, last):
                for tt in range(TT):
                    m = mm(PS[2][:, stat_col + tt:stat_col + tt + 1], tile[:, tt * P:(tt + 1) * P], ones[:, :],
                           first and tt == 0, last)
                return m

            def spread(dst, col):
                return mm(dst, col.broadcast_to([P, P]), ident[:, :], True, True)

            def prenorm(n):
                for g in range(KT):
                    eng.wait_ge(S["xsq"], KT * n + g + 1)
                    m = column_sums(0, work[:, g, :], g, g == 0, g == KT - 1)
                m.then_inc(S["xstat"], 1)
                eng.wait_ge(S["xrs"], n + 1)
                spread(PS[3][:, 0:P], rs[:, 0:1])
                spread(PS[3][:, P:2 * P], rs[:, 1:2]).then_inc(S["xbc"], 1)

            def postnorm(n):
                for b in range(4):
                    eng.wait_ge(S["ysq"], 4 * n + b + 1)
                    for g in (2 * b, 2 * b + 1):
                        m = column_sums(4, work[:, g, :], g, g == 0, g == KT - 1)
                m.then_inc(S["ystat"], 1)
                eng.wait_ge(S["yrs"], n + 1)
                spread(PS[3][:, 2 * P:3 * P], rs[:, 2:3])
                spread(PS[3][:, 3 * P:4 * P], rs[:, 3:4]).then_inc(S["ybc"], 1)

            eng.wait_ge(S["d_small"], 16 * 6)
            eng.transpose(PS[2][:, 0:ROWS1], rows1[0:ROWS1, :], ident[0:ROWS1, 0:ROWS1])
            eng.transpose(PS[2][:, P:P + ROWS2], rows2[0:ROWS2, :], ident[0:ROWS2, 0:ROWS2])
            mm(PS[3][0:ATT_HEADS, 0:SEQ], rel_in, onehot, True, True).then_inc(S["colsT"], 1)
            eng.wait_ge(S["d_x"], 16)
            for g in range(KT):
                for tt in range(TT):
                    m = eng.transpose(PS[4 + g // 2][:, (g % 2) * SEQ + tt * P:(g % 2) * SEQ + (tt + 1) * P],
                                      x_in[:, tt, g * P:(g + 1) * P], ident[:, :])
                if g % 2 == 1:
                    m.then_inc(S["xin"], 1)
            eng.wait_ge(S["const"], 2)
            eng.wait_ge(S["cols"], 2)
            eng.wait_ge(S["u"], 1)
            prenorm(0)

            def level_scores(i):
                half, lv = items[i]
                dst = PS[2 + i % 2]
                if i >= 2:
                    eng.wait_ge(S["pred"], i - 1)
                if lv != 7:
                    eng.wait_ge(S["q"], decays_to(i))
                    eng.wait_ge(S["k"], decays_to(i))
                for h in range(2):
                    for tt in range(TT):
                        if lv == 7:
                            qq, kk = g_qk[:, 2 * half + h, 0, :], g_qk[:, 2 * half + h, 1, :]
                        else:
                            qq = scr1[:, 2 + i % 2, h * SEQ:(h + 1) * SEQ]
                            kk = scr2[:, i % 2, h * SEQ:(h + 1) * SEQ]
                        if lv == 8:
                            if tt == 0:
                                m = mm(dst[:, h * P:(h + 1) * P], kk[:, 0:P], qq[:, P:2 * P], True, True)
                        else:
                            c = slice(tt * P, (tt + 1) * P)
                            m = mm(dst[:, (2 * h + tt) * P:(2 * h + tt + 1) * P], kk[:, c], qq[:, c], True, True)
                m.then_inc(S["smm"], 1)

            def gated_out():
                eng.wait_ge(S["pred"], len(items))
                for h in range(HEADS):
                    dst = PS[2 + h // 2][:, (h % 2) * SEQ:(h % 2 + 1) * SEQ]
                    v0, v1 = g_v[:, 0, h * DK:(h + 1) * DK], g_v[:, 1, h * DK:(h + 1) * DK]
                    mm(dst[:, 0:P], v0, wf[:, (2 * h) * P:(2 * h + 1) * P], True, True)
                    mm(dst[:, P:2 * P], v0, wf[:, 1024 + h * P:1024 + (h + 1) * P], True, False)
                    m = mm(dst[:, P:2 * P], v1, wf[:, (2 * h + 1) * P:(2 * h + 2) * P], False, True)
                m.then_inc(S["hout"], 1)

            def ret_scores():
                eng.wait_ge(S["rope"], 4)
                for h in range(HEADS):
                    rq, rk = r_qk[:, h, 0, :], r_qk[:, h, 1, :]
                    mm(PS[4 + h][:, 0:SEQ], rk[:, 0:P], rq, True, True)
                    m = mm(PS[4 + h][:, SEQ:SEQ + P], rk[:, P:2 * P], rq[:, P:2 * P], True, True)
                m.then_inc(S["rmm"], 1)

            def values_out(dst, v, c0, probs, last_sem):
                for g in range(2):
                    o = dst[:, g * SEQ:(g + 1) * SEQ]
                    mm(o, v[:, 0, c0 + g * P:c0 + (g + 1) * P], probs[:, 0:SEQ], True, False)
                    m = mm(o[:, P:2 * P], v[:, 1, c0 + g * P:c0 + (g + 1) * P], probs[:, SEQ:SEQ + P], False, True)
                m.then_inc(last_sem, 1)

            def head_sums(dst, sq_of, groups):
                for h in range(HEADS):
                    for tt in range(TT):
                        for g in range(groups):
                            m = mm(dst[:, 2 * h + tt:2 * h + tt + 1], sq_of(h, g)[:, tt * P:(tt + 1) * P], ones[:, :],
                                   g == 0, g == groups - 1)
                return m

            def head_spread(dst_of, cols):
                for h in range(HEADS):
                    for tt in range(TT):
                        m = spread(dst_of(h)[:, tt * P:(tt + 1) * P], cols[:, 2 * h + tt:2 * h + tt + 1])
                return m

            def gate_products():
                eng.wait_ge(S["d_wg"], 32)
                for tt in range(TT):
                    for k in range(KT):
                        m = mm(PS[4][:, 8 * tt:8 * tt + 8], work[:, k, tt * P:(tt + 1) * P], wg[:, k, :],
                               k == 0, k == KT - 1)
                m.then_inc(S["gmm"], 1)

            def gate_cumsum():
                eng.wait_ge(S["gsp"], 1)
                eng.wait_ge(S["d_causal"], 16)
                o = PS[4]
                mm(o[:, 32:36], upper, glf[:, 0, :], True, True)
                mm(o[:, 36:40], ones[:, 0:1].broadcast_to([P, P]), glf[:, 0, :], True, False)
                mm(o[:, 36:40], upper, glf[:, 1, :], False, True).then_inc(S["gbm"], 1)

            def gate_rows():
                eng.wait_ge(S["g"], 1)
                for tt in range(TT):
                    m = eng.transpose(PS[7][0:HEADS, tt * P:(tt + 1) * P], gg[:, tt, :], ident[:, :])
                m.then_inc(S["gT"], 1)

            def gate_max():
                eng.wait_ge(S["M"], 1)
                for h in range(HEADS):
                    m = mm(PS[5 + h // 2][:, (h % 2) * SEQ:(h % 2 + 1) * SEQ],
                           ident[0:HEADS, h:h + 1].broadcast_to([HEADS, P]), MT, True, True)
                for tt in range(TT):
                    m = eng.transpose(PS[7][:, 256 + 4 * tt:260 + 4 * tt], MT[:, tt * P:(tt + 1) * P],
                                      ident[0:HEADS, 0:HEADS])
                m.then_inc(S["Mb"], 1)

            def ml_scores(h):
                eng.wait_ge(S["qk"], 4)
                if h >= 2:
                    eng.wait_ge(S["ms"], h - 1)
                q, k, o = m_qk[:, h, :], m_qk[:, HEADS + h, :], PS[2 + h % 2]
                mm(o[:, 0:SEQ], k[:, 0:P], q, True, True)
                mm(o[:, SEQ:SEQ + P], k[:, P:2 * P], q[:, P:2 * P], True, True).then_inc(S["msc"], 1)

            def ml_out(h):
                eng.wait_ge(S["ms"], h + 1)
                wait_evac(eng, last_of("mv"))
                if h == 0:
                    eng.wait_ge(S["warg"], HEADS)
                if h >= 2:
                    eng.wait_ge(S["mev"], 2 * (h - 1))
                s = m_s[:, h, :]
                mm(PS[4][:, 64 + h:65 + h], s[:, 0:P], ones[:, :], True, True)
                mm(PS[4][:, 68 + h:69 + h], s[:, P:2 * P], ones[:, :], True, False)
                mm(PS[4][:, 68 + h:69 + h], s[:, SEQ:SEQ + P], ones[:, :], False, True)
                values_out(PS[5 + h % 2], m_v, h * RET_DV, s, S["mout"])

            def att_scores(h):
                if h == 0:
                    wait_evac(eng, last_of("ak"))
                if h >= 2:
                    eng.wait_ge(S["lg"], h - 1)
                q, k, o = a_q[:, h, :], a_k[:, h, :], PS[2 + h % 2]
                mm(o[:, 0:P], q[:, 0:P], k[:, 0:P], True, True)
                mm(o[:, P:P + SEQ], q[:, P:2 * P], k, True, True).then_inc(S["asc"], 1)

            def att_turn(h):
                eng.wait_ge(S["p"], h + 1)
                if h >= 2:
                    eng.wait_ge(S["pt"], h - 1)
                pr = wf[:, 384 * (h % 2):384 * (h % 2 + 1)]
                for j in range(3):
                    m = eng.transpose(PS[4 + h % 2][:, j * P:(j + 1) * P], pr[:, j * P:(j + 1) * P], ident[:, :])
                m.then_inc(S["tr"], 1)

            def att_out(h):
                eng.wait_ge(S["pt"], h + 1)
                if h >= 2:
                    eng.wait_ge(S["aout_v"], h - 1)
                pt, o = wf[:, 768 + 384 * (h % 2):768 + 384 * (h % 2 + 1)], PS[6 + h % 2]
                mm(o[:, 0:SEQ], a_v[:, 0, h * P:(h + 1) * P], pt[:, 0:SEQ], True, False)
                mm(o[:, P:2 * P], a_v[:, 1, h * P:(h + 1) * P], pt[:, SEQ:SEQ + P], False, True).then_inc(S["aout"], 1)

            for u in range(NU):
                kind, _, _, role, i = UNITS[u]
                if role in ("up0", "mqk", "up1", "aq") and i == 0:
                    n = ("up0", "mqk", "up1", "aq").index(role)
                    postnorm(n)
                    prenorm(n + 1)
                eng.wait_ge(S["hi"], u + 1)
                eng.wait_ge(S["lo_dve"] if u % 2 == 0 else S["lo_pool"], u // 2 + 1)
                if kind == "A":
                    if A_OF[u] >= 2:
                        wait_evac(eng, A_UNITS[A_OF[u] - 2])
                    if role == "ada" and i == 0:
                        eng.wait_ge(S["c_split"], 1)
                    a_forward(u)
                else:
                    p = PHASE[role]
                    if p in (1, 3):
                        eng.wait_ge(S["yl_dve"], (p // 2) * 16 + i + 1)
                    else:
                        eng.wait_ge(S["yl_pool"], y_pairs_before(p, False) + i + 1)
                    if i == 0 and p == 4:
                        eng.wait_ge(S["aout_v"], ATT_HEADS)
                    if i == 0 and p == 5:
                        eng.wait_ge(S["acc_free4"], 4)
                    if i == 0 and p == 6:
                        eng.wait_ge(S["acc_free5"], 4)
                    b_forward(u)

                for j in range(len(items)):
                    if u == item_unit(j) + 1:
                        level_scores(j)
                if u == at("rv", 2):
                    ret_scores()
                if u == item_unit(17) + 2:
                    gated_out()
                if u == item_unit(17) + 3:
                    eng.wait_ge(S["hsq"], 1)
                    head_sums(PS[3], lambda h, g: g_sq[:, h * SEQ:(h + 1) * SEQ], 1).then_inc(S["hst"], 1)
                if u == last_of("rgate"):
                    eng.wait_ge(S["hrs"], 1)
                    head_spread(lambda h: PS[2 + h // 2][:, (h % 2) * SEQ:(h % 2 + 1) * SEQ], rs).then_inc(S["hbc"], 1)
                    for h in range(HEADS):
                        eng.wait_ge(S["rdec"], h + 1)
                        values_out(PS[4 + h], r_v, h * RET_DV, wf[:, 512 * h:512 * h + 384], S["rout"])
                if u == at("ada", 2):
                    eng.wait_ge(S["rev"], 8)
                    head_sums(PS[4], lambda h, g: wf[:, 512 * h + g * SEQ:512 * h + (g + 1) * SEQ], 2).then_inc(S["rst"], 1)
                if u == at("ada", 3):
                    eng.wait_ge(S["rrs"], 1)
                    head_spread(lambda h: PS[5 + h // 2][:, (h % 2) * SEQ:(h % 2 + 1) * SEQ], rs[:, 8:16]).then_inc(S["rbc"], 1)

                if u == at("mqk"):
                    gate_products()
                if u == at("mqk", 1):
                    gate_cumsum()
                if u == at("mqk", 2):
                    gate_rows()
                if u == at("mqk", 3):
                    gate_max()
                for h in range(HEADS):
                    if u == at("mv", h):
                        ml_scores(h)
                    if u == at("mog", h):
                        ml_out(h)
                if u == last_of("mog"):
                    eng.wait_ge(S["mev"], 8)
                    eng.wait_ge(S["fls"], 1)
                    head_sums(PS[7], lambda h, g: m_sq[:, h, g * SEQ:(g + 1) * SEQ], 2).then_inc(S["mst"], 1)
                    eng.wait_ge(S["mc"], 1)
                    head_spread(lambda h: PS[2 + h // 2][:, (h % 2) * SEQ:(h % 2 + 1) * SEQ],
                                gc[:, :]).then_inc(S["mbc"], 1)

                for h in range(ATT_HEADS):
                    if u == a_unit(h):
                        att_scores(h)
                    if u == a_unit(h) + 2:
                        att_turn(h)
                    if u == a_unit(h) + 3:
                        att_out(h)

            prenorm(5)
            for g in range(KT):
                eng.wait_ge(S["h"], 5 * KT + g + 1)
                for tt in range(TT):
                    m = eng.transpose(PS[4 + 2 * tt + g // 4][:, (g % 4) * P:(g % 4 + 1) * P],
                                      work[:, g, tt * P:(tt + 1) * P], ident[:, :])
                if g % 4 == 3:
                    m.then_inc(S["fin_mm"], 1)

        @block.vector
        def _(eng):
            steps = [0]

            def link(ins):
                steps[0] += 1
                ins.then_inc(S["step_dve"], 1)
                eng.wait_ge(S["step_dve"], steps[0])

            def tt(o, x, y, op):
                return eng.tensor_tensor(o, x, y, op)

            def ts(o, x, c1, c2, op0, op1=ALU.bypass):
                return eng.tensor_scalar(o, x, c1, c2, op0, op1)

            def stt(o, x, c, y, op0, op1):
                return eng.scalar_tensor_tensor(out=o, in0=x, scalar=c, in1=y, op0=op0, op1=op1)

            def split(u):
                eng.wait_ge(raw_sem[u % RING], 16 * (u // RING + 1))
                eng.wait_ge(S["hi"], u + 1)
                if u >= RING:
                    wait_used(eng, u - RING)
                tt(wl[:, u % RING, :], raw[:, u % RING, :], wh[:, u % RING, :].bitcast(F32),
                   ALU.subtract).then_inc(S["lo_dve"], 1)

            def gain(n, g):
                if n < 4:
                    c = R_NORM + 32 * (n // 2) + 16 * (n % 2) + g
                    return col1[:, c:c + 1]
                return gs[:, g:g + 1] if n == 4 else col2[:, R2_FINAL + g:R2_FINAL + g + 1]

            def prenorm(n):
                eng.wait_ge(S["xsd"], n + 1)
                eng.reciprocal(rs[:, 0:2], sd[:, 0:2]).then_inc(S["xrs"], 1)
                eng.wait_ge(S["xbc"], n + 1)
                for g in range(KT):
                    m = stt(work[:, g, :], xT[:, g, :], gain(n, g), PS[3][:, 0:SEQ], ALU.mult, ALU.mult)
                    if n != 4:
                        m.then_inc(S["h"], 1)
                        continue
                    m.then_inc(S["h_part"], 1)
                    eng.wait_ge(S["h_part"], g + 1)
                    ts(work[:, g, :], work[:, g, :], mod[:, g:g + 1], None, ALU.add).then_inc(S["h"], 1)

            def postnorm(n):
                eng.wait_ge(S["ysd"], n + 1)
                eng.reciprocal(rs[:, 2:4], sd[:, 2:4]).then_inc(S["yrs"], 1)
                eng.wait_ge(S["ybs"], n + 1)
                for g in range(KT):
                    c = R_NORM + 32 * (n // 2) + 16 * (n % 2) + 8 + g
                    stt(work[:, g, :], acc_group(g), col1[:, c:c + 1], ybs, ALU.mult, ALU.mult).then_inc(S["t"], 1)

            eng.memset(ones[:, :], 1.0).then_inc(S["const"], 1)
            eng.memset(eps[:, :], EPS).then_inc(S["const"], 1)
            link(eng.memset(u_row, -MASKED))
            eng.wait_ge(S["colsT"], 1)
            tensor = eng.tensor_copy
            tensor(col1[:, :], PS[2][:, 0:ROWS1]).then_inc(S["cols"], 1)
            tensor(col2[:, :], PS[2][:, P:P + ROWS2]).then_inc(S["cols"], 1)
            tensor(masks[:, :, :].rearrange("p l t -> p (l t)"), g_lf).then_inc(S["masks"], 1)
            tensor(u_row[:, P - 1:P - 1 + SEQ], PS[3][0:ATT_HEADS, 0:SEQ]).then_inc(S["u"], 1)
            for b in range(4):
                eng.wait_ge(S["xin"], b + 1)
                tensor(xT[:, 2 * b:2 * b + 2, :], PS[4 + b][:, :].rearrange("p (k t) -> p k t", k=2)).then_inc(S["xcopy"], 1)
            prenorm(0)
            low = [col1[:, R_LOWER + HEADS * r:R_LOWER + HEADS * (r + 1)] for r in range(3)]
            link(tt(lbs[:, 2, :], low[0], low[1], ALU.max))
            link(tt(lbs[:, 2, :], lbs[:, 2, :], low[2], ALU.max))
            for r in range(3):
                tt(lb[:, r, :], low[r], lbs[:, 2, :], ALU.subtract).then_inc(S["low"], 1)
            eng.wait_ge(S["lowe"], 1)
            link(tt(lbs[:, 2, :], lb[:, 0, :], lb[:, 1, :], ALU.add))
            link(tt(lbs[:, 2, :], lbs[:, 2, :], lb[:, 2, :], ALU.add))
            link(eng.reciprocal(lbs[:, 3, :], lbs[:, 2, :]))
            link(tt(lbs[:, 0, :], lb[:, 0, :], lbs[:, 3, :], ALU.mult))
            link(ts(lbs[:, 1, :], lbs[:, 0, :], -1.0, 1.0, ALU.mult, ALU.add))
            eng.wait_ge(S["c_act"], 1)
            link(tensor(csp[:, :, 0], cf[:, :]))
            tt(csp[:, :, 1], cf[:, :], csp[:, :, 0].bitcast(F32), ALU.subtract).then_inc(S["c_split"], 1)

            def rope(u):
                i, which = UNITS[u][4], 0 if UNITS[u][3] == "rq" else 1
                dst = r_qk[:, 2 * i:2 * i + 2, which, :]
                tmp = scr2[:, 2 + i % 2, :].rearrange("p (h t) -> p h t", h=2)
                ps = bank(u)[:, :].rearrange("p (h t) -> p h t", h=2)
                half = P // 2

                def both(x):
                    return x.unsqueeze(1).broadcast_to([x.shape[0], 2, SEQ])

                if i == 0 and which == 0:
                    eng.wait_ge(S["d_tables"], 16)
                link(tt(dst, ps, both(cosT), ALU.mult))
                link(tt(tmp[0:half], ps[half:P], both(sinT[half:P]), ALU.mult))
                tt(tmp[half:P], ps[0:half], both(sinT[0:half]), ALU.mult).then_inc(S["evac_dve"], 1)
                eng.wait_ge(S["evac_dve"], evac_value(u))
                tt(dst, dst, tmp, ALU.add).then_inc(S["rope"], 1)

            def conv_taps(u):
                i = UNITS[u][4]
                ps = bank(u)[:, :].rearrange("p (h t) -> p h t", h=2)
                for j in range(4):
                    for g in range(2):
                        c = 2 * i + g
                        w = col1[:, R_CONVW + 8 * (3 - j) + c:R_CONVW + 8 * (3 - j) + c + 1]
                        y = m_qk[:, c, :]
                        if j == 0:
                            m = ts(y, ps[:, g, :], w, col1[:, R_CONVB + c:R_CONVB + c + 1], ALU.mult, ALU.add)
                        else:
                            m = stt(y[:, j:], ps[:, g, 0:SEQ - j], w, y[:, j:], ALU.mult, ALU.add)
                    if j < 3:
                        link(m)
                m.then_inc(S["evac_dve"], 1)

            def short_conv(u):
                i = UNITS[u][4]
                eng.wait_ge(S["evac_act"], evac_value(u - 1))
                tt(c_u, bank(u)[:, :], c_u, ALU.mult).then_inc(S["evac_dve"], 1)
                eng.wait_ge(S["evac_dve"], evac_value(u))
                for j in range(3):
                    for g in range(2):
                        kt = 2 * i + g
                        w = col2[:, R2_CONVW + 8 * (2 - j) + kt:R2_CONVW + 8 * (2 - j) + kt + 1]
                        x, y = c_u[:, g * SEQ:(g + 1) * SEQ], c_y[:, kt, :]
                        if j == 0:
                            m = ts(y, x, w, None, ALU.mult)
                        else:
                            m = stt(y[:, j:], x[:, 0:SEQ - j], w, y[:, j:], ALU.mult, ALU.add)
                    link(m)

            def level_decays(i):
                half, lv = items[i]
                if lv == 7:
                    return
                if i >= 2 and items[i - 2][1] != 7:
                    eng.wait_ge(S["q"], decays_to(i - 2))
                    eng.wait_ge(S["k"], decays_to(i - 2))
                m = LEVELS[lv] if lv < 7 else 128
                b = g_b[:, half * 512:(half + 1) * 512].rearrange("p (n w) -> p n w", w=2 * m)
                e = scr1[:, i % 2, :].rearrange("p (n w) -> p n w", w=2 * m)
                n = 256 // m

                def at_col(j, w):
                    return b[:, :, j:j + 1].broadcast_to([P, n, w])

                if m < 64:
                    tt(e[:, :, m:2 * m], b[:, :, m:2 * m], at_col(m - 1, m), ALU.subtract)
                    tt(e[:, :, 0:m], at_col(m - 1, m), b[:, :, 0:m], ALU.subtract).then_inc(S["diff"], 1)
                elif m == 64:
                    tensor(e[:, :, 64:128], b[:, :, 64:128])
                    tt(e[:, :, 0:64], at_col(63, 64), b[:, :, 0:64], ALU.subtract).then_inc(S["diff"], 1)
                else:
                    tensor(e[:, :, 128:192], b[:, :, 128:192])
                    tt(e[:, :, 192:256], b[:, :, 192:256], at_col(191, 64), ALU.add)
                    link(tt(e[:, :, 0:64], at_col(63, 64), b[:, :, 0:64], ALU.subtract))
                    tt(e[:, :, 0:64], e[:, :, 0:64], at_col(127, 64), ALU.add)
                    tt(e[:, :, 64:128], at_col(127, 64), b[:, :, 64:128], ALU.subtract).then_inc(S["diff"], 1)

            def level_queries(i):
                half, lv = items[i]
                if lv == 7:
                    return
                eng.wait_ge(S["e"], decays_to(i))
                if i >= 2:
                    eng.wait_ge(S["smm"], i - 1)
                tt(scr1[:, 2 + i % 2, :].rearrange("p (h t) -> p h t", h=2), g_qk[:, 2 * half:2 * half + 2, 0, :],
                   scr1[:, i % 2, :].rearrange("p (h t) -> p h t", h=2), ALU.mult).then_inc(S["q"], 1)

            def level_pick(i):
                half, lv = items[i]
                eng.wait_ge(S["smm"], i + 1)
                if i == 0:
                    eng.wait_ge(S["masks"], 1)
                if i >= 1:
                    eng.wait_ge(S["pred"], i)
                if lv == 8:
                    tensor(wf[:, 1024 + half * SEQ:1024 + (half + 1) * SEQ], PS[2 + i % 2][:, 0:SEQ]).then_inc(S["pred"], 1)
                else:
                    eng.copy_predicated(
                        wf[:, half * 512:(half + 1) * 512].rearrange("p (n t) -> p n t", n=4),
                        masks[:, lv, :].unsqueeze(1).broadcast_to([P, 4, P]),
                        PS[2 + i % 2][:, :].rearrange("p (n t) -> p n t", n=4)).then_inc(S["pred"], 1)

            def att_logits(h):
                eng.wait_ge(S["asc"], h + 1)
                if h == 0:
                    eng.wait_ge(S["d_bias"], 16)
                if h >= 2:
                    eng.wait_ge(S["tr"], h - 1)
                o, ps = wf[:, 384 * (h % 2):384 * (h % 2 + 1)], PS[2 + h % 2]
                stt(o[:, 0:P], ps[:, 0:P], QK_SCALE, bias[:, h, P - 1::-1], ALU.mult, ALU.add)
                stt(o[:, P:P + SEQ], ps[:, P:P + SEQ], QK_SCALE, bias[:, h, SEQ - 1::-1], ALU.mult,
                    ALU.add).then_inc(S["lg"], 1)
                eng.wait_ge(S["lg"], h + 1)
                if h >= 2:
                    eng.wait_ge(S["aexp"], h - 1)
                eng.tensor_reduce(mx[:, h % 2, 0:1], o[:, 0:P], AX_X, ALU.max)
                link(eng.tensor_reduce(mx[:, h % 2, 1:2], o[:, P:P + SEQ], AX_X, ALU.max))
                ts(mx[:, h % 2, :], mx[:, h % 2, :], -1.0, None, ALU.mult).then_inc(S["mxn"], 1)

            def att_norm(h):
                eng.wait_ge(S["aexp"], h + 1)
                o = wf[:, 384 * (h % 2):384 * (h % 2 + 1)]
                link(eng.reciprocal(sm[:, h % 2, :], sm[:, h % 2, :]))
                ts(o[:, 0:P], o[:, 0:P], sm[:, h % 2, 0:1], None, ALU.mult)
                ts(o[:, P:P + SEQ], o[:, P:P + SEQ], sm[:, h % 2, 1:2], None, ALU.mult).then_inc(S["p"], 1)

            def att_gate(h):
                eng.wait_ge(S["aout"], h + 1)
                if h == 0:
                    wait_evac(eng, last_of("ag"))
                tt(a_g[:, h, :], PS[6 + h % 2][:, 0:SEQ], a_g[:, h, :], ALU.mult).then_inc(S["aout_v"], 1)

            def hidden_low(layer, i):
                eng.wait_ge(S["yh"], y_pairs_before(2 * layer + 1, True) + i + 1)
                if i >= RING:
                    wait_used(eng, at(f"out{2 * layer + 1}", i - RING))
                tt(flat2(yl, i % RING), wf[:, 512 * (i % RING):512 * (i % RING + 1)], flat2(yh, i % RING).bitcast(F32),
                   ALU.subtract).then_inc(S["yl_dve"], 1)

            for u in range(-AHEAD, NU):
                role, i = UNITS[u][3:] if u >= 0 else ("", 0)
                if role in ("up0", "mqk", "up1", "aq") and i == 0:
                    n = ("up0", "mqk", "up1", "aq").index(role)
                    postnorm(n)
                    prenorm(n + 1)
                s = u + AHEAD
                if s < NU and s % 2 == 0:
                    split(s)
                if u < 0:
                    continue
                if EVAC.get(role) == "dve":
                    wait_used(eng, u)
                if role in ("rq", "rk"):
                    rope(u)
                elif role == "ada":
                    tensor(modp[:, 2 * i:2 * i + 2, :].rearrange("p a b -> p (a b)"), bank(u)[:, 0:4]).then_inc(S["evac_dve"], 1)
                elif role in ("up0", "up1"):
                    ts(wf[:, 512 * (i % RING):512 * (i % RING + 1)], bank(u)[:, :], 0.0, None, ALU.max).then_inc(S["evac_dve"], 1)
                elif role == "mqk":
                    conv_taps(u)
                elif role == "cx":
                    short_conv(u)
                elif role == "cb":
                    tt(c_y[:, 2 * i:2 * i + 2, :].rearrange("p k t -> p (k t)"), bank(u)[:, :],
                       c_y[:, 2 * i:2 * i + 2, :].rearrange("p k t -> p (k t)"), ALU.mult).then_inc(S["evac_dve"], 1)
                elif role == "cg":
                    wait_evac(eng, u)
                    eng.wait_ge(S["evac_dve"], evac_value(u - 1))
                    pair = c_y[:, 2 * i:2 * i + 2, :].rearrange("p k t -> p (k t)")
                    tt(pair, pair, c_t, ALU.mult).then_inc(S["y_src"], 1)
                if u >= 1 and UNITS[u - 1][3] in ("up0", "up1"):
                    hidden_low(0 if UNITS[u - 1][3] == "up0" else 1, UNITS[u - 1][4])

                if u == at("hf", 1):
                    wait_evac(eng, u)
                    for h in range(HEADS):
                        m = ts(g_b[:, h * SEQ:(h + 1) * SEQ], g_qk[:, h, 1, :], lbs[:, 1, h:h + 1], lbs[:, 0, h:h + 1],
                               ALU.mult, ALU.add)
                    m.then_inc(S["f"], 1)
                    eng.wait_ge(S["f"], 1)
                    ts(g_qk[:, :, 1, :], g_b.rearrange("p (h t) -> p h t", h=HEADS), -1.0, 1.0, ALU.mult,
                       ALU.add).then_inc(S["k_hg"], 1)
                    eng.wait_ge(S["hl"], KT)
                    link(eng.memset(wf[:, 0:1024], 0.0))
                if u == at("hq"):
                    eng.wait_ge(S["lf"], 1)
                    eng.wait_ge(S["k_hg"], 1)
                    eng.wait_ge(S["d_tables"], 16)
                    for h in range(HEADS):
                        c = slice(h * SEQ, (h + 1) * SEQ)
                        m = eng.tensor_tensor_scan(g_b[:, c], reset, g_lf[:, c], 0.0, ALU.mult, ALU.add)
                    m.then_inc(S["b"], 1)
                    eng.wait_ge(S["b"], 1)
                if u == at("hq", 1):
                    wait_evac(eng, u)
                for j in range(len(items)):
                    if u == item_unit(j) + 2:
                        level_pick(j)
                for j in range(len(items)):
                    if u == item_unit(j) + 1:
                        level_queries(j)
                for j in range(len(items)):
                    if u == item_unit(j):
                        level_decays(j)
                if u == item_unit(17) + 3:
                    eng.wait_ge(S["hout"], 1)
                    eng.wait_ge(S["rmm"], 1)
                    for h in range(HEADS):
                        o = wf[:, 512 * h:512 * h + 384]
                        tt(o[:, 0:SEQ], PS[4 + h][:, 0:SEQ], ret_dec[:, h, :], ALU.mult)
                        tt(o[:, SEQ:SEQ + P], PS[4 + h][:, SEQ:SEQ + P], ret_dec[:, h, 0:P], ALU.mult).then_inc(S["rdec"], 1)
                if u == last_of("rgate"):
                    eng.wait_ge(S["hsd"], 1)
                    eng.reciprocal(rs[:, 0:8], sd[:, 0:8]).then_inc(S["hrs"], 1)
                    wait_evac(eng, at("hgate", 1))
                    eng.wait_ge(S["hev"], 2)
                    link(stt(g_gate, g_gate, col1[:, R_HG:R_HG + 1], g_o, ALU.mult, ALU.mult))
                    eng.wait_ge(S["hbc"], 1)
                    for b in range(2):
                        tt(g_o[:, 512 * b:512 * (b + 1)], g_gate[:, 512 * b:512 * (b + 1)], PS[2 + b][:, :],
                           ALU.mult).then_inc(S["y_src"], 1)
                if u == at("ada", 3):
                    eng.wait_ge(S["rsd"], 1)
                    eng.reciprocal(rs[:, 8:16], sd[:, 8:16]).then_inc(S["rrs"], 1)
                    wait_evac(eng, last_of("rgate"))
                    eng.wait_ge(S["rev"], 8)
                    for g in range(2):
                        m = stt(r_gate[:, g::2, :], r_gate[:, g::2, :], col1[:, R_RET + g:R_RET + g + 1],
                                r_qk[:, :, g, :], ALU.mult, ALU.mult)
                    link(m)
                    eng.wait_ge(S["rbc"], 1)
                    for h in range(HEADS):
                        b = PS[5 + h // 2][:, (h % 2) * SEQ:(h % 2 + 1) * SEQ].unsqueeze(1).broadcast_to([P, 2, SEQ])
                        tt(r_gate[:, 2 * h:2 * h + 2, :], r_gate[:, 2 * h:2 * h + 2, :], b, ALU.mult).then_inc(S["y_src"], 1)
                if u == at("out0", 1):
                    wait_evac(eng, last_of("ada"))
                    link(tt(mod[:, :], modp[:, :, 0], modp[:, :, 1], ALU.add))
                    link(tt(mod[:, :], mod[:, :], col2[:, R2_BADA:R2_BADA + 24], ALU.add))
                    link(stt(gs[:, :], mod[:, KT:2 * KT], 1.0, col2[:, R2_NORM:R2_NORM + KT], ALU.add, ALU.mult))

                if u == at("mqk"):
                    eng.wait_ge(S["gmm"], 1)
                    eng.wait_ge(S["d_wg"], 32)
                    tt(gz[:, :, :], PS[4][:, 0:16].rearrange("p (t j) -> p t j", t=2),
                       gzb[:, :].unsqueeze(1).broadcast_to([P, 2, 8]), ALU.add).then_inc(S["gz"], 1)
                    eng.wait_ge(S["gcap"], 1)
                    ts(gz[:, :, :], gcap[:, :, :], CAP, None, ALU.mult).then_inc(S["gz"], 1)
                if u == at("mqk", 2):
                    eng.wait_ge(S["gbm"], 1)
                    tt(gg[:, :, :], gz[:, :, 0:4], PS[4][:, 32:40].rearrange("p (t j) -> p t j", t=2), ALU.add)
                    tensor(gB[:, :, :], PS[4][:, 32:40].rearrange("p (t j) -> p t j", t=2)).then_inc(S["g"], 1)
                if u == at("mqk", 3):
                    eng.wait_ge(S["gT"], 1)
                    link(tensor(gT, PS[7][0:HEADS, 0:SEQ]))
                    eng.tensor_tensor_scan(MT, gT, gT, 0.0, ALU.max, ALU.max).then_inc(S["M"], 1)
                for h in range(HEADS):
                    if u == at("mv", h):
                        if h == 0:
                            eng.wait_ge(S["Mb"], 1)
                            tt(gm[:, :, :], gB[:, :, :], PS[7][:, 256:264].rearrange("p (t j) -> p t j", t=2),
                               ALU.subtract).then_inc(S["fls"], 1)
                        mb = PS[5 + h // 2][:, (h % 2) * SEQ:(h % 2 + 1) * SEQ]
                        stt(m_w[:, h, 0:SEQ], mb, gg[:, 0, h:h + 1], causal, ALU.subtract, ALU.add)
                        stt(m_w[:, h, SEQ:384], mb[:, P:SEQ], gg[:, 1, h:h + 1], causal[:, 0:P], ALU.subtract,
                            ALU.add).then_inc(S["warg"], 1)
                    if u == at("mv", h) + 1:
                        eng.wait_ge(S["msc"], h + 1)
                        eng.wait_ge(S["w"], h + 1)
                        stt(m_s[:, h, :], PS[2 + h % 2][:, 0:384], QK_SCALE, m_w[:, h, :], ALU.mult,
                            ALU.mult).then_inc(S["ms"], 1)
                if u == last_of("mog"):
                    eng.wait_ge(S["mout"], 4)
                    link(tensor(gden[:, :, :], PS[4][:, 64:72].rearrange("p (t h) -> p t h", t=2)))
                    link(stt(gdi[:, :, :], gden[:, :, :], -1.0, gden[:, :, :], ALU.mult, ALU.max))
                    eng.wait_ge(S["fl"], 1)
                    link(tt(gdi[:, :, :], gdi[:, :, :], gm[:, :, :], ALU.max))
                    link(eng.reciprocal(gden[:, :, :], gdi[:, :, :]))
                    eng.wait_ge(S["mst"], 1)
                    by_t = gc[:, :].rearrange("p (h t) -> p t h", t=2)
                    link(tt(by_t, PS[7][:, 0:8].rearrange("p (h t) -> p t h", t=2), gden[:, :, :], ALU.mult))
                    tt(by_t, by_t, gden[:, :, :], ALU.mult).then_inc(S["mvar"], 1)
                    eng.wait_ge(S["msd"], 1)
                    link(eng.reciprocal(rs[:, 0:8], sd[:, 0:8]))
                    tt(by_t, rs[:, 0:8].rearrange("p (h t) -> p t h", t=2), gden[:, :, :], ALU.mult).then_inc(S["mc"], 1)
                    wait_evac(eng, u)
                    for g in range(2):
                        m = stt(m_og[:, g::2, :], m_og[:, g::2, :], col1[:, R_ML + g:R_ML + g + 1], m_o[:, g::2, :],
                                ALU.mult, ALU.mult)
                    link(m)
                    eng.wait_ge(S["mbc"], 1)
                    for h in range(HEADS):
                        b = PS[2 + h // 2][:, (h % 2) * SEQ:(h % 2 + 1) * SEQ].unsqueeze(1).broadcast_to([P, 2, SEQ])
                        tt(m_og[:, 2 * h:2 * h + 2, :], m_og[:, 2 * h:2 * h + 2, :], b, ALU.mult).then_inc(S["y_src"], 1)

                for h in range(ATT_HEADS):
                    if u == a_unit(h) + 4:
                        att_gate(h)
                for h in range(ATT_HEADS):
                    if u == a_unit(h) + 2:
                        att_norm(h)
                for h in range(ATT_HEADS):
                    if u == a_unit(h) + 1:
                        att_logits(h)
                if u == last_of("out4"):
                    eng.wait_ge(S["yl_pool"], y_pairs_before(5, False))
                    for b in range(4):
                        wait_acc(eng, 4, b)
                        tensor(y_conv[:, 2 * b:2 * b + 2, :].rearrange("p k t -> p (k t)"), PS[4 + b][:, :]).then_inc(S["acc_free4"], 1)
                if role == "mc":
                    wait_evac(eng, u)
                    eng.wait_ge(S["acc_free4"], i + 1)
                    tt(o_mc[:, 2 * i:2 * i + 2, :], o_mc[:, 2 * i:2 * i + 2, :], y_conv[:, 2 * i:2 * i + 2, :],
                       ALU.mult).then_inc(S["mcm"], 1)
                if u == last_of("out5"):
                    for b in range(4):
                        wait_acc(eng, 5, b)
                        wait_evac(eng, at("ma", b))
                        pair = o_ma[:, 2 * b:2 * b + 2, :].rearrange("p k t -> p (k t)")
                        tt(pair, PS[4 + b][:, :], pair, ALU.mult).then_inc(S["acc_free5"], 1)
                        eng.wait_ge(S["acc_free5"], b + 1)
                        eng.wait_ge(S["mcm"], b + 1)
                        tt(pair, pair, o_mc[:, 2 * b:2 * b + 2, :].rearrange("p k t -> p (k t)"), ALU.add).then_inc(S["merged"], 1)

            for g in range(KT):
                if g % 2 == 0:
                    wait_acc(eng, 6, g // 2)
                stt(xT[:, g, :], acc_group(g), mod[:, 2 * KT + g:2 * KT + g + 1], xT[:, g, :], ALU.mult,
                    ALU.add).then_inc(S["x_last"], 1)
            prenorm(5)

        @block.scalar
        def _(eng):
            def act(o, x, f, **more):
                return eng.activation(o, x, f, **more)

            def high(u):
                eng.wait_ge(raw_sem[u % RING], 16 * (u // RING + 1))
                if u >= RING:
                    wait_used(eng, u - RING)
                eng.copy(wh[:, u % RING, :], raw[:, u % RING, :]).then_inc(S["hi"], 1)

            def root(o, stat, n):
                return act(o, stat, ACT.Sqrt, scale=1.0 / n, bias=eps[:, 0:1])

            def prenorm(n):
                for g in range(KT):
                    if n == 0:
                        eng.wait_ge(S["xcopy"], g // 2 + 1)
                    elif n < 5:
                        eng.wait_ge(S["x_new"], KT * n - KT + g + 1)
                    else:
                        eng.wait_ge(S["x_last"], g + 1)
                    act(work[:, g, :], xT[:, g, :], ACT.Square).then_inc(S["xsq"], 1)
                eng.wait_ge(S["xstat"], n + 1)
                if n == 0:
                    eng.wait_ge(S["const"], 2)
                root(sd[:, 0:2], PS[2][:, 0:2], D).then_inc(S["xsd"], 1)
                if n < 5:
                    for g in range(KT):
                        eng.wait_ge(S["h"], KT * n + g + 1)
                        eng.copy(hh[:, g, :], work[:, g, :]).then_inc(S["hh"], 1)

            def postnorm(n):
                for b in range(4):
                    wait_acc(eng, n, b)
                    act(work[:, 2 * b:2 * b + 2, :].rearrange("p k t -> p (k t)"), PS[4 + b][:, :],
                        ACT.Square).then_inc(S["ysq"], 1)
                eng.wait_ge(S["ystat"], n + 1)
                root(sd[:, 2:4], PS[2][:, 4:6], D).then_inc(S["ysd"], 1)
                eng.wait_ge(S["ybc"], n + 1)
                eng.copy(ybs, PS[3][:, SEQ:2 * SEQ]).then_inc(S["ybs"], 1)

            def y_high(p, i):
                if p in (0, 2, 4):
                    eng.wait_ge(S["y_src"], {0: 0, 2: 6, 4: 10}[p] + i + 1)
                elif p == 5:
                    eng.wait_ge(S["aout_v"], 2 * i + 2)
                    wait_used(eng, at("out4", i))
                else:
                    eng.wait_ge(S["merged"], i + 1)
                eng.copy(flat2(yh, i), y_source(p, i)).then_inc(S["yh"], 1)

            small = (
                (ident[:, :], a["tbl"][:, T_IDENT:T_IDENT + P]),
                (rows1[0:ROWS1, :], a["rows1"]),
                (rows2[0:ROWS2, :], a["rows2"]),
                (rel_in, a["rel_bias"]),
                (onehot, a["tbl"][0:32, T_ONEHOT:T_ONEHOT + SEQ]),
                (g_lf, a["tbl"][:, T_MASKS:T_END]),
            )
            for dst, src in small:
                eng.dma_start(dst, src).then_inc(S["d_small"], 16)
            eng.dma_start(tables[:, :], a["tbl"][:, 0:T_CAUSAL]).then_inc(S["d_tables"], 16)
            eng.dma_start(wg[:, :, :], a["od_w_in"][:, 3072:3080].rearrange("(k p) c -> p k c", p=P)).then_inc(S["d_wg"], 16)
            eng.dma_start(gzb[:, :], a["gate_b"].broadcast_to([P, 8])).then_inc(S["d_wg"], 16)
            eng.wait_ge(S["cols"], 2)
            act(cf[:, :], col2[:, R2_C:R2_C + KT], ACT.Silu).then_inc(S["c_act"], 1)
            prenorm(0)
            eng.wait_ge(S["low"], 3)
            act(lb[:, :, :], lb[:, :, :], ACT.Exp).then_inc(S["lowe"], 1)
            eng.wait_ge(S["u"], 1)
            eng.dma_start(scratch_dram, u_row).then_inc(S["d_u"], 16)

            for u in range(-AHEAD, NU):
                role, i = UNITS[u][3:] if u >= 0 else ("", 0)
                if role in ("up0", "mqk", "up1", "aq") and i == 0:
                    n = ("up0", "mqk", "up1", "aq").index(role)
                    postnorm(n)
                    prenorm(n + 1)
                if u + AHEAD < NU:
                    high(u + AHEAD)
                if u < 0:
                    continue
                if EVAC.get(role) == "act":
                    wait_used(eng, u)
                ps = bank(u)[:, :] if u in A_OF else None
                pair = ps.rearrange("p (h t) -> p h t", h=2) if u in A_OF else None
                if role == "hf":
                    act(g_qk[:, 2 * i:2 * i + 2, 1, :], pair, ACT.Sigmoid).then_inc(S["evac_act"], 1)
                elif role == "hq":
                    act(g_qk[:, 2 * i:2 * i + 2, 0, :], pair, ACT.Silu).then_inc(S["evac_act"], 1)
                elif role == "hi":
                    eng.copy(g_v[:, :, i * UCOLS:(i + 1) * UCOLS], pair).then_inc(S["evac_act"], 1)
                elif role == "rv":
                    eng.copy(r_v[:, :, i * UCOLS:(i + 1) * UCOLS], pair).then_inc(S["evac_act"], 1)
                elif role == "hgate":
                    act(g_gate[:, 512 * i:512 * (i + 1)], ps, ACT.Silu).then_inc(S["evac_act"], 1)
                elif role == "rgate":
                    if i == 0:
                        eng.wait_ge(S["d_u"], 16)
                    act(r_gate[:, 2 * i:2 * i + 2, :], pair, ACT.Silu).then_inc(S["evac_act"], 1)
                elif role == "mv":
                    eng.copy(m_v[:, :, i * UCOLS:(i + 1) * UCOLS], pair).then_inc(S["evac_act"], 1)
                elif role == "mog":
                    act(m_og[:, 2 * i:2 * i + 2, :], pair, ACT.Sigmoid).then_inc(S["evac_act"], 1)
                elif role in ("aq", "ak"):
                    eng.copy((a_q if role == "aq" else a_k)[:, 2 * i:2 * i + 2, :], pair).then_inc(S["evac_act"], 1)
                elif role == "av":
                    eng.copy(a_v[:, :, i * UCOLS:(i + 1) * UCOLS], pair).then_inc(S["evac_act"], 1)
                elif role == "ag":
                    act(a_g[:, 2 * i:2 * i + 2, :], pair, ACT.Silu).then_inc(S["evac_act"], 1)
                elif role == "cc":
                    eng.wait_ge(S["y_src"], 10 + i)
                    eng.copy(c_u, ps).then_inc(S["evac_act"], 1)
                elif role == "cg":
                    if i >= 1:
                        eng.wait_ge(S["y_src"], 10 + i)
                    act(c_t, ps, ACT.Silu).then_inc(S["evac_act"], 1)
                elif role in ("mc", "ma"):
                    if i == 0:
                        eng.wait_ge(S["asc"], ATT_HEADS)
                    act((o_mc if role == "mc" else o_ma)[:, 2 * i:2 * i + 2, :], pair, ACT.Sigmoid).then_inc(S["evac_act"], 1)
                elif role in ("up0", "up1"):
                    layer = 0 if role == "up0" else 1
                    c = slice(512 * (i % RING), 512 * (i % RING + 1))
                    eng.wait_ge(S["evac_dve"], evac_value(u))
                    act(wf[:, c], wf[:, c], ACT.Square).then_inc(S["sq"], 1)
                    eng.wait_ge(S["sq"], 16 * layer + i + 1)
                    if i >= RING:
                        wait_used(eng, at(f"out{2 * layer + 1}", i - RING))
                    eng.copy(flat2(yh, i % RING), wf[:, c]).then_inc(S["yh"], 1)
                elif role == "mqk":
                    eng.wait_ge(S["evac_dve"], evac_value(u))
                    act(m_qk[:, 2 * i:2 * i + 2, :], m_qk[:, 2 * i:2 * i + 2, :], ACT.Silu).then_inc(S["qk"], 1)

                if u == at("hf", 1):
                    eng.wait_ge(S["f"], 1)
                    eng.wait_ge(S["masks"], 1)
                    act(g_lf, g_b, ACT.Ln).then_inc(S["lf"], 1)
                for j in range(len(items)):
                    if u == item_unit(j) and items[j][1] != 7:
                        eng.wait_ge(S["diff"], decays_to(j))
                        act(scr1[:, j % 2, :], scr1[:, j % 2, :], ACT.Exp).then_inc(S["e"], 1)
                if u == item_unit(17) + 2:
                    eng.wait_ge(S["hout"], 1)
                    for b in range(2):
                        eng.copy(g_o[:, 512 * b:512 * (b + 1)], PS[2 + b][:, :]).then_inc(S["hev"], 1)
                        m = act(g_sq[:, 512 * b:512 * (b + 1)], PS[2 + b][:, :], ACT.Square)
                    m.then_inc(S["hsq"], 1)
                if u == item_unit(17) + 3:
                    eng.wait_ge(S["hst"], 1)
                    root(sd[:, 0:8], PS[3][:, 0:8], DK).then_inc(S["hsd"], 1)
                if u == at("ada"):
                    for h in range(HEADS):
                        eng.wait_ge(S["rout"], h + 1)
                        eng.copy(r_qk[:, h, :, :].rearrange("p a b -> p (a b)"), PS[4 + h][:, :]).then_inc(S["rev"], 1)
                        act(wf[:, 512 * h:512 * (h + 1)], PS[4 + h][:, :], ACT.Square).then_inc(S["rev"], 1)
                if u == at("ada", 2):
                    eng.wait_ge(S["rst"], 1)
                    root(sd[:, 8:16], PS[4][:, 0:8], RET_DV).then_inc(S["rsd"], 1)
                for p, where in ((0, at("ada")), (0, at("ada", 3))):
                    if u == where:
                        for j in (range(2) if where == at("ada") else range(2, 6)):
                            y_high(p, j)

                if u == at("mqk"):
                    eng.wait_ge(S["gz"], 1)
                    act(gcap[:, :, :], gz[:, :, :], ACT.Tanh, scale=1.0 / CAP).then_inc(S["gcap"], 1)
                    eng.wait_ge(S["gz"], 2)
                    act(glf[:, :, :], gz[:, :, 4:8], ACT.Exp, scale=-1.0).then_inc(S["gle"], 1)
                    eng.wait_ge(S["gle"], 1)
                    act(glf[:, :, :], glf[:, :, :], ACT.Ln, bias=ones[:, 0:1]).then_inc(S["gsp"], 1)
                for h in range(HEADS):
                    if u == at("mv", h):
                        if h == 0:
                            eng.wait_ge(S["fls"], 1)
                            act(gm[:, :, :], gm[:, :, :], ACT.Exp).then_inc(S["fl"], 1)
                        eng.wait_ge(S["warg"], h + 1)
                        act(m_w[:, h, :], m_w[:, h, :], ACT.Exp, scale=-1.0).then_inc(S["w"], 1)
                    if u == at("mog", h):
                        eng.wait_ge(S["mout"], h + 1)
                        eng.wait_ge(S["msc"], HEADS)
                        eng.copy(m_o[:, 2 * h:2 * h + 2, :].rearrange("p k t -> p (k t)"), PS[5 + h % 2][:, :]).then_inc(S["mev"], 1)
                        act(m_sq[:, h, :], PS[5 + h % 2][:, :], ACT.Square).then_inc(S["mev"], 1)
                if u == last_of("mog"):
                    eng.wait_ge(S["mvar"], 1)
                    root(sd[:, 0:8], gc[:, :], RET_DV).then_inc(S["msd"], 1)
                    for j in range(4):
                        y_high(2, j)

                for h in range(ATT_HEADS):
                    if u == a_unit(h) + 3:
                        eng.wait_ge(S["tr"], h + 1)
                        if h >= 2:
                            eng.wait_ge(S["aout"], h - 1)
                        eng.copy(wf[:, 768 + 384 * (h % 2):768 + 384 * (h % 2 + 1)], PS[4 + h % 2][:, 0:384]).then_inc(S["pt"], 1)
                for h in range(ATT_HEADS):
                    if u == a_unit(h) + 1:
                        eng.wait_ge(S["mxn"], h + 1)
                        o = wf[:, 384 * (h % 2):384 * (h % 2 + 1)]
                        act(o[:, 0:P], o[:, 0:P], ACT.Exp, bias=mx[:, h % 2, 0:1], accum_out=sm[:, h % 2, 0:1])
                        act(o[:, P:384], o[:, P:384], ACT.Exp, bias=mx[:, h % 2, 1:2],
                            accum_out=sm[:, h % 2, 1:2]).then_inc(S["aexp"], 1)
                if role == "cg":
                    y_high(4, i)
                if role == "mc":
                    y_high(5, i)
                if u == last_of("out5"):
                    for j in range(4):
                        y_high(6, j)

            prenorm(5)
            for b in range(4):
                tt_, k = b // 2, b % 2
                eng.wait_ge(S["fin_mm"], k + 1)
            for tt_ in range(TT):
                for k in range(2):
                    eng.copy(fin_t[:, tt_, 512 * k:512 * (k + 1)], PS[4 + 2 * tt_ + k][:, :]).then_inc(S["fin"], 1)

        @block.gpsimd
        def _(eng):
            def split(u):
                eng.wait_ge(raw_sem[u % RING], 16 * (u // RING + 1))
                eng.wait_ge(S["hi"], u + 1)
                if u >= RING:
                    wait_used(eng, u - RING)
                eng.tensor_tensor(wl[:, u % RING, :], raw[:, u % RING, :], wh[:, u % RING, :].bitcast(F32),
                                  ALU.subtract).then_inc(S["lo_pool"], 1)

            def prenorm(n):
                for g in range(KT):
                    eng.wait_ge(S["hh"], KT * n + g + 1)
                    eng.tensor_tensor(hl[:, g, :], work[:, g, :], hh[:, g, :].bitcast(F32), ALU.subtract).then_inc(S["hl"], 1)

            def postnorm(n):
                for g in range(KT):
                    eng.wait_ge(S["t"], KT * n + g + 1)
                    eng.tensor_tensor(xT[:, g, :], xT[:, g, :], work[:, g, :], ALU.add).then_inc(S["x_new"], 1)

            def y_low(p, i):
                eng.wait_ge(S["yh"], y_pairs_before(p, True) + i + 1)
                eng.tensor_tensor(flat2(yl, i), y_source(p, i), flat2(yh, i).bitcast(F32), ALU.subtract).then_inc(S["yl_pool"], 1)

            prenorm(0)
            for u in range(-AHEAD, NU):
                role, i = UNITS[u][3:] if u >= 0 else ("", 0)
                if role in ("up0", "mqk", "up1", "aq") and i == 0:
                    n = ("up0", "mqk", "up1", "aq").index(role)
                    postnorm(n)
                    prenorm(n + 1)
                s = u + AHEAD
                if s < NU and s % 2 == 1:
                    split(s)
                if u < 0:
                    continue
                for j in range(len(items)):
                    if u == item_unit(j) + 1 and items[j][1] != 7:
                        half = items[j][0]
                        eng.wait_ge(S["e"], decays_to(j))
                        if j >= 2:
                            eng.wait_ge(S["smm"], j - 1)
                        eng.tensor_tensor(scr2[:, j % 2, :].rearrange("p (h t) -> p h t", h=2),
                                          g_qk[:, 2 * half:2 * half + 2, 1, :],
                                          scr1[:, j % 2, :].rearrange("p (h t) -> p h t", h=2), ALU.mult).then_inc(S["k"], 1)
                if u == at("ada"):
                    for j in range(2):
                        y_low(0, j)
                if u == at("ada", 3):
                    for j in range(2, 6):
                        y_low(0, j)
                if u == last_of("mog"):
                    for j in range(4):
                        y_low(2, j)
                if role == "cg":
                    y_low(4, i)
                if role == "mc":
                    y_low(5, i)
                if u == last_of("out5"):
                    for j in range(4):
                        y_low(6, j)


def kernel(**inputs):
    from concourse import bacc
    from concourse.bass_utils import run_bass_kernel_spmd

    x = {k: np.asarray(v) for k, v in inputs.items()}
    tbl = shape_tables()

    def rows(*parts):
        return np.concatenate([np.ascontiguousarray(p).reshape(-1, P) for p in parts], 0)

    arrays = {
        "x": x["x"][0], "tbl": tbl,
        "rows1": rows(x["norm_g"], x["hg_lower_bound"], x["ev_hg_norm_g"], x["ev_ret_norm_g"], x["od_conv_w"],
                      x["od_conv_b"], x["od_ml_norm_g"]),
        "rows2": rows(x["c_2"], x["norm_g_2"], x["b_ada_2"], x["conv_w_2"], x["final_g_2"]),
        "rel_bias": x["rel_bias_2"], "gate_b": x["od_gate_b"].reshape(1, 8),
        "ev_w_in": x["ev_w_in"][0], "ev_w_out": x["ev_w_out"][0], "od_w_in": x["od_w_in"][0],
        "od_w_out": x["od_w_out"][0], "mlp_w1_0": x["mlp_w1"][0], "mlp_w1_1": x["mlp_w1"][1],
        "mlp_w2_0": x["mlp_w2"][0], "mlp_w2_1": x["mlp_w2"][1], "w_ada": x["w_ada_2"][0], "w_in": x["w_in_2"][0],
        "w_o_attn": x["w_o_attn_2"][0], "w_o_conv": x["w_o_conv_2"][0], "w_out": x["w_out_2"][0],
    }
    arrays = {f"in_{k}": np.ascontiguousarray(v) for k, v in arrays.items()}
    nc = bacc.Bacc("TRN2", target_bir_lowering=False, num_devices=1)
    aps = {k[3:]: nc.dram_tensor(k, v.shape, mybir.dt.from_np(v.dtype), kind="ExternalInput").ap()
           for k, v in arrays.items()}
    out = nc.dram_tensor("out", (SEQ, D), F32, kind="ExternalOutput").ap()
    build(nc, aps, out)
    r = run_bass_kernel_spmd(nc, [arrays], core_ids=[0])
    return r.results[0]["out"].reshape(1, SEQ, D)
```

```python
from contextlib import ExitStack

import numpy as np

import concourse.bass as bass
from concourse import mybir

F32 = mybir.dt.float32
F32R = mybir.dt.float32r
U8 = mybir.dt.uint8
ALU = mybir.AluOpType
ACT = mybir.ActivationFunctionType
AX_X = mybir.AxisListType.X

P = 128
D = 1024
SEQ = 256
KT = D // P
TT = SEQ // P
CHUNK = 64
HEADS = 4
DK = 128
RET_DV = 256
FF = 4096
ATT_HEADS = 8
EPS = 1e-6
CAP = 15.0
QK_SCALE = float(np.float32(128.0) ** -0.5)
MASKED = 1e30

UCOLS = 256
UELEMS = KT * UCOLS
RING = 4
AHEAD = 3

T_COS, T_SIN = 0, 256
T_RET = 512
T_RESET = 1536
T_CAUSAL = 1792
T_UPPER = 2048
T_IDENT = 2176
T_ONEHOT = 2304
T_MASKS = 2560
T_END = 3584
LEVELS = (64, 32, 16, 8, 4, 2, 1)

R_NORM = 0
R_LOWER = 64
R_HG, R_RET = 76, 77
R_CONVW, R_CONVB = 79, 111
R_ML = 119
ROWS1 = 121
R2_C, R2_NORM, R2_BADA, R2_CONVW, R2_FINAL = 0, 8, 16, 40, 64
ROWS2 = 72


def shape_tables():
    f32 = np.float32
    tbl = np.zeros((P, T_END), f32)
    half = P // 2
    inv = (f32(10000.0) ** (-np.arange(half, dtype=f32) / f32(half))).astype(f32)
    ang = (np.arange(SEQ, dtype=f32)[:, None] * inv[None, :]).astype(f32)
    cos, sin = np.cos(ang).T, np.sin(ang).T
    tbl[:half, T_COS:T_COS + SEQ] = cos
    tbl[half:, T_COS:T_COS + SEQ] = cos
    tbl[:half, T_SIN:T_SIN + SEQ] = sin
    tbl[half:, T_SIN:T_SIN + SEQ] = -sin
    s = np.arange(P, dtype=np.float64)[:, None]
    t = np.arange(SEQ, dtype=np.float64)[None, :]
    for h in range(HEADS):
        log_g = np.log1p(-np.exp2(-5.0 - h))
        dec = np.where(t >= s, np.exp(log_g * np.maximum(t - s, 0.0)), 0.0)
        tbl[:, T_RET + h * SEQ:T_RET + (h + 1) * SEQ] = dec * float(DK) ** -0.5
    tbl[:, T_RESET:T_RESET + SEQ] = (np.arange(SEQ) % CHUNK != 0)[None, :]
    tbl[:, T_CAUSAL:T_CAUSAL + SEQ] = np.where(t >= s, 0.0, MASKED)
    tbl[:, T_UPPER:T_UPPER + P] = t[:, :P] >= s
    tbl[:, T_IDENT:T_IDENT + P] = np.eye(P)
    n = np.arange(SEQ)
    large = 16 + (np.log(np.maximum(n, 1).astype(f32) / f32(16)) / f32(np.log(8.0)) * f32(16)).astype(np.int32)
    bucket = np.where(n < 16, n, np.minimum(large, 31))
    tbl[:32, T_ONEHOT:T_ONEHOT + SEQ] = np.arange(32)[:, None] == bucket[None, :]
    masks = np.zeros((P, len(LEVELS) + 1, P), f32)
    i = np.arange(P)
    for n_level, m in enumerate(LEVELS):
        same = (i[:, None] // (2 * m)) == (i[None, :] // (2 * m))
        masks[:, n_level] = same & (i[:, None] % (2 * m) < m) & (i[None, :] % (2 * m) >= m)
    masks[:, len(LEVELS)] = np.eye(P)
    tbl[:, T_MASKS:T_END] = masks.reshape(P, -1)
    return tbl


def weight_units():
    A, B = "A", "B"
    us = []

    def cols(w, c0, n, role):
        us.extend((A, w, c0 + UCOLS * i, role, i) for i in range(n // UCOLS))

    def rows(w, n, role):
        us.extend((B, w, 2 * P * i, role, i) for i in range(n // (2 * P)))

    cols("ev_w_in", 512, 512, "hf")
    cols("ev_w_in", 0, 512, "hq")
    cols("ev_w_in", 1024, 512, "hi")
    cols("ev_w_in", 2048, 512, "rq")
    cols("ev_w_in", 2560, 512, "rk")
    cols("ev_w_in", 3072, 1024, "rv")
    cols("ev_w_in", 4096, 1024, "rgate")
    cols("ev_w_in", 1536, 512, "hgate")
    us.extend(("B", "ev_w_out", (512 + 2 * P * i) % 1536, "out0", i) for i in range(6))
    mlp(us, 0)
    cols("od_w_in", 0, 1024, "mqk")
    cols("od_w_in", 1024, 1024, "mv")
    cols("od_w_in", 2048, 1024, "mog")
    rows("od_w_out", 1024, "out2")
    mlp(us, 1)
    cols("w_in", 0, 1024, "aq")
    cols("w_in", 1024, 1024, "ak")
    cols("w_in", 2048, 1024, "av")
    cols("w_in", 3072, 1024, "ag")
    for c in range(4):
        for role, c0 in (("cc", 5120), ("cx", 6144), ("cb", 4096), ("cg", 7168)):
            us.append((A, "w_in", c0 + UCOLS * c, role, c))
    rows("w_o_conv", 1024, "out4")
    cols("w_in", 9216, 1024, "mc")
    cols("w_in", 8192, 1024, "ma")
    rows("w_o_attn", 1024, "out5")
    rows("w_out", 1024, "out6")
    return us


def mlp(us, layer):
    for j in range(9):
        if 1 <= j < 7:
            us.append(("C", "w_ada", UCOLS * (6 * layer + j - 1), "ada", 6 * layer + j - 1))
        if j < 8:
            us.extend(("A", f"mlp_w1_{layer}", 512 * j + UCOLS * i, f"up{layer}", 2 * j + i) for i in range(2))
        if j >= 1:
            us.extend(("B", f"mlp_w2_{layer}", 512 * (j - 1) + 2 * P * i, f"out{2 * layer + 1}", 2 * (j - 1) + i)
                      for i in range(2))


UNITS = weight_units()
NU = len(UNITS)
A_OF = {}
SPLIT_OF = {}
for _u, _it in enumerate(UNITS):
    if _it[0] == "A":
        A_OF[_u] = len(A_OF)
    if _it[0] != "C":
        SPLIT_OF[_u] = len(SPLIT_OF)
EVAC = {"hf": "act", "hq": "act", "hi": "act", "rq": "dve", "rk": "dve", "rv": "act", "hgate": "act",
        "rgate": "act", "up0": "dve", "up1": "dve", "mqk": "dve", "mv": "act", "mog": "act",
        "aq": "act", "ak": "act", "av": "act", "ag": "act", "cc": "act", "cx": "dve", "cb": "dve",
        "cg": "act", "mc": "act", "ma": "act"}
FORM = {r: "F" for r in EVAC} | {"hi": "T", "rv": "T", "mv": "T", "av": "T"}
EVAC_UNITS = {e: [u for u in A_OF if EVAC[UNITS[u][3]] == e] for e in ("act", "dve")}
A_UNITS = list(A_OF)
PHASE = {f"out{p}": p for p in range(7)}
PHASE_KT = (12, 32, 8, 32, 8, 8, 8)


def at(role, i=0):
    return next(u for u, it in enumerate(UNITS) if it[3] == role and it[4] == i)


def last_of(role):
    return max(u for u, it in enumerate(UNITS) if it[3] == role)


def build(nc, a, out):
    ctx = ExitStack()
    with ctx:
        cursor = [(nc.sbuf_base + 63) // 64 * 64]

        def place(name, shape, dt, at_byte=None):
            size = int(np.prod(shape[1:])) * (1 if dt == U8 else 4)
            if at_byte is None:
                at_byte = cursor[0]
                cursor[0] += (size + 31) // 32 * 32
            return nc.alloc_sbuf_tensor_at(name, list(shape), dt, offset=at_byte)

        raw = place("raw", (P, RING, UELEMS), F32)
        wh = place("wh", (P, RING, UELEMS), F32R)
        wl = place("wl", (P, RING, UELEMS), F32R)
        xT = place("xT", (P, KT, SEQ), F32)
        hh = place("hh", (P, KT, SEQ), F32R)
        hl = place("hl", (P, KT, SEQ), F32R)
        y_at = cursor[0]
        yh = place("yh", (P, 12, SEQ), F32R)
        yl = place("yl", (P, 12, SEQ), F32R)
        scr1 = place("scr1", (P, 4, 512), F32, y_at + 4096)
        scr2 = place("scr2", (P, 4, 512), F32, y_at + 12288 + 4096)
        work = place("work", (P, KT, SEQ), F32)
        arena = place("arena", (P, 11264), F32)
        tables = place("tables", (P, 1792), F32)
        masks_at = cursor[0]
        masks = place("masks", (P, 8, P), U8)
        bias = place("bias", (P, ATT_HEADS, SEQ), F32, masks_at - 7168)
        ident = place("ident", (P, P), F32)
        col1 = place("col1", (P, ROWS1), F32)
        col2 = place("col2", (P, ROWS2), F32)
        wg = place("wg", (P, KT, 8), F32)
        mod = place("mod", (P, 24), F32)
        cf = place("cf", (P, KT), F32)
        ones = place("ones", (P, 1), F32)
        eps = place("eps", (P, 1), F32)
        sd = place("sd", (P, 16), F32)
        rs = place("rs", (P, 16), F32)
        lb = place("lb", (P, 3, HEADS), F32)
        lbs = place("lbs", (P, 4, HEADS), F32)
        gz = place("gz", (P, 2, 8), F32)
        gzb = place("gzb", (P, 8), F32)
        gcap = place("gcap", (P, 2, 8), F32)
        glf = place("glf", (P, 2, 4), F32)
        gB = place("gB", (P, 2, 4), F32)
        gg = place("gg", (P, 2, 4), F32)
        gm = place("gm", (P, 2, 4), F32)
        gden = place("gden", (P, 2, 4), F32)
        gdi = place("gdi", (P, 2, 4), F32)
        gc = place("gc", (P, 8), F32)
        gs = place("gs", (P, KT), F32)
        mx = place("mx", (P, 2, 2), F32)
        sm = place("sm", (P, 2, 2), F32)
        assert cursor[0] <= nc.sbuf_usable_end, (cursor[0], nc.sbuf_usable_end)

        PS = [ctx.enter_context(nc.psum_tensor(f"bank{i}", [P, 512], F32)) for i in range(8)]
        scratch_dram = nc.dram_tensor("bias_scratch", (ATT_HEADS, 384), F32, kind="Internal").ap()

        names = (
            "raw0 raw1 raw2 raw3 hi lo_dve lo_pool used evac_act evac_dve "
            "d_x d_small d_tables d_causal d_wg d_u d_bias d_out "
            "const d_masks masks cols colsT xin xcopy step_dve step_act lo_ada mod x_dve x_pool yg "
            "xsq xstat xsd xrs xbc h h_part hh hl ysq ystat ysd yrs ybc t x_last acc "
            "low lowe c_act f lf k_hg b diff e q k smm pred hout hev hsq hst hsd hrs hbc "
            "rope rmm rdec rout rev rst rsd rrs rbc y_src yh yl_pool yl_dve sq "
            "gmm gz gcap gsp gbm g gT M Mb fls fl warg w msc ms mout mev mst mvar msd mc mbc qk "
            "u asc lg mxn gle aexp p tr pt aout aout_v mcm merged acc_free4 acc_free5 fin_mm fin"
        ).split()
        S = {n: ctx.enter_context(nc.semaphore("s_" + n)) for n in names}
        raw_sem = [S["raw0"], S["raw1"], S["raw2"], S["raw3"]]
        block = ctx.enter_context(nc.Block())

        wf = work[:, :, :].rearrange("p k t -> p (k t)")
        ar = arena[:, :]

        def view(lo, *dims):
            v = ar[:, lo:lo + int(np.prod(dims))]
            if len(dims) == 1:
                return v
            if len(dims) == 2:
                return v.rearrange("p (a b) -> p a b", a=dims[0])
            return v.rearrange("p (a b c) -> p a b c", a=dims[0], b=dims[1])

        x_in = view(8192, TT, D)
        rows1, rows2 = ar[:, 10240:10368], ar[:, 10368:10496]
        rel_in, onehot = ar[0:32, 10496:10504], ar[0:32, 10512:10768]
        u_row = ar[0:ATT_HEADS, 10768:11152]
        g_qk = view(0, HEADS, 2, SEQ)
        g_b = view(2048, HEADS * SEQ)
        g_v = view(3072, TT, 512)
        g_gate = view(4096, HEADS * SEQ)
        r_qk = view(5120, HEADS, 2, SEQ)
        r_v = view(7168, TT, D)
        r_gate = view(9216, KT, SEQ)
        r_o = view(7168, HEADS, 2, SEQ)
        r_p = view(5120, HEADS, 512)
        g_o, g_sq = view(0, HEADS * SEQ), view(1024, HEADS * SEQ)
        g_lf = scr1[:, 0:2, :].rearrange("p a b -> p (a b)")
        cosT, sinT = tables[:, 0:SEQ], tables[:, SEQ:2 * SEQ]
        ret_dec = tables[:, T_RET:T_RET + HEADS * SEQ].rearrange("p (h t) -> p h t", h=HEADS)
        reset = tables[:, T_RESET:T_RESET + SEQ]
        m_qk = view(0, 2 * HEADS, SEQ)
        m_v = view(2048, TT, D)
        m_og = view(4096, KT, SEQ)
        m_w = view(6144, HEADS, 384)
        m_s = view(7680, HEADS, 384)
        m_o = view(9216, KT, SEQ)
        m_sq = view(0, HEADS, 512)
        causal, upper = tables[:, 0:SEQ], tables[:, SEQ:SEQ + P]
        gT, MT = wf[0:HEADS, 0:SEQ], wf[0:HEADS, SEQ:2 * SEQ]
        a_q, a_k = view(0, KT, SEQ), view(2048, KT, SEQ)
        a_v, a_g = view(4096, TT, D), view(6144, KT, SEQ)
        c_y = view(8192, KT, SEQ)
        c_u, c_t = view(10240, 512), view(10752, 512)
        o_ma, o_mc = view(0, KT, SEQ), view(2048, KT, SEQ)
        y_conv = c_y
        fin_t = view(0, TT, D)
        yg = view(0, KT, SEQ)
        items = [(half, lv) for half in range(2) for lv in range(9)]

        def mod_part(i):
            return view(4096 + UCOLS * (i % 2), UCOLS)

        PRENORM = {at("hf"): 0, at("up0"): 1, at("mqk"): 2, at("up1"): 3, at("aq"): 4}

        ITEM_UNITS = [at("hi", 1) + n for n, c in enumerate((1, 1, 1, 1, 1, 2, 2, 2, 2, 2, 2, 1)) for _ in range(c)]
        assert len(ITEM_UNITS) == len(items)
        SCAN_END = ITEM_UNITS[-1]

        def items_of(u):
            return [j for j in range(len(items)) if ITEM_UNITS[j] == u]

        def decays_to(i):
            return sum(lv != 7 for _, lv in items[:i + 1])

        X_ORDER = (2, 0, 3, 1)

        def x_pairs(n):
            return X_ORDER if 1 <= n <= 4 else (0, 1, 2, 3)

        def a_unit(h):
            return at("cc") - 1 + (3 * h) // 2

        def acc_group(g):
            return PS[4 + g // 2][:, (g % 2) * SEQ:(g % 2 + 1) * SEQ]

        def y_pairs_before(p, mlp_too):
            return sum(PHASE_KT[q] // 2 for q in range(p) if mlp_too or q not in (1, 3))

        def y_source(p, i):
            if p == 0:
                return view(9216 + 512 * i, 512) if i < 4 else view(512 * (i - 4), 512)
            base = {2: 4096, 4: 8192, 5: 6144, 6: 0}[p]
            return view(base + 512 * i, 512)

        def wait_acc(eng, p, b):
            if b < 3:
                eng.wait_ge(S["acc"], 7 * p + 2 * b + 2)
            else:
                wait_used(eng, last_of(f"out{p}"))

        def flat2(t, i):
            return t[:, 2 * i:2 * i + 2, :].rearrange("p k t -> p (k t)")

        def evac_value(u):
            return EVAC_UNITS[EVAC[UNITS[u][3]]].index(u) + 1

        def wait_evac(eng, u):
            eng.wait_ge(S["evac_act"] if EVAC[UNITS[u][3]] == "act" else S["evac_dve"], evac_value(u))

        def wait_used(eng, u):
            eng.wait_ge(S["used"], u + 1)

        def split_by(u):
            return "ada" if u not in SPLIT_OF else "dve" if SPLIT_OF[u] % 2 == 0 else "pool"

        def wait_low(eng, u):
            by = split_by(u)
            if by == "ada":
                eng.wait_ge(S["lo_ada"], UNITS[u][4] + 1)
            else:
                eng.wait_ge(S["lo_dve"] if by == "dve" else S["lo_pool"], SPLIT_OF[u] // 2 + 1)

        def unit_src(u):
            kind, w, c0, _, _ = UNITS[u]
            src = a[w]
            if kind != "B":
                return src[:, c0:c0 + UCOLS].rearrange("(k p) c -> p k c", p=P)
            return src[c0:c0 + 2 * P, :].rearrange("(k p) c -> p k c", p=P)

        def slot(t, u, kind):
            return t[:, u % RING, :].rearrange("p (k c) -> p k c", k=2 if kind == "B" else KT)

        def bank(u):
            return PS[A_OF[u] % 2]

        @block.sync
        def _(eng):
            small = (
                (ident[:, :], a["tbl"][:, T_IDENT:T_IDENT + P]),
                (rows1[0:ROWS1, :], a["rows1"]),
                (rows2[0:ROWS2, :], a["rows2"]),
                (rel_in, a["rel_bias"]),
                (onehot, a["tbl"][0:32, T_ONEHOT:T_ONEHOT + SEQ]),
            )
            for dst, src in small:
                eng.dma_start(dst, src).then_inc(S["d_small"], 16)
            eng.dma_start(x_in, a["x"].rearrange("(t p) d -> p t d", p=P)).then_inc(S["d_x"], 16)
            for u in range(NU):
                if u == 1:
                    eng.dma_start(g_lf, a["tbl"][:, T_MASKS:T_END]).then_inc(S["d_masks"], 16)
                if u == RING:
                    eng.dma_start(tables[:, :], a["tbl"][:, 0:T_CAUSAL]).then_inc(S["d_tables"], 16)
                    eng.dma_start(wg[:, :, :],
                                  a["od_w_in"][:, 3072:3080].rearrange("(k p) c -> p k c", p=P)).then_inc(S["d_wg"], 16)
                    eng.dma_start(gzb[:, :], a["gate_b"].broadcast_to([P, 8])).then_inc(S["d_wg"], 16)
                if u == at("mqk"):
                    eng.wait_ge(S["y_src"], 6)
                    eng.dma_start(tables[:, 0:384], a["tbl"][:, T_CAUSAL:T_CAUSAL + 384]).then_inc(S["d_causal"], 16)
                if u == at("aq"):
                    eng.wait_ge(S["warg"], HEADS)
                    eng.wait_ge(S["gbm"], 1)
                    eng.wait_ge(S["d_u"], 16)
                    src = scratch_dram
                    eng.dma_start(bias[:, :, :], bass.AP(tensor=src.tensor, offset=src.offset,
                                                         ap=[[1, P], [384, ATT_HEADS], [1, SEQ]])).then_inc(S["d_bias"], 16)
                if u >= RING:
                    wait_low(eng, u - RING)
                eng.dma_start(slot(raw, u, UNITS[u][0]), unit_src(u)).then_inc(raw_sem[u % RING], 16)
            eng.wait_ge(S["fin"], 4)
            eng.dma_start(out.rearrange("(t p) d -> p t d", p=P), fin_t).then_inc(S["d_out"], 16)
            eng.wait_ge(S["d_out"], 16)

        @block.tensor
        def _(eng):
            def mm(o, l, r, start, stop):
                return eng.matmul(o, l, r, start=start, stop=stop, skip_group_check=True)

            def a_first(u, norm):
                w_hi, w_lo, o = slot(wh, u, "A"), slot(wl, u, "A"), bank(u)
                for k in range(KT):
                    eng.wait_ge(S["hh"], KT * norm + k + 1)
                    for w in (w_hi, w_lo):
                        for g in range(2):
                            mm(o[:, g * SEQ:(g + 1) * SEQ], w[:, k, g * P:(g + 1) * P], hh[:, k, :],
                               k == 0 and g == 0 and w is w_hi, False)
                for k in range(KT):
                    eng.wait_ge(S["hl"], KT * norm + k + 1)
                    for g in range(2):
                        m = mm(o[:, g * SEQ:(g + 1) * SEQ], w_hi[:, k, g * P:(g + 1) * P], hl[:, k, :],
                               False, k == KT - 1)
                m.then_inc(S["used"], 1)

            def a_forward(u, between):
                role, i = UNITS[u][3:]
                w_hi, w_lo, o = slot(wh, u, "A"), slot(wl, u, "A"), bank(u)
                for g in range(2):
                    if g == 1 and between is not None:
                        between()
                    for k in range(KT):
                        first, last = k == 0, k == KT - 1
                        c = slice(g * P, (g + 1) * P)
                        if FORM[role] == "F":
                            dst = o[:, g * SEQ:(g + 1) * SEQ]
                            mm(dst, w_hi[:, k, c], hh[:, k, :], first, False)
                            mm(dst, w_hi[:, k, c], hl[:, k, :], False, False)
                            m = mm(dst, w_lo[:, k, c], hh[:, k, :], False, last)
                        else:
                            dst = o[:, g * UCOLS:(g + 1) * UCOLS]
                            mm(dst, hh[:, k, c], w_hi[:, k, :], first, False)
                            mm(dst, hh[:, k, c], w_lo[:, k, :], False, False)
                            m = mm(dst, hl[:, k, c], w_hi[:, k, :], False, last)
                m.then_inc(S["used"], 1)

            def mod_sums(u):
                i = UNITS[u][4]
                part = mod_part(i)
                for g in range(2):
                    m = mm(PS[2][:, 8 + 2 * i + g:9 + 2 * i + g], part[:, g * P:(g + 1) * P], ones[:, :], True, True)
                m.then_inc(S["used"], 1)

            def b_forward(u):
                role, i = UNITS[u][3:]
                p = PHASE[role]
                w_hi, w_lo = slot(wh, u, "B"), slot(wl, u, "B")
                kt = 2 * i if p not in (1, 3) else 2 * (i % 4)
                end = i == PHASE_KT[p] // 2 - 1
                for g in range(KT):
                    c = slice(g * P, (g + 1) * P)
                    dst = acc_group(g)
                    for k in range(2):
                        mm(dst, w_hi[:, k, c], yh[:, kt + k, :], i == 0 and k == 0 and g % 2 == 0, False)
                        mm(dst, w_hi[:, k, c], yl[:, kt + k, :], False, False)
                        m = mm(dst, w_lo[:, k, c], yh[:, kt + k, :], False, end and k == 1)
                    if end and g < KT - 1:
                        m.then_inc(S["acc"], 1)
                m.then_inc(S["used"], 1)

            def column_sums(stat_col, tile, g, first, last):
                for tt in range(TT):
                    m = mm(PS[2][:, stat_col + tt:stat_col + tt + 1], tile[:, tt * P:(tt + 1) * P], ones[:, :],
                           first and tt == 0, last)
                return m

            def spread(dst, col):
                return mm(dst, col.broadcast_to([P, P]), ident[:, :], True, True)

            def prenorm(n):
                for j, b in enumerate(x_pairs(n)):
                    eng.wait_ge(S["xsq"], 4 * n + j + 1)
                    for g in (2 * b, 2 * b + 1):
                        m = column_sums(0, work[:, g, :], g, j == 0 and g == 2 * b, j == 3 and g == 2 * b + 1)
                m.then_inc(S["xstat"], 1)
                eng.wait_ge(S["xrs"], n + 1)
                spread(PS[3][:, 0:P], rs[:, 0:1])
                spread(PS[3][:, P:2 * P], rs[:, 1:2]).then_inc(S["xbc"], 1)

            def postnorm(n):
                for b in range(4):
                    eng.wait_ge(S["ysq"], 4 * n + b + 1)
                    for g in (2 * b, 2 * b + 1):
                        m = column_sums(4, work[:, g, :], g, g == 0, g == KT - 1)
                m.then_inc(S["ystat"], 1)
                eng.wait_ge(S["yrs"], n + 1)
                spread(PS[3][:, 2 * P:3 * P], rs[:, 2:3])
                spread(PS[3][:, 3 * P:4 * P], rs[:, 3:4]).then_inc(S["ybc"], 1)

            eng.wait_ge(S["d_small"], 16 * 5)
            eng.transpose(PS[2][:, 0:ROWS1], rows1[0:ROWS1, :], ident[0:ROWS1, 0:ROWS1])
            eng.transpose(PS[2][:, P:P + ROWS2], rows2[0:ROWS2, :], ident[0:ROWS2, 0:ROWS2])
            mm(PS[3][0:ATT_HEADS, 0:SEQ], rel_in, onehot, True, True).then_inc(S["colsT"], 1)
            eng.wait_ge(S["d_x"], 16)
            for g in range(KT):
                for tt in range(TT):
                    m = eng.transpose(PS[4 + g // 2][:, (g % 2) * SEQ + tt * P:(g % 2) * SEQ + (tt + 1) * P],
                                      x_in[:, tt, g * P:(g + 1) * P], ident[:, :])
                if g % 2 == 1:
                    m.then_inc(S["xin"], 1)
            eng.wait_ge(S["const"], 2)
            eng.wait_ge(S["cols"], 2)
            eng.wait_ge(S["u"], 1)
            prenorm(0)

            def level_scores(i):
                half, lv = items[i]
                dst = PS[2 + i % 2]
                if i >= 2:
                    eng.wait_ge(S["pred"], i - 1)
                if lv != 7:
                    eng.wait_ge(S["q"], decays_to(i))
                    eng.wait_ge(S["k"], decays_to(i))
                for h in range(2):
                    for tt in range(TT):
                        if lv == 7:
                            qq, kk = g_qk[:, 2 * half + h, 0, :], g_qk[:, 2 * half + h, 1, :]
                        else:
                            qq = scr1[:, 2 + i % 2, h * SEQ:(h + 1) * SEQ]
                            kk = scr2[:, i % 2, h * SEQ:(h + 1) * SEQ]
                        if lv == 8:
                            if tt == 0:
                                m = mm(dst[:, h * P:(h + 1) * P], kk[:, 0:P], qq[:, P:2 * P], True, True)
                        else:
                            c = slice(tt * P, (tt + 1) * P)
                            m = mm(dst[:, (2 * h + tt) * P:(2 * h + tt + 1) * P], kk[:, c], qq[:, c], True, True)
                m.then_inc(S["smm"], 1)

            def gated_out():
                eng.wait_ge(S["pred"], len(items))
                for h in range(HEADS):
                    dst = PS[2 + h // 2][:, (h % 2) * SEQ:(h % 2 + 1) * SEQ]
                    v0, v1 = g_v[:, 0, h * DK:(h + 1) * DK], g_v[:, 1, h * DK:(h + 1) * DK]
                    mm(dst[:, 0:P], v0, wf[:, (2 * h) * P:(2 * h + 1) * P], True, True)
                    mm(dst[:, P:2 * P], v0, wf[:, 1024 + h * P:1024 + (h + 1) * P], True, False)
                    m = mm(dst[:, P:2 * P], v1, wf[:, (2 * h + 1) * P:(2 * h + 2) * P], False, True)
                m.then_inc(S["hout"], 1)

            def ret_scores():
                eng.wait_ge(S["rope"], 4)
                for h in range(HEADS):
                    rq, rk = r_qk[:, h, 0, :], r_qk[:, h, 1, :]
                    mm(PS[4 + h][:, 0:SEQ], rk[:, 0:P], rq, True, True)
                    m = mm(PS[4 + h][:, SEQ:SEQ + P], rk[:, P:2 * P], rq[:, P:2 * P], True, True)
                m.then_inc(S["rmm"], 1)

            def values_out(dst, v, c0, probs, last_sem):
                for g in range(2):
                    o = dst[:, g * SEQ:(g + 1) * SEQ]
                    mm(o, v[:, 0, c0 + g * P:c0 + (g + 1) * P], probs[:, 0:SEQ], True, False)
                    m = mm(o[:, P:2 * P], v[:, 1, c0 + g * P:c0 + (g + 1) * P], probs[:, SEQ:SEQ + P], False, True)
                m.then_inc(last_sem, 1)

            def head_sums(dst, sq_of, groups):
                for h in range(HEADS):
                    for tt in range(TT):
                        for g in range(groups):
                            m = mm(dst[:, 2 * h + tt:2 * h + tt + 1], sq_of(h, g)[:, tt * P:(tt + 1) * P], ones[:, :],
                                   g == 0, g == groups - 1)
                return m

            def head_spread(dst_of, cols):
                for h in range(HEADS):
                    for tt in range(TT):
                        m = spread(dst_of(h)[:, tt * P:(tt + 1) * P], cols[:, 2 * h + tt:2 * h + tt + 1])
                return m

            def gate_products():
                eng.wait_ge(S["d_wg"], 32)
                for tt in range(TT):
                    for k in range(KT):
                        m = mm(PS[4][:, 8 * tt:8 * tt + 8], work[:, k, tt * P:(tt + 1) * P], wg[:, k, :],
                               k == 0, k == KT - 1)
                m.then_inc(S["gmm"], 1)

            def gate_cumsum():
                eng.wait_ge(S["gsp"], 1)
                eng.wait_ge(S["d_causal"], 16)
                o = PS[4]
                mm(o[:, 32:36], upper, glf[:, 0, :], True, True)
                mm(o[:, 36:40], ones[:, 0:1].broadcast_to([P, P]), glf[:, 0, :], True, False)
                mm(o[:, 36:40], upper, glf[:, 1, :], False, True).then_inc(S["gbm"], 1)

            def gate_rows():
                eng.wait_ge(S["g"], 1)
                for tt in range(TT):
                    m = eng.transpose(PS[7][0:HEADS, tt * P:(tt + 1) * P], gg[:, tt, :], ident[:, :])
                m.then_inc(S["gT"], 1)

            def gate_max():
                eng.wait_ge(S["M"], 1)
                for h in range(HEADS):
                    m = mm(PS[5 + h // 2][:, (h % 2) * SEQ:(h % 2 + 1) * SEQ],
                           ident[0:HEADS, h:h + 1].broadcast_to([HEADS, P]), MT, True, True)
                for tt in range(TT):
                    m = eng.transpose(PS[7][:, 256 + 4 * tt:260 + 4 * tt], MT[:, tt * P:(tt + 1) * P],
                                      ident[0:HEADS, 0:HEADS])
                m.then_inc(S["Mb"], 1)

            def ml_scores(h):
                eng.wait_ge(S["qk"], 4)
                if h >= 2:
                    eng.wait_ge(S["ms"], h - 1)
                q, k, o = m_qk[:, h, :], m_qk[:, HEADS + h, :], PS[2 + h % 2]
                mm(o[:, 0:SEQ], k[:, 0:P], q, True, True)
                mm(o[:, SEQ:SEQ + P], k[:, P:2 * P], q[:, P:2 * P], True, True).then_inc(S["msc"], 1)

            def ml_out(h):
                eng.wait_ge(S["ms"], h + 1)
                wait_evac(eng, last_of("mv"))
                if h == 0:
                    eng.wait_ge(S["warg"], HEADS)
                if h >= 2:
                    eng.wait_ge(S["mev"], 2 * (h - 1))
                s = m_s[:, h, :]
                mm(PS[4][:, 64 + h:65 + h], s[:, 0:P], ones[:, :], True, True)
                mm(PS[4][:, 68 + h:69 + h], s[:, P:2 * P], ones[:, :], True, False)
                mm(PS[4][:, 68 + h:69 + h], s[:, SEQ:SEQ + P], ones[:, :], False, True)
                values_out(PS[5 + h % 2], m_v, h * RET_DV, s, S["mout"])

            def ml_spread():
                eng.wait_ge(S["mc"], 1)
                head_spread(lambda h: PS[2 + h // 2][:, (h % 2) * SEQ:(h % 2 + 1) * SEQ],
                            gc[:, :]).then_inc(S["mbc"], 1)

            def hg_spread():
                eng.wait_ge(S["hrs"], 1)
                head_spread(lambda h: PS[2 + h // 2][:, (h % 2) * SEQ:(h % 2 + 1) * SEQ], rs).then_inc(S["hbc"], 1)

            def att_scores(h):
                if h == 0:
                    wait_evac(eng, last_of("ak"))
                if h >= 2:
                    eng.wait_ge(S["lg"], h - 1)
                q, k, o = a_q[:, h, :], a_k[:, h, :], PS[2 + h % 2]
                mm(o[:, 0:P], q[:, 0:P], k[:, 0:P], True, True)
                mm(o[:, P:P + SEQ], q[:, P:2 * P], k, True, True).then_inc(S["asc"], 1)

            def att_turn(h):
                eng.wait_ge(S["p"], h + 1)
                if h >= 2:
                    eng.wait_ge(S["pt"], h - 1)
                pr = wf[:, 384 * (h % 2):384 * (h % 2 + 1)]
                for j in range(3):
                    m = eng.transpose(PS[4 + h % 2][:, j * P:(j + 1) * P], pr[:, j * P:(j + 1) * P], ident[:, :])
                m.then_inc(S["tr"], 1)

            def att_out(h):
                eng.wait_ge(S["pt"], h + 1)
                if h >= 2:
                    eng.wait_ge(S["aout_v"], h - 1)
                pt, o = wf[:, 768 + 384 * (h % 2):768 + 384 * (h % 2 + 1)], PS[6 + h % 2]
                mm(o[:, 0:SEQ], a_v[:, 0, h * P:(h + 1) * P], pt[:, 0:SEQ], True, False)
                mm(o[:, P:2 * P], a_v[:, 1, h * P:(h + 1) * P], pt[:, SEQ:SEQ + P], False, True).then_inc(S["aout"], 1)

            for u in range(NU):
                kind, _, _, role, i = UNITS[u]
                if role in ("up0", "mqk", "up1", "aq") and i == 0:
                    n = ("up0", "mqk", "up1", "aq").index(role)
                    postnorm(n)
                    prenorm(n + 1)
                if kind != "C":
                    eng.wait_ge(S["hi"], SPLIT_OF[u] + 1)
                wait_low(eng, u)
                if kind == "A":
                    if A_OF[u] >= 2:
                        wait_evac(eng, A_UNITS[A_OF[u] - 2])
                    if u in PRENORM:
                        a_first(u, PRENORM[u])
                    else:
                        a_forward(u, {at("mog", 3): ml_spread, at("hgate", 1): hg_spread}.get(u))
                elif kind == "C":
                    mod_sums(u)
                else:
                    p = PHASE[role]
                    if p in (1, 3):
                        eng.wait_ge(S["yl_dve"], (p // 2) * 16 + i + 1)
                    else:
                        eng.wait_ge(S["yl_pool"], y_pairs_before(p, False) + i + 1)
                    if i == 0 and p == 4:
                        eng.wait_ge(S["aout_v"], ATT_HEADS)
                    if i == 0 and p == 5:
                        eng.wait_ge(S["acc_free4"], 4)
                    if i == 0 and p == 6:
                        eng.wait_ge(S["acc_free5"], 4)
                    b_forward(u)

                for j in items_of(u):
                    level_scores(j)
                if u == at("rv"):
                    ret_scores()
                if u == at("rgate"):
                    wait_evac(eng, last_of("rv"))
                    for h in range(HEADS):
                        eng.wait_ge(S["rdec"], h + 1)
                        values_out(PS[4 + h], r_v, h * RET_DV, r_p[:, h, :], S["rout"])
                if u == at("rgate", 2):
                    eng.wait_ge(S["rev"], 8)
                    head_sums(PS[4], lambda h, g: r_qk[:, h, g, :], 2).then_inc(S["rst"], 1)
                if u == at("rgate", 3):
                    gated_out()
                    eng.wait_ge(S["rrs"], 1)
                    head_spread(lambda h: PS[5 + h // 2][:, (h % 2) * SEQ:(h % 2 + 1) * SEQ], rs[:, 8:16]).then_inc(S["rbc"], 1)
                if u == at("hgate"):
                    eng.wait_ge(S["hsq"], 1)
                    head_sums(PS[4], lambda h, g: g_sq[:, h * SEQ:(h + 1) * SEQ], 1).then_inc(S["hst"], 1)

                if u == at("mqk"):
                    gate_products()
                if u == at("mqk", 1):
                    gate_cumsum()
                if u == at("mqk", 2):
                    gate_rows()
                if u == at("mqk", 3):
                    gate_max()
                for h in range(HEADS):
                    if u == at("mv", h):
                        ml_scores(h)
                    if u == at("mog", h // 2):
                        ml_out(h)
                if u == at("mog", 2):
                    eng.wait_ge(S["mev"], 8)
                    eng.wait_ge(S["fls"], 1)
                    head_sums(PS[7], lambda h, g: m_sq[:, h, g * SEQ:(g + 1) * SEQ], 2).then_inc(S["mst"], 1)

                for h in range(ATT_HEADS):
                    if u == a_unit(h):
                        att_scores(h)
                    if u == a_unit(h) + 3:
                        att_turn(h)
                    if u == a_unit(h) + 4:
                        att_out(h)

            prenorm(5)
            for g in range(KT):
                eng.wait_ge(S["h"], 5 * KT + g + 1)
                for tt in range(TT):
                    m = eng.transpose(PS[4 + 2 * tt + g // 4][:, (g % 4) * P:(g % 4 + 1) * P],
                                      work[:, g, tt * P:(tt + 1) * P], ident[:, :])
                if g % 4 == 3:
                    m.then_inc(S["fin_mm"], 1)

        @block.vector
        def _(eng):
            steps = [0]

            def link(ins):
                steps[0] += 1
                ins.then_inc(S["step_dve"], 1)
                eng.wait_ge(S["step_dve"], steps[0])

            def tt(o, x, y, op):
                return eng.tensor_tensor(o, x, y, op)

            def ts(o, x, c1, c2, op0, op1=ALU.bypass):
                return eng.tensor_scalar(o, x, c1, c2, op0, op1)

            def stt(o, x, c, y, op0, op1):
                return eng.scalar_tensor_tensor(out=o, in0=x, scalar=c, in1=y, op0=op0, op1=op1)

            def split(u):
                eng.wait_ge(raw_sem[u % RING], 16 * (u // RING + 1))
                eng.wait_ge(S["hi"], SPLIT_OF[u] + 1)
                if u >= RING:
                    wait_used(eng, u - RING)
                tt(wl[:, u % RING, :], raw[:, u % RING, :], wh[:, u % RING, :].bitcast(F32),
                   ALU.subtract).then_inc(S["lo_dve"], 1)

            def mod_rows(u):
                eng.wait_ge(raw_sem[u % RING], 16 * (u // RING + 1))
                wait_used(eng, u - RING)
                eng.wait_ge(S["c_act"], 1)
                w, o = slot(raw, u, "C"), mod_part(UNITS[u][4])
                link(ts(o, w[:, 0, :], cf[:, 0:1], None, ALU.mult))
                for k in range(1, KT - 1):
                    link(stt(o, w[:, k, :], cf[:, k:k + 1], o, ALU.mult, ALU.add))
                stt(o, w[:, KT - 1, :], cf[:, KT - 1:KT], o, ALU.mult, ALU.add).then_inc(S["lo_ada"], 1)

            def gain(n, g):
                if n < 4:
                    c = R_NORM + 32 * (n // 2) + 16 * (n % 2) + g
                    return col1[:, c:c + 1]
                return gs[:, g:g + 1] if n == 4 else col2[:, R2_FINAL + g:R2_FINAL + g + 1]

            def prenorm(n):
                eng.wait_ge(S["xsd"], n + 1)
                eng.reciprocal(rs[:, 0:2], sd[:, 0:2]).then_inc(S["xrs"], 1)
                eng.wait_ge(S["xbc"], n + 1)
                for g in range(KT):
                    m = stt(work[:, g, :], xT[:, g, :], gain(n, g), PS[3][:, 0:SEQ], ALU.mult, ALU.mult)
                    if n != 4:
                        m.then_inc(S["h"], 1)
                        continue
                    m.then_inc(S["h_part"], 1)
                    if g >= 1:
                        shift(g - 1)
                if n == 4:
                    shift(KT - 1)

            def shift(g):
                eng.wait_ge(S["h_part"], g + 1)
                ts(work[:, g, :], work[:, g, :], mod[:, g:g + 1], None, ALU.add).then_inc(S["h"], 1)

            def pair_of(t, b):
                return t[:, 2 * b:2 * b + 2, :].rearrange("p k t -> p (k t)")

            def scale_y(n, j):
                b = X_ORDER[j]
                eng.wait_ge(S["yg"], 4 * n + j + 1)
                tt(yg[:, 2 * b:2 * b + 2, :], yg[:, 2 * b:2 * b + 2, :],
                   PS[3][:, SEQ:2 * SEQ].unsqueeze(1).broadcast_to([P, 2, SEQ]), ALU.mult).then_inc(S["t"], 1)

            def postnorm(n):
                eng.wait_ge(S["ysd"], n + 1)
                eng.reciprocal(rs[:, 2:4], sd[:, 2:4]).then_inc(S["yrs"], 1)
                eng.wait_ge(S["ybc"], n + 1)
                scale_y(n, 0)
                scale_y(n, 1)
                scale_y(n, 2)
                for j in (1, 3):
                    if j == 3:
                        scale_y(n, 3)
                    eng.wait_ge(S["t"], 4 * n + j + 1)
                    tt(pair_of(xT, X_ORDER[j]), pair_of(xT, X_ORDER[j]), pair_of(yg, X_ORDER[j]), ALU.add).then_inc(S["x_dve"], 1)

            eng.memset(ones[:, :], 1.0).then_inc(S["const"], 1)
            eng.memset(eps[:, :], EPS).then_inc(S["const"], 1)
            link(eng.memset(u_row, -MASKED))
            eng.wait_ge(S["colsT"], 1)
            tensor = eng.tensor_copy
            tensor(col1[:, :], PS[2][:, 0:ROWS1]).then_inc(S["cols"], 1)
            tensor(col2[:, :], PS[2][:, P:P + ROWS2]).then_inc(S["cols"], 1)
            tensor(u_row[:, P - 1:P - 1 + SEQ], PS[3][0:ATT_HEADS, 0:SEQ]).then_inc(S["u"], 1)
            eng.wait_ge(S["cols"], 2)
            low = [col1[:, R_LOWER + HEADS * r:R_LOWER + HEADS * (r + 1)] for r in range(3)]
            link(tt(lbs[:, 2, :], low[0], low[1], ALU.max))
            link(tt(lbs[:, 2, :], lbs[:, 2, :], low[2], ALU.max))
            for r in range(3):
                tt(lb[:, r, :], low[r], lbs[:, 2, :], ALU.subtract).then_inc(S["low"], 1)
            for b in range(4):
                eng.wait_ge(S["xin"], b + 1)
                tensor(xT[:, 2 * b:2 * b + 2, :], PS[4 + b][:, :].rearrange("p (k t) -> p k t", k=2)).then_inc(S["xcopy"], 1)
            prenorm(0)
            eng.wait_ge(S["d_masks"], 16)
            tensor(masks[:, :, :].rearrange("p l t -> p (l t)"), g_lf).then_inc(S["masks"], 1)

            def rope(u):
                i, which = UNITS[u][4], 0 if UNITS[u][3] == "rq" else 1
                dst = r_qk[:, 2 * i:2 * i + 2, which, :]
                tmp = scr2[:, 2 + i % 2, :].rearrange("p (h t) -> p h t", h=2)
                ps = bank(u)[:, :].rearrange("p (h t) -> p h t", h=2)
                half = P // 2

                def both(x):
                    return x.unsqueeze(1).broadcast_to([x.shape[0], 2, SEQ])

                if i == 0 and which == 0:
                    eng.wait_ge(S["d_tables"], 16)
                link(tt(dst, ps, both(cosT), ALU.mult))
                link(tt(tmp[0:half], ps[half:P], both(sinT[half:P]), ALU.mult))
                tt(tmp[half:P], ps[0:half], both(sinT[0:half]), ALU.mult).then_inc(S["evac_dve"], 1)
                eng.wait_ge(S["evac_dve"], evac_value(u))
                tt(dst, dst, tmp, ALU.add).then_inc(S["rope"], 1)

            def conv_taps(u):
                i = UNITS[u][4]
                ps = bank(u)[:, :].rearrange("p (h t) -> p h t", h=2)
                for j in range(4):
                    for g in range(2):
                        c = 2 * i + g
                        w = col1[:, R_CONVW + 8 * (3 - j) + c:R_CONVW + 8 * (3 - j) + c + 1]
                        y = m_qk[:, c, :]
                        if j == 0:
                            m = ts(y, ps[:, g, :], w, col1[:, R_CONVB + c:R_CONVB + c + 1], ALU.mult, ALU.add)
                        else:
                            m = stt(y[:, j:], ps[:, g, 0:SEQ - j], w, y[:, j:], ALU.mult, ALU.add)
                    if j < 3:
                        link(m)
                m.then_inc(S["evac_dve"], 1)

            def short_conv(u):
                i = UNITS[u][4]
                eng.wait_ge(S["evac_act"], evac_value(u - 1))
                tt(c_u, bank(u)[:, :], c_u, ALU.mult).then_inc(S["evac_dve"], 1)
                eng.wait_ge(S["evac_dve"], evac_value(u))
                for j in range(3):
                    for g in range(2):
                        kt = 2 * i + g
                        w = col2[:, R2_CONVW + 8 * (2 - j) + kt:R2_CONVW + 8 * (2 - j) + kt + 1]
                        x, y = c_u[:, g * SEQ:(g + 1) * SEQ], c_y[:, kt, :]
                        if j == 0:
                            m = ts(y, x, w, None, ALU.mult)
                        else:
                            m = stt(y[:, j:], x[:, 0:SEQ - j], w, y[:, j:], ALU.mult, ALU.add)
                    link(m)

            def level_decays(i):
                half, lv = items[i]
                if lv == 7:
                    return
                if i >= 2 and items[i - 2][1] != 7:
                    eng.wait_ge(S["q"], decays_to(i - 2))
                    eng.wait_ge(S["k"], decays_to(i - 2))
                m = LEVELS[lv] if lv < 7 else 128
                b = g_b[:, half * 512:(half + 1) * 512].rearrange("p (n w) -> p n w", w=2 * m)
                e = scr1[:, i % 2, :].rearrange("p (n w) -> p n w", w=2 * m)
                n = 256 // m

                def at_col(j, w):
                    return b[:, :, j:j + 1].broadcast_to([P, n, w])

                if m < 64:
                    tt(e[:, :, m:2 * m], b[:, :, m:2 * m], at_col(m - 1, m), ALU.subtract)
                    tt(e[:, :, 0:m], at_col(m - 1, m), b[:, :, 0:m], ALU.subtract).then_inc(S["diff"], 1)
                elif m == 64:
                    tensor(e[:, :, 64:128], b[:, :, 64:128])
                    tt(e[:, :, 0:64], at_col(63, 64), b[:, :, 0:64], ALU.subtract).then_inc(S["diff"], 1)
                else:
                    tensor(e[:, :, 128:192], b[:, :, 128:192])
                    tt(e[:, :, 192:256], b[:, :, 192:256], at_col(191, 64), ALU.add)
                    link(tt(e[:, :, 0:64], at_col(63, 64), b[:, :, 0:64], ALU.subtract))
                    tt(e[:, :, 0:64], e[:, :, 0:64], at_col(127, 64), ALU.add)
                    tt(e[:, :, 64:128], at_col(127, 64), b[:, :, 64:128], ALU.subtract).then_inc(S["diff"], 1)

            def level_queries(i):
                half, lv = items[i]
                if lv == 7:
                    return
                eng.wait_ge(S["e"], decays_to(i))
                if i >= 2:
                    eng.wait_ge(S["smm"], i - 1)
                tt(scr1[:, 2 + i % 2, :].rearrange("p (h t) -> p h t", h=2), g_qk[:, 2 * half:2 * half + 2, 0, :],
                   scr1[:, i % 2, :].rearrange("p (h t) -> p h t", h=2), ALU.mult).then_inc(S["q"], 1)

            def level_pick(i):
                half, lv = items[i]
                eng.wait_ge(S["smm"], i + 1)
                if i == 0:
                    eng.wait_ge(S["masks"], 1)
                if i >= 1:
                    eng.wait_ge(S["pred"], i)
                if lv == 8:
                    tensor(wf[:, 1024 + half * SEQ:1024 + (half + 1) * SEQ], PS[2 + i % 2][:, 0:SEQ]).then_inc(S["pred"], 1)
                else:
                    eng.copy_predicated(
                        wf[:, half * 512:(half + 1) * 512].rearrange("p (n t) -> p n t", n=4),
                        masks[:, lv, :].unsqueeze(1).broadcast_to([P, 4, P]),
                        PS[2 + i % 2][:, :].rearrange("p (n t) -> p n t", n=4)).then_inc(S["pred"], 1)

            def att_logits(h):
                eng.wait_ge(S["asc"], h + 1)
                if h == 0:
                    eng.wait_ge(S["d_bias"], 16)
                if h >= 2:
                    eng.wait_ge(S["tr"], h - 1)
                o, ps = wf[:, 384 * (h % 2):384 * (h % 2 + 1)], PS[2 + h % 2]
                stt(o[:, 0:P], ps[:, 0:P], QK_SCALE, bias[:, h, P - 1::-1], ALU.mult, ALU.add)
                stt(o[:, P:P + SEQ], ps[:, P:P + SEQ], QK_SCALE, bias[:, h, SEQ - 1::-1], ALU.mult,
                    ALU.add).then_inc(S["lg"], 1)
                eng.wait_ge(S["lg"], h + 1)
                if h >= 2:
                    eng.wait_ge(S["aexp"], h - 1)
                eng.tensor_reduce(mx[:, h % 2, 0:1], o[:, 0:P], AX_X, ALU.max)
                link(eng.tensor_reduce(mx[:, h % 2, 1:2], o[:, P:P + SEQ], AX_X, ALU.max))
                ts(mx[:, h % 2, :], mx[:, h % 2, :], -1.0, None, ALU.mult).then_inc(S["mxn"], 1)

            def att_norm(h):
                eng.wait_ge(S["aexp"], h + 1)
                o = wf[:, 384 * (h % 2):384 * (h % 2 + 1)]
                link(eng.reciprocal(sm[:, h % 2, :], sm[:, h % 2, :]))
                ts(o[:, 0:P], o[:, 0:P], sm[:, h % 2, 0:1], None, ALU.mult)
                ts(o[:, P:P + SEQ], o[:, P:P + SEQ], sm[:, h % 2, 1:2], None, ALU.mult).then_inc(S["p"], 1)

            def att_gate(h):
                eng.wait_ge(S["aout"], h + 1)
                if h == 0:
                    wait_evac(eng, last_of("ag"))
                tt(a_g[:, h, :], PS[6 + h % 2][:, 0:SEQ], a_g[:, h, :], ALU.mult).then_inc(S["aout_v"], 1)

            def hidden_low(layer, i):
                eng.wait_ge(S["yh"], y_pairs_before(2 * layer + 1, True) + i + 1)
                if i >= RING:
                    wait_used(eng, at(f"out{2 * layer + 1}", i - RING))
                tt(flat2(yl, i % RING), wf[:, 512 * (i % RING):512 * (i % RING + 1)], flat2(yh, i % RING).bitcast(F32),
                   ALU.subtract).then_inc(S["yl_dve"], 1)

            def gate_out(h):
                for g in range(2):
                    m = stt(m_og[:, 2 * h + g, :], m_og[:, 2 * h + g, :], col1[:, R_ML + g:R_ML + g + 1],
                            m_o[:, 2 * h + g, :], ALU.mult, ALU.mult)
                link(m)
                eng.wait_ge(S["mbc"], 1)
                b = PS[2 + h // 2][:, (h % 2) * SEQ:(h % 2 + 1) * SEQ].unsqueeze(1).broadcast_to([P, 2, SEQ])
                tt(m_og[:, 2 * h:2 * h + 2, :], m_og[:, 2 * h:2 * h + 2, :], b, ALU.mult).then_inc(S["y_src"], 1)

            def before(u):
                for j in items_of(u - 1):
                    level_pick(j)
                for j in items_of(u):
                    level_queries(j)
                if u == at("rgate"):
                    eng.wait_ge(S["rmm"], 1)
                    for h in range(HEADS):
                        o = r_p[:, h, :]
                        tt(o[:, 0:SEQ], PS[4 + h][:, 0:SEQ], ret_dec[:, h, :], ALU.mult)
                        tt(o[:, SEQ:SEQ + P], PS[4 + h][:, SEQ:SEQ + P], ret_dec[:, h, 0:P], ALU.mult).then_inc(S["rdec"], 1)
                if u == at("rgate", 3):
                    eng.wait_ge(S["rsd"], 1)
                    eng.reciprocal(rs[:, 8:16], sd[:, 8:16]).then_inc(S["rrs"], 1)
                if u == at("hgate", 1):
                    eng.wait_ge(S["hsd"], 1)
                    eng.reciprocal(rs[:, 0:8], sd[:, 0:8]).then_inc(S["hrs"], 1)

                if u == at("mqk", 1):
                    eng.wait_ge(S["gmm"], 1)
                    eng.wait_ge(S["d_wg"], 32)
                    tt(gz[:, :, :], PS[4][:, 0:16].rearrange("p (t j) -> p t j", t=2),
                       gzb[:, :].unsqueeze(1).broadcast_to([P, 2, 8]), ALU.add).then_inc(S["gz"], 1)
                    eng.wait_ge(S["gcap"], 1)
                    ts(gz[:, :, :], gcap[:, :, :], CAP, None, ALU.mult).then_inc(S["gz"], 1)
                if u == at("mqk", 2):
                    eng.wait_ge(S["gbm"], 1)
                    tt(gg[:, :, :], gz[:, :, 0:4], PS[4][:, 32:40].rearrange("p (t j) -> p t j", t=2), ALU.add)
                    tensor(gB[:, :, :], PS[4][:, 32:40].rearrange("p (t j) -> p t j", t=2)).then_inc(S["g"], 1)
                if u == at("mqk", 3):
                    eng.wait_ge(S["gT"], 1)
                    link(tensor(gT, PS[7][0:HEADS, 0:SEQ]))
                    eng.tensor_tensor_scan(MT, gT, gT, 0.0, ALU.max, ALU.max).then_inc(S["M"], 1)
                for h in range(HEADS):
                    if u == at("mv", h) + 1:
                        eng.wait_ge(S["msc"], h + 1)
                        eng.wait_ge(S["w"], h + 1)
                        stt(m_s[:, h, :], PS[2 + h % 2][:, 0:384], QK_SCALE, m_w[:, h, :], ALU.mult,
                            ALU.mult).then_inc(S["ms"], 1)
                    if u == at("mv", h):
                        if h == 0:
                            eng.wait_ge(S["Mb"], 1)
                            tt(gm[:, :, :], gB[:, :, :], PS[7][:, 256:264].rearrange("p (t j) -> p t j", t=2),
                               ALU.subtract).then_inc(S["fls"], 1)
                        mb = PS[5 + h // 2][:, (h % 2) * SEQ:(h % 2 + 1) * SEQ]
                        stt(m_w[:, h, 0:SEQ], mb, gg[:, 0, h:h + 1], causal, ALU.subtract, ALU.add)
                        stt(m_w[:, h, SEQ:384], mb[:, P:SEQ], gg[:, 1, h:h + 1], causal[:, 0:P], ALU.subtract,
                            ALU.add).then_inc(S["warg"], 1)
                if u == at("mog", 2):
                    eng.wait_ge(S["mout"], 4)
                    link(tensor(gden[:, :, :], PS[4][:, 64:72].rearrange("p (t h) -> p t h", t=2)))
                    link(stt(gdi[:, :, :], gden[:, :, :], -1.0, gden[:, :, :], ALU.mult, ALU.max))
                    eng.wait_ge(S["fl"], 1)
                    link(tt(gdi[:, :, :], gdi[:, :, :], gm[:, :, :], ALU.max))
                    link(eng.reciprocal(gden[:, :, :], gdi[:, :, :]))
                if u == at("mog", 3):
                    eng.wait_ge(S["mst"], 1)
                    by_t = gc[:, :].rearrange("p (h t) -> p t h", t=2)
                    link(tt(by_t, PS[7][:, 0:8].rearrange("p (h t) -> p t h", t=2), gden[:, :, :], ALU.mult))
                    tt(by_t, by_t, gden[:, :, :], ALU.mult).then_inc(S["mvar"], 1)
                    eng.wait_ge(S["msd"], 1)
                    link(eng.reciprocal(rs[:, 0:8], sd[:, 0:8]))
                    tt(by_t, rs[:, 0:8].rearrange("p (h t) -> p t h", t=2), gden[:, :, :], ALU.mult).then_inc(S["mc"], 1)
                    wait_evac(eng, u - 1)
                    eng.wait_ge(S["mev"], 8)
                    for h in range(HEADS - 1):
                        gate_out(h)

                for h in range(ATT_HEADS):
                    if u == a_unit(h) + 5:
                        att_gate(h)
                for h in range(ATT_HEADS):
                    if u == a_unit(h) + 3:
                        att_norm(h)
                for h in range(ATT_HEADS):
                    if u == a_unit(h) + 1:
                        att_logits(h)

            for u in range(-AHEAD, NU):
                role, i = UNITS[u][3:] if u >= 0 else ("", 0)
                if role in ("up0", "mqk", "up1", "aq") and i == 0:
                    n = ("up0", "mqk", "up1", "aq").index(role)
                    postnorm(n)
                    prenorm(n + 1)
                before(u)
                s = u + AHEAD
                if s < NU and split_by(s) == "dve":
                    split(s)
                if s < NU and split_by(s) == "ada":
                    mod_rows(s)
                if u == -1:
                    eng.wait_ge(S["lowe"], 1)
                    link(tt(lbs[:, 2, :], lb[:, 0, :], lb[:, 1, :], ALU.add))
                    link(tt(lbs[:, 2, :], lbs[:, 2, :], lb[:, 2, :], ALU.add))
                    link(eng.reciprocal(lbs[:, 3, :], lbs[:, 2, :]))
                    link(tt(lbs[:, 0, :], lb[:, 0, :], lbs[:, 3, :], ALU.mult))
                    link(ts(lbs[:, 1, :], lbs[:, 0, :], -1.0, 1.0, ALU.mult, ALU.add))
                if u < 0:
                    continue
                if EVAC.get(role) == "dve":
                    wait_used(eng, u)
                if role in ("rq", "rk"):
                    rope(u)
                elif role == "ada":
                    wait_used(eng, u)
                    c = slice(2 * i, 2 * i + 2)
                    tt(mod[:, c], PS[2][:, 8 + 2 * i:10 + 2 * i], col2[:, R2_BADA + 2 * i:R2_BADA + 2 * i + 2],
                       ALU.add).then_inc(S["mod"], 1)
                    if i == 7:
                        eng.wait_ge(S["mod"], 8)
                        link(stt(gs[:, :], mod[:, KT:2 * KT], 1.0, col2[:, R2_NORM:R2_NORM + KT], ALU.add, ALU.mult))
                elif role in ("up0", "up1"):
                    ts(wf[:, 512 * (i % RING):512 * (i % RING + 1)], bank(u)[:, :], 0.0, None, ALU.max).then_inc(S["evac_dve"], 1)
                elif role == "mqk":
                    conv_taps(u)
                elif role == "cx":
                    short_conv(u)
                elif role == "cb":
                    tt(c_y[:, 2 * i:2 * i + 2, :].rearrange("p k t -> p (k t)"), bank(u)[:, :],
                       c_y[:, 2 * i:2 * i + 2, :].rearrange("p k t -> p (k t)"), ALU.mult).then_inc(S["evac_dve"], 1)
                elif role == "cg":
                    wait_evac(eng, u)
                    eng.wait_ge(S["evac_dve"], evac_value(u - 1))
                    pair = c_y[:, 2 * i:2 * i + 2, :].rearrange("p k t -> p (k t)")
                    tt(pair, pair, c_t, ALU.mult).then_inc(S["y_src"], 1)
                v = next((w for w in range(u - 1, -1, -1) if UNITS[w][0] != "C"), None)
                if role != "ada" and v is not None and UNITS[v][3] in ("up0", "up1"):
                    hidden_low(0 if UNITS[v][3] == "up0" else 1, UNITS[v][4])

                if u == at("hf", 1):
                    wait_evac(eng, u)
                    for h in range(HEADS):
                        m = ts(g_b[:, h * SEQ:(h + 1) * SEQ], g_qk[:, h, 1, :], lbs[:, 1, h:h + 1], lbs[:, 0, h:h + 1],
                               ALU.mult, ALU.add)
                    m.then_inc(S["f"], 1)
                    eng.wait_ge(S["f"], 1)
                    ts(g_qk[:, :, 1, :], g_b.rearrange("p (h t) -> p h t", h=HEADS), -1.0, 1.0, ALU.mult,
                       ALU.add).then_inc(S["k_hg"], 1)
                    eng.wait_ge(S["hl"], KT)
                    link(eng.memset(wf[:, 0:1024], 0.0))
                if u == at("hq"):
                    eng.wait_ge(S["lf"], 1)
                    eng.wait_ge(S["k_hg"], 1)
                    eng.wait_ge(S["d_tables"], 16)
                    for h in range(HEADS):
                        c = slice(h * SEQ, (h + 1) * SEQ)
                        m = eng.tensor_tensor_scan(g_b[:, c], reset, g_lf[:, c], 0.0, ALU.mult, ALU.add)
                    m.then_inc(S["b"], 1)
                    eng.wait_ge(S["b"], 1)
                if u == at("hq", 1):
                    wait_evac(eng, u)
                for j in items_of(u + 1):
                    level_decays(j)
                if u == at("hgate"):
                    wait_evac(eng, u - 1)
                    eng.wait_ge(S["rbc"], 1)
                    for h in range(HEADS):
                        b = PS[5 + h // 2][:, (h % 2) * SEQ:(h % 2 + 1) * SEQ].unsqueeze(1).broadcast_to([P, 2, SEQ])
                        for g in range(2):
                            m = stt(r_gate[:, 2 * h + g, :], r_gate[:, 2 * h + g, :], col1[:, R_RET + g:R_RET + g + 1],
                                    r_o[:, h, g, :], ALU.mult, ALU.mult)
                        link(m)
                        tt(r_gate[:, 2 * h:2 * h + 2, :], r_gate[:, 2 * h:2 * h + 2, :], b, ALU.mult).then_inc(S["y_src"], 1)
                if u == at("hgate", 1):
                    wait_evac(eng, u)
                    for b in range(2):
                        c = slice(512 * b, 512 * (b + 1))
                        link(stt(g_gate[:, c], g_gate[:, c], col1[:, R_HG:R_HG + 1], g_o[:, c], ALU.mult, ALU.mult))
                        if b == 0:
                            eng.wait_ge(S["hbc"], 1)
                        tt(g_o[:, c], g_gate[:, c], PS[2 + b][:, :], ALU.mult).then_inc(S["y_src"], 1)

                if u == last_of("mog"):
                    wait_evac(eng, u)
                    gate_out(HEADS - 1)
                if u == last_of("out4"):
                    eng.wait_ge(S["yl_pool"], y_pairs_before(5, False))
                    for b in range(4):
                        wait_acc(eng, 4, b)
                        tensor(y_conv[:, 2 * b:2 * b + 2, :].rearrange("p k t -> p (k t)"), PS[4 + b][:, :]).then_inc(S["acc_free4"], 1)
                if role == "mc":
                    wait_evac(eng, u)
                    eng.wait_ge(S["acc_free4"], i + 1)
                    tt(o_mc[:, 2 * i:2 * i + 2, :], o_mc[:, 2 * i:2 * i + 2, :], y_conv[:, 2 * i:2 * i + 2, :],
                       ALU.mult).then_inc(S["mcm"], 1)
                if u == last_of("out5"):
                    for b in range(4):
                        wait_acc(eng, 5, b)
                        wait_evac(eng, at("ma", b))
                        pair = o_ma[:, 2 * b:2 * b + 2, :].rearrange("p k t -> p (k t)")
                        tt(pair, PS[4 + b][:, :], pair, ALU.mult).then_inc(S["acc_free5"], 1)
                        eng.wait_ge(S["acc_free5"], b + 1)
                        eng.wait_ge(S["mcm"], b + 1)
                        tt(pair, pair, o_mc[:, 2 * b:2 * b + 2, :].rearrange("p k t -> p (k t)"), ALU.add).then_inc(S["merged"], 1)

            for g in range(KT):
                if g % 2 == 0:
                    wait_acc(eng, 6, g // 2)
                stt(xT[:, g, :], acc_group(g), mod[:, 2 * KT + g:2 * KT + g + 1], xT[:, g, :], ALU.mult,
                    ALU.add).then_inc(S["x_last"], 1)
            prenorm(5)

        @block.scalar
        def _(eng):
            def act(o, x, f, **more):
                return eng.activation(o, x, f, **more)

            def high(u):
                eng.wait_ge(raw_sem[u % RING], 16 * (u // RING + 1))
                if u >= RING:
                    wait_used(eng, u - RING)
                eng.copy(wh[:, u % RING, :], raw[:, u % RING, :]).then_inc(S["hi"], 1)

            def root(o, stat, n):
                return act(o, stat, ACT.Sqrt, scale=1.0 / n, bias=eps[:, 0:1])

            def prenorm(n):
                for j, b in enumerate(x_pairs(n)):
                    if n == 0:
                        eng.wait_ge(S["xcopy"], j + 1)
                    elif n == 5:
                        eng.wait_ge(S["x_last"], 2 * j + 2)
                    elif j % 2 == 0:
                        eng.wait_ge(S["x_pool"], 2 * (n - 1) + j // 2 + 1)
                    else:
                        eng.wait_ge(S["x_dve"], 2 * (n - 1) + j // 2 + 1)
                    act(flat2(work, b), flat2(xT, b), ACT.Square).then_inc(S["xsq"], 1)
                eng.wait_ge(S["xstat"], n + 1)
                if n == 0:
                    eng.wait_ge(S["const"], 2)
                root(sd[:, 0:2], PS[2][:, 0:2], D).then_inc(S["xsd"], 1)
                if n < 5:
                    for g in range(KT):
                        eng.wait_ge(S["h"], KT * n + g + 1)
                        eng.copy(hh[:, g, :], work[:, g, :]).then_inc(S["hh"], 1)

            def postnorm(n):
                for b in range(4):
                    wait_acc(eng, n, b)
                    act(work[:, 2 * b:2 * b + 2, :].rearrange("p k t -> p (k t)"), PS[4 + b][:, :],
                        ACT.Square).then_inc(S["ysq"], 1)
                eng.wait_ge(S["ystat"], n + 1)
                root(sd[:, 2:4], PS[2][:, 4:6], D).then_inc(S["ysd"], 1)
                for j, b in enumerate(X_ORDER):
                    for g in (2 * b, 2 * b + 1):
                        c = R_NORM + 32 * (n // 2) + 16 * (n % 2) + 8 + g
                        m = act(yg[:, g, :], acc_group(g), ACT.Copy, scale=col1[:, c:c + 1])
                    m.then_inc(S["yg"], 1)

            def y_high(p, i):
                if p in (0, 2, 4):
                    eng.wait_ge(S["y_src"], {0: 0, 2: 6, 4: 10}[p] + i + 1)
                elif p == 5:
                    eng.wait_ge(S["aout_v"], 2 * i + 2)
                    wait_used(eng, at("out4", i))
                else:
                    eng.wait_ge(S["merged"], i + 1)
                eng.copy(flat2(yh, i), y_source(p, i)).then_inc(S["yh"], 1)

            eng.wait_ge(S["const"], 2)
            act(sd[:, 0:1], eps[:, :], ACT.Sqrt).then_inc(S["step_act"], 1)
            eng.wait_ge(S["step_act"], 1)
            prenorm(0)
            eng.wait_ge(S["u"], 1)
            eng.dma_start(scratch_dram, u_row).then_inc(S["d_u"], 16)

            def before(u):
                if u == at("rgate", 1):
                    eng.wait_ge(S["rout"], 4)
                    for h in range(HEADS):
                        eng.copy(r_o[:, h, :, :].rearrange("p a b -> p (a b)"), PS[4 + h][:, :]).then_inc(S["rev"], 1)
                        act(r_qk[:, h, :, :].rearrange("p a b -> p (a b)"), PS[4 + h][:, :], ACT.Square).then_inc(S["rev"], 1)
                if u == at("rgate", 3):
                    eng.wait_ge(S["rst"], 1)
                    root(sd[:, 8:16], PS[4][:, 0:8], RET_DV).then_inc(S["rsd"], 1)

                if u == at("mqk", 1):
                    eng.wait_ge(S["gz"], 1)
                    act(gcap[:, :, :], gz[:, :, :], ACT.Tanh, scale=1.0 / CAP).then_inc(S["gcap"], 1)
                    eng.wait_ge(S["gz"], 2)
                    act(glf[:, :, :], gz[:, :, 4:8], ACT.Exp, scale=-1.0).then_inc(S["gle"], 1)
                    eng.wait_ge(S["gle"], 1)
                    act(glf[:, :, :], glf[:, :, :], ACT.Ln, bias=ones[:, 0:1]).then_inc(S["gsp"], 1)
                for h in range(HEADS):
                    if u == at("mv", h):
                        if h == 0:
                            eng.wait_ge(S["fls"], 1)
                            act(gm[:, :, :], gm[:, :, :], ACT.Exp).then_inc(S["fl"], 1)
                        eng.wait_ge(S["warg"], h + 1)
                        act(m_w[:, h, :], m_w[:, h, :], ACT.Exp, scale=-1.0).then_inc(S["w"], 1)
                    if u == at("mog", 1 + h // 2):
                        eng.wait_ge(S["mout"], h + 1)
                        eng.wait_ge(S["msc"], HEADS)
                        eng.copy(m_o[:, 2 * h:2 * h + 2, :].rearrange("p k t -> p (k t)"), PS[5 + h % 2][:, :]).then_inc(S["mev"], 1)
                        act(m_sq[:, h, :], PS[5 + h % 2][:, :], ACT.Square).then_inc(S["mev"], 1)
                if u == at("mog", 3):
                    eng.wait_ge(S["mvar"], 1)
                    root(sd[:, 0:8], gc[:, :], RET_DV).then_inc(S["msd"], 1)

                for h in range(ATT_HEADS):
                    if u == a_unit(h) + 4:
                        eng.wait_ge(S["tr"], h + 1)
                        if h >= 2:
                            eng.wait_ge(S["aout"], h - 1)
                        eng.copy(wf[:, 768 + 384 * (h % 2):768 + 384 * (h % 2 + 1)], PS[4 + h % 2][:, 0:384]).then_inc(S["pt"], 1)
                for h in range(ATT_HEADS):
                    if u == a_unit(h) + 2:
                        eng.wait_ge(S["mxn"], h + 1)
                        o = wf[:, 384 * (h % 2):384 * (h % 2 + 1)]
                        act(o[:, 0:P], o[:, 0:P], ACT.Exp, bias=mx[:, h % 2, 0:1], accum_out=sm[:, h % 2, 0:1])
                        act(o[:, P:384], o[:, P:384], ACT.Exp, bias=mx[:, h % 2, 1:2],
                            accum_out=sm[:, h % 2, 1:2]).then_inc(S["aexp"], 1)

            for u in range(-AHEAD, NU):
                role, i = UNITS[u][3:] if u >= 0 else ("", 0)
                if role in ("up0", "mqk", "up1", "aq") and i == 0:
                    n = ("up0", "mqk", "up1", "aq").index(role)
                    postnorm(n)
                    prenorm(n + 1)
                if u + AHEAD in SPLIT_OF:
                    high(u + AHEAD)
                if u == -1:
                    eng.wait_ge(S["low"], 3)
                    act(lb[:, :, :], lb[:, :, :], ACT.Exp).then_inc(S["lowe"], 1)
                before(u)
                if u < 0:
                    continue
                if EVAC.get(role) == "act":
                    wait_used(eng, u)
                ps = bank(u)[:, :] if u in A_OF else None
                pair = ps.rearrange("p (h t) -> p h t", h=2) if u in A_OF else None
                if role == "hf":
                    act(g_qk[:, 2 * i:2 * i + 2, 1, :], pair, ACT.Sigmoid).then_inc(S["evac_act"], 1)
                elif role == "hq":
                    act(g_qk[:, 2 * i:2 * i + 2, 0, :], pair, ACT.Silu).then_inc(S["evac_act"], 1)
                    if i == 1:
                        act(cf[:, :], col2[:, R2_C:R2_C + KT], ACT.Silu).then_inc(S["c_act"], 1)
                elif role == "hi":
                    eng.copy(g_v[:, :, i * UCOLS:(i + 1) * UCOLS], pair).then_inc(S["evac_act"], 1)
                elif role == "rv":
                    eng.copy(r_v[:, :, i * UCOLS:(i + 1) * UCOLS], pair).then_inc(S["evac_act"], 1)
                elif role == "hgate":
                    act(g_gate[:, 512 * i:512 * (i + 1)], ps, ACT.Silu).then_inc(S["evac_act"], 1)
                elif role == "rgate":
                    if i == 0:
                        eng.wait_ge(S["d_u"], 16)
                    act(r_gate[:, 2 * i:2 * i + 2, :], pair, ACT.Silu).then_inc(S["evac_act"], 1)
                elif role == "mv":
                    eng.copy(m_v[:, :, i * UCOLS:(i + 1) * UCOLS], pair).then_inc(S["evac_act"], 1)
                elif role == "mog":
                    act(m_og[:, 2 * i:2 * i + 2, :], pair, ACT.Sigmoid).then_inc(S["evac_act"], 1)
                elif role in ("aq", "ak"):
                    eng.copy((a_q if role == "aq" else a_k)[:, 2 * i:2 * i + 2, :], pair).then_inc(S["evac_act"], 1)
                elif role == "av":
                    eng.copy(a_v[:, :, i * UCOLS:(i + 1) * UCOLS], pair).then_inc(S["evac_act"], 1)
                elif role == "ag":
                    act(a_g[:, 2 * i:2 * i + 2, :], pair, ACT.Silu).then_inc(S["evac_act"], 1)
                elif role == "cc":
                    eng.wait_ge(S["y_src"], 10 + i)
                    eng.copy(c_u, ps).then_inc(S["evac_act"], 1)
                elif role == "cg":
                    if i >= 1:
                        eng.wait_ge(S["y_src"], 10 + i)
                    act(c_t, ps, ACT.Silu).then_inc(S["evac_act"], 1)
                elif role in ("mc", "ma"):
                    if i == 0:
                        eng.wait_ge(S["asc"], ATT_HEADS)
                    act((o_mc if role == "mc" else o_ma)[:, 2 * i:2 * i + 2, :], pair, ACT.Sigmoid).then_inc(S["evac_act"], 1)
                elif role in ("up0", "up1"):
                    layer = 0 if role == "up0" else 1
                    c = slice(512 * (i % RING), 512 * (i % RING + 1))
                    eng.wait_ge(S["evac_dve"], evac_value(u))
                    act(wf[:, c], wf[:, c], ACT.Square).then_inc(S["sq"], 1)
                    eng.wait_ge(S["sq"], 16 * layer + i + 1)
                    if i >= RING:
                        wait_used(eng, at(f"out{2 * layer + 1}", i - RING))
                    eng.copy(flat2(yh, i % RING), wf[:, c]).then_inc(S["yh"], 1)
                elif role == "mqk":
                    eng.wait_ge(S["evac_dve"], evac_value(u))
                    act(m_qk[:, 2 * i:2 * i + 2, :], m_qk[:, 2 * i:2 * i + 2, :], ACT.Silu).then_inc(S["qk"], 1)

                if u == at("hf", 1):
                    eng.wait_ge(S["f"], 1)
                    eng.wait_ge(S["masks"], 1)
                    act(g_lf, g_b, ACT.Ln).then_inc(S["lf"], 1)
                for j in items_of(u + 1):
                    if items[j][1] != 7:
                        eng.wait_ge(S["diff"], decays_to(j))
                        act(scr1[:, j % 2, :], scr1[:, j % 2, :], ACT.Exp).then_inc(S["e"], 1)
                if u == at("rgate", 3):
                    eng.wait_ge(S["hout"], 1)
                    for b in range(2):
                        eng.copy(g_o[:, 512 * b:512 * (b + 1)], PS[2 + b][:, :]).then_inc(S["hev"], 1)
                        m = act(g_sq[:, 512 * b:512 * (b + 1)], PS[2 + b][:, :], ACT.Square)
                    m.then_inc(S["hsq"], 1)
                if u == at("hgate"):
                    eng.wait_ge(S["hst"], 1)
                    root(sd[:, 0:8], PS[4][:, 0:8], DK).then_inc(S["hsd"], 1)
                    y_high(0, 0)
                    y_high(0, 1)
                if u == at("hgate", 1):
                    for j in range(2, 6):
                        y_high(0, j)

                if u == last_of("mog"):
                    for j in range(4):
                        y_high(2, j)
                if role == "cg":
                    y_high(4, i)
                if role == "mc":
                    y_high(5, i)
                if u == last_of("out5"):
                    for j in range(4):
                        y_high(6, j)

            prenorm(5)
            for b in range(4):
                tt_, k = b // 2, b % 2
                eng.wait_ge(S["fin_mm"], k + 1)
            for tt_ in range(TT):
                for k in range(2):
                    eng.copy(fin_t[:, tt_, 512 * k:512 * (k + 1)], PS[4 + 2 * tt_ + k][:, :]).then_inc(S["fin"], 1)

        @block.gpsimd
        def _(eng):
            def split(u):
                eng.wait_ge(raw_sem[u % RING], 16 * (u // RING + 1))
                eng.wait_ge(S["hi"], SPLIT_OF[u] + 1)
                if u >= RING:
                    wait_used(eng, u - RING)
                eng.tensor_tensor(wl[:, u % RING, :], raw[:, u % RING, :], wh[:, u % RING, :].bitcast(F32),
                                  ALU.subtract).then_inc(S["lo_pool"], 1)

            def prenorm(n):
                for g in range(KT):
                    eng.wait_ge(S["hh"], KT * n + g + 1)
                    eng.tensor_tensor(hl[:, g, :], work[:, g, :], hh[:, g, :].bitcast(F32), ALU.subtract).then_inc(S["hl"], 1)

            def postnorm(n):
                for j in (0, 2):
                    eng.wait_ge(S["t"], 4 * n + j + 1)
                    eng.tensor_tensor(flat2(xT, X_ORDER[j]), flat2(xT, X_ORDER[j]), flat2(yg, X_ORDER[j]),
                                      ALU.add).then_inc(S["x_pool"], 1)

            def y_low(p, i):
                eng.wait_ge(S["yh"], y_pairs_before(p, True) + i + 1)
                eng.tensor_tensor(flat2(yl, i), y_source(p, i), flat2(yh, i).bitcast(F32), ALU.subtract).then_inc(S["yl_pool"], 1)

            prenorm(0)
            for u in range(-AHEAD, NU):
                role, i = UNITS[u][3:] if u >= 0 else ("", 0)
                if role in ("up0", "mqk", "up1", "aq") and i == 0:
                    n = ("up0", "mqk", "up1", "aq").index(role)
                    postnorm(n)
                    prenorm(n + 1)
                for j in items_of(u):
                    if items[j][1] != 7:
                        half = items[j][0]
                        eng.wait_ge(S["e"], decays_to(j))
                        if j >= 2:
                            eng.wait_ge(S["smm"], j - 1)
                        eng.tensor_tensor(scr2[:, j % 2, :].rearrange("p (h t) -> p h t", h=2),
                                          g_qk[:, 2 * half:2 * half + 2, 1, :],
                                          scr1[:, j % 2, :].rearrange("p (h t) -> p h t", h=2), ALU.mult).then_inc(S["k"], 1)
                s = u + AHEAD
                if s < NU and split_by(s) == "pool":
                    split(s)
                if u < 0:
                    continue
                if u == at("hgate"):
                    y_low(0, 0)
                    y_low(0, 1)
                if u == at("hgate", 1):
                    for j in range(2, 6):
                        y_low(0, j)
                if u == last_of("mog"):
                    for j in range(4):
                        y_low(2, j)
                if role == "cg":
                    y_low(4, i)
                if role == "mc":
                    y_low(5, i)
                if u == last_of("out5"):
                    for j in range(4):
                        y_low(6, j)


def kernel(**inputs):
    from concourse import bacc
    from concourse.bass_utils import run_bass_kernel_spmd

    x = {k: np.asarray(v) for k, v in inputs.items()}
    tbl = shape_tables()

    def rows(*parts):
        return np.concatenate([np.ascontiguousarray(p).reshape(-1, P) for p in parts], 0)

    arrays = {
        "x": x["x"][0], "tbl": tbl,
        "rows1": rows(x["norm_g"], x["hg_lower_bound"], x["ev_hg_norm_g"], x["ev_ret_norm_g"], x["od_conv_w"],
                      x["od_conv_b"], x["od_ml_norm_g"]),
        "rows2": rows(x["c_2"], x["norm_g_2"], x["b_ada_2"], x["conv_w_2"], x["final_g_2"]),
        "rel_bias": x["rel_bias_2"], "gate_b": x["od_gate_b"].reshape(1, 8),
        "ev_w_in": x["ev_w_in"][0], "ev_w_out": x["ev_w_out"][0], "od_w_in": x["od_w_in"][0],
        "od_w_out": x["od_w_out"][0], "mlp_w1_0": x["mlp_w1"][0], "mlp_w1_1": x["mlp_w1"][1],
        "mlp_w2_0": x["mlp_w2"][0], "mlp_w2_1": x["mlp_w2"][1], "w_ada": x["w_ada_2"][0], "w_in": x["w_in_2"][0],
        "w_o_attn": x["w_o_attn_2"][0], "w_o_conv": x["w_o_conv_2"][0], "w_out": x["w_out_2"][0],
    }
    arrays = {f"in_{k}": np.ascontiguousarray(v) for k, v in arrays.items()}
    nc = bacc.Bacc("TRN2", target_bir_lowering=False, num_devices=1)
    aps = {k[3:]: nc.dram_tensor(k, v.shape, mybir.dt.from_np(v.dtype), kind="ExternalInput").ap()
           for k, v in arrays.items()}
    out = nc.dram_tensor("out", (SEQ, D), F32, kind="ExternalOutput").ap()
    build(nc, aps, out)
    r = run_bass_kernel_spmd(nc, [arrays], core_ids=[0])
    return r.results[0]["out"].reshape(1, SEQ, D)
```

```python
from contextlib import ExitStack

import numpy as np

import concourse.bass as bass
from concourse import mybir

F32 = mybir.dt.float32
F32R = mybir.dt.float32r
U8 = mybir.dt.uint8
ALU = mybir.AluOpType
ACT = mybir.ActivationFunctionType
AX_X = mybir.AxisListType.X

P = 128
D = 1024
SEQ = 256
KT = D // P
TT = SEQ // P
CHUNK = 64
HEADS = 4
DK = 128
RET_DV = 256
FF = 4096
ATT_HEADS = 8
EPS = 1e-6
CAP = 15.0
QK_SCALE = float(np.float32(128.0) ** -0.5)
MASKED = 1e30

UCOLS = 256
UELEMS = KT * UCOLS
RING = 4
AHEAD = 3

T_COS, T_SIN = 0, 256
T_RET = 512
T_RESET = 1536
T_CAUSAL = 1792
T_UPPER = 2048
T_IDENT = 2176
T_ONEHOT = 2304
T_MASKS = 2560
T_END = 3584
LEVELS = (64, 32, 16, 8, 4, 2, 1)

R_NORM = 0
R_LOWER = 64
R_HG, R_RET = 76, 77
R_CONVW, R_CONVB = 79, 111
R_ML = 119
ROWS1 = 121
R2_C, R2_NORM, R2_BADA, R2_CONVW = 0, 8, 16, 40
ROWS2 = 64


def shape_tables():
    f32 = np.float32
    tbl = np.zeros((P, T_END), f32)
    half = P // 2
    inv = (f32(10000.0) ** (-np.arange(half, dtype=f32) / f32(half))).astype(f32)
    ang = (np.arange(SEQ, dtype=f32)[:, None] * inv[None, :]).astype(f32)
    cos, sin = np.cos(ang).T, np.sin(ang).T
    tbl[:half, T_COS:T_COS + SEQ] = cos
    tbl[half:, T_COS:T_COS + SEQ] = cos
    tbl[:half, T_SIN:T_SIN + SEQ] = sin
    tbl[half:, T_SIN:T_SIN + SEQ] = -sin
    s = np.arange(P, dtype=np.float64)[:, None]
    t = np.arange(SEQ, dtype=np.float64)[None, :]
    for h in range(HEADS):
        log_g = np.log1p(-np.exp2(-5.0 - h))
        dec = np.where(t >= s, np.exp(log_g * np.maximum(t - s, 0.0)), 0.0)
        tbl[:, T_RET + h * SEQ:T_RET + (h + 1) * SEQ] = dec * float(DK) ** -0.5
    tbl[:, T_RESET:T_RESET + SEQ] = (np.arange(SEQ) % CHUNK != 0)[None, :]
    tbl[:, T_CAUSAL:T_CAUSAL + SEQ] = np.where(t >= s, 0.0, MASKED)
    tbl[:, T_UPPER:T_UPPER + P] = t[:, :P] >= s
    tbl[:, T_IDENT:T_IDENT + P] = np.eye(P)
    n = np.arange(SEQ)
    large = 16 + (np.log(np.maximum(n, 1).astype(f32) / f32(16)) / f32(np.log(8.0)) * f32(16)).astype(np.int32)
    bucket = np.where(n < 16, n, np.minimum(large, 31))
    tbl[:32, T_ONEHOT:T_ONEHOT + SEQ] = np.arange(32)[:, None] == bucket[None, :]
    masks = np.zeros((P, len(LEVELS) + 1, P), f32)
    i = np.arange(P)
    for n_level, m in enumerate(LEVELS):
        same = (i[:, None] // (2 * m)) == (i[None, :] // (2 * m))
        masks[:, n_level] = same & (i[:, None] % (2 * m) < m) & (i[None, :] % (2 * m) >= m)
    masks[:, len(LEVELS)] = np.eye(P)
    tbl[:, T_MASKS:T_END] = masks.reshape(P, -1)
    return tbl


QK_ORDER = (0, 2, 1, 3)


def weight_units():
    A, B = "A", "B"
    us = []

    def cols(w, c0, n, role):
        us.extend((A, w, c0 + UCOLS * i, role, i) for i in range(n // UCOLS))

    def rows(w, n, role):
        us.extend((B, w, 2 * P * i, role, i) for i in range(n // (2 * P)))

    cols("ev_w_in", 512, 512, "hf")
    cols("ev_w_in", 0, 512, "hq")
    cols("ev_w_in", 1024, 512, "hi")
    cols("ev_w_in", 2048, 512, "rq")
    cols("ev_w_in", 2560, 512, "rk")
    cols("ev_w_in", 3072, 1024, "rv")
    cols("ev_w_in", 4096, 1024, "rgate")
    cols("ev_w_in", 1536, 512, "hgate")
    us.extend(("B", "ev_w_out", (512 + 2 * P * i) % 1536, "out0", i) for i in range(6))
    mlp(us, 0)
    cols("od_w_in", 1024, 1024, "mv")
    us.extend((A, "od_w_in", UCOLS * QK_ORDER[i], "mqk", i) for i in range(4))
    cols("od_w_in", 2048, 1024, "mog")
    rows("od_w_out", 1024, "out2")
    mlp(us, 1)
    cols("w_in", 0, 1024, "aq")
    cols("w_in", 1024, 1024, "ak")
    cols("w_in", 2048, 1024, "av")
    cols("w_in", 3072, 1024, "ag")
    for c in range(4):
        for role, c0 in (("cc", 5120), ("cx", 6144), ("cb", 4096), ("cg", 7168)):
            us.append((A, "w_in", c0 + UCOLS * c, role, c))
    rows("w_o_conv", 1024, "out4")
    cols("w_in", 9216, 1024, "mc")
    cols("w_in", 8192, 1024, "ma")
    rows("w_o_attn", 1024, "out5")
    rows("w_out", 1024, "out6")
    return us


def mlp(us, layer):
    for j in range(9):
        if 2 <= j < 8:
            us.append(("C", "w_ada", UCOLS * (6 * layer + j - 2), "ada", 6 * layer + j - 2))
        if j < 8:
            us.extend(("A", f"mlp_w1_{layer}", 512 * j + UCOLS * i, f"up{layer}", 2 * j + i) for i in range(2))
        if j >= 1:
            us.extend(("B", f"mlp_w2_{layer}", 512 * (j - 1) + 2 * P * i, f"out{2 * layer + 1}", 2 * (j - 1) + i)
                      for i in range(2))


UNITS = weight_units()
NU = len(UNITS)
A_OF = {}
SPLIT_OF = {}
for _u, _it in enumerate(UNITS):
    if _it[0] == "A":
        A_OF[_u] = len(A_OF)
    if _it[0] != "C":
        SPLIT_OF[_u] = len(SPLIT_OF)
LOW_OF = {}
for _u in range(NU):
    _by = "ada" if _u not in SPLIT_OF else "dve" if SPLIT_OF[_u] % 2 == 1 or _u == 0 else "pool"
    LOW_OF[_u] = (_by, 1 + sum(_b == _by for _b, _ in LOW_OF.values()))
EVAC = {"hf": "act", "hq": "act", "hi": "act", "rq": "dve", "rk": "dve", "rv": "act", "hgate": "act",
        "rgate": "act", "up0": "dve", "up1": "dve", "mqk": "dve", "mv": "act", "mog": "dve",
        "aq": "act", "ak": "act", "av": "act", "ag": "act", "cc": "act", "cx": "dve", "cb": "dve",
        "cg": "act", "mc": "act", "ma": "act"}
FORM = {r: "F" for r in EVAC} | {"hi": "T", "rv": "T", "mv": "T", "av": "T"}
EVAC_UNITS = {e: [u for u in A_OF if EVAC[UNITS[u][3]] == e] for e in ("act", "dve")}
A_UNITS = list(A_OF)
PHASE = {f"out{p}": p for p in range(7)}
PHASE_KT = (12, 32, 8, 32, 8, 8, 8)


def at(role, i=0):
    return next(u for u, it in enumerate(UNITS) if it[3] == role and it[4] == i)


def last_of(role):
    return max(u for u, it in enumerate(UNITS) if it[3] == role)


def build(nc, a, out):
    ctx = ExitStack()
    with ctx:
        cursor = [(nc.sbuf_base + 63) // 64 * 64]

        def place(name, shape, dt, at_byte=None):
            size = int(np.prod(shape[1:])) * (1 if dt == U8 else 4)
            if at_byte is None:
                at_byte = cursor[0]
                cursor[0] += (size + 31) // 32 * 32
            return nc.alloc_sbuf_tensor_at(name, list(shape), dt, offset=at_byte)

        raw = place("raw", (P, RING, UELEMS), F32)
        wh = place("wh", (P, RING, UELEMS), F32R)
        wl = place("wl", (P, RING, UELEMS), F32R)
        xT = place("xT", (P, KT, SEQ), F32)
        hh = place("hh", (P, KT, SEQ), F32R)
        hl = place("hl", (P, KT, SEQ), F32R)
        y_at = cursor[0]
        yh = place("yh", (P, 12, SEQ), F32R)
        yl = place("yl", (P, 12, SEQ), F32R)
        scr1 = place("scr1", (P, 4, 512), F32, y_at + 4096)
        scr2 = place("scr2", (P, 4, 512), F32, y_at + 12288 + 4096)
        work = place("work", (P, KT, SEQ), F32)
        arena = place("arena", (P, 11264), F32)
        tables = place("tables", (P, 1792), F32)
        masks_at = cursor[0]
        masks = place("masks", (P, 8, P), U8)
        bias = place("bias", (P, ATT_HEADS, SEQ), F32, masks_at - 7168)
        ident = place("ident", (P, P), F32)
        col1 = place("col1", (P, ROWS1), F32)
        col2 = place("col2", (P, ROWS2), F32)
        wg = place("wg", (P, KT, 8), F32)
        mod = place("mod", (P, 24), F32)
        cf = place("cf", (P, KT), F32)
        ones = place("ones", (P, 1), F32)
        eps = place("eps", (P, 1), F32)
        sd = place("sd", (P, 16), F32)
        rs = place("rs", (P, 16), F32)
        lb = place("lb", (P, 3, HEADS), F32)
        lbs = place("lbs", (P, 4, HEADS), F32)
        gz = place("gz", (P, 2, 8), F32)
        gzb = place("gzb", (P, 8), F32)
        gcap = place("gcap", (P, 2, 8), F32)
        glf = place("glf", (P, 2, 4), F32)
        gB = place("gB", (P, 2, 4), F32)
        gg = place("gg", (P, 2, 4), F32)
        gm = place("gm", (P, 2, 4), F32)
        gden = place("gden", (P, 2, 4), F32)
        gdi = place("gdi", (P, 2, 4), F32)
        gc = place("gc", (P, 8), F32)
        gs = place("gs", (P, KT), F32)
        mx = place("mx", (P, 2, 2), F32)
        sm = place("sm", (P, 2, 2), F32)
        assert cursor[0] <= nc.sbuf_usable_end, (cursor[0], nc.sbuf_usable_end)

        PS = [ctx.enter_context(nc.psum_tensor(f"bank{i}", [P, 512], F32)) for i in range(8)]
        scratch_dram = nc.dram_tensor("bias_scratch", (ATT_HEADS, 384), F32, kind="Internal").ap()

        names = (
            "raw0 raw1 raw2 raw3 hi lo_dve lo_pool used evac_act evac_dve "
            "d_x d_small d_tables d_causal d_wg d_u d_bias d_out "
            "const d_masks masks cols colsT xin xcopy_dve xcopy_act x0_ssq step_dve lo_ada mod x_dve x_pool yg "
            "xsq xsum ysum xstat xsd xrs xbc h h_part hh hl ysq ystat ysd yrs ybc t x_last acc "
            "low lowe c_act f lf k_hg b diff e q k smm pred hout hev hsq hst hsd hrs "
            "rope rmm rsum rdec rout rev rst rsd rrs y_src yh yl_pool yl_dve sq "
            "conv og msum gmm gz gcap gsp gbm g gT M Mb fls fl warg w msc ms mout mev mst mvar msd mc mbc qk "
            "u asc lg mxn gle aexp p tr pt aout aout_v mcm merged acc_free4 acc_free5 d_gain "
            "fin_mm fin_ssq fin_sum fin_g fin_sd fin_rs fin_dve fin_act"
        ).split()
        S = {n: ctx.enter_context(nc.semaphore("s_" + n)) for n in names}
        raw_sem = [S["raw0"], S["raw1"], S["raw2"], S["raw3"]]
        block = ctx.enter_context(nc.Block())

        wf = work[:, :, :].rearrange("p k t -> p (k t)")
        ar = arena[:, :]

        def view(lo, *dims):
            v = ar[:, lo:lo + int(np.prod(dims))]
            if len(dims) == 1:
                return v
            if len(dims) == 2:
                return v.rearrange("p (a b) -> p a b", a=dims[0])
            return v.rearrange("p (a b c) -> p a b c", a=dims[0], b=dims[1])

        x_in = view(8192, TT, D)
        rows1, rows2 = ar[:, 10240:10368], ar[:, 10368:10496]
        rel_in, onehot = ar[0:32, 10496:10504], ar[0:32, 10512:10768]
        u_row = ar[0:ATT_HEADS, 10768:11152]
        g_qk = view(0, HEADS, 2, SEQ)
        g_b = view(2048, HEADS * SEQ)
        g_v = view(3072, TT, 512)
        g_gate = view(4096, HEADS * SEQ)
        r_qk = view(5120, HEADS, 2, SEQ)
        r_v = view(7168, TT, D)
        r_gate = view(9216, KT, SEQ)
        r_o = view(7168, HEADS, 2, SEQ)
        r_p = view(5120, HEADS, 512)
        r_row = view(5120, HEADS * SEQ)
        g_o, g_sq = view(0, HEADS * SEQ), view(1024, HEADS * SEQ)
        g_lf = scr1[:, 0:2, :].rearrange("p a b -> p (a b)")
        cosT, sinT = tables[:, 0:SEQ], tables[:, SEQ:2 * SEQ]
        ret_dec = tables[:, T_RET:T_RET + HEADS * SEQ].rearrange("p (h t) -> p h t", h=HEADS)
        reset = tables[:, T_RESET:T_RESET + SEQ]
        m_qk = view(0, 2 * HEADS, SEQ)
        m_v = view(2048, TT, D)
        m_og = view(4096, KT, SEQ)
        m_w = view(6144, HEADS, 384)
        m_s = view(7680, HEADS, 384)
        m_o = view(9216, KT, SEQ)
        m_sq = view(0, HEADS, 512)
        m_raw = view(9216, 2, 2, SEQ)
        causal, upper = tables[:, 0:SEQ], tables[:, SEQ:SEQ + P]
        gT, MT = wf[0:HEADS, 0:SEQ], wf[0:HEADS, SEQ:2 * SEQ]
        a_q, a_k = view(0, KT, SEQ), view(2048, KT, SEQ)
        a_v, a_g = view(4096, TT, D), view(6144, KT, SEQ)
        c_y = view(8192, KT, SEQ)
        c_u, c_t = view(10240, 512), view(10752, 512)
        o_ma, o_mc = view(0, KT, SEQ), view(2048, KT, SEQ)
        y_conv = c_y
        fin_t, fin_gain = view(0, TT, D), view(4096, D)
        yg = view(0, KT, SEQ)
        xsq = view(2048, KT, SEQ)
        xsq_rows = view(2048, TT, D)
        items = [(half, lv) for half in range(2) for lv in range(9)]

        def mod_part(i):
            return view(4096 + UCOLS * (i % 2), UCOLS)

        PRENORM = {at("hf"): 0, at("up0"): 1, at("mv"): 2, at("up1"): 3, at("aq"): 4}

        ITEM_UNITS = [at("hi", 1) + n for n, c in enumerate((1, 1, 1, 1, 1, 2, 2, 2, 2, 2, 2, 1)) for _ in range(c)]
        assert len(ITEM_UNITS) == len(items)
        SCAN_END = ITEM_UNITS[-1]

        def items_of(u):
            return [j for j in range(len(items)) if ITEM_UNITS[j] == u]

        def decays_to(i):
            return sum(lv != 7 for _, lv in items[:i + 1])

        X_ORDER = (2, 0, 3, 1)

        def x_pairs(n):
            return X_ORDER if 1 <= n <= 4 else (0, 1, 2, 3)

        def x_tiles(n):
            return [2 * b + g for b in x_pairs(n) for g in range(2)]

        LATE = (1, 2, 3)
        x_row = {1: view(10240, SEQ), 2: tables[:, 384:384 + SEQ], 3: view(10240, SEQ)}

        def x_rms(n):
            return x_row[n].unsqueeze(1).broadcast_to([P, 2, SEQ])

        def a_unit(h):
            return at("cc") - 1 + (3 * h) // 2

        def fin_bank(t, half):
            return PS[2 * t + half]

        def acc_group(g):
            return PS[4 + g // 2][:, (g % 2) * SEQ:(g % 2 + 1) * SEQ]

        def y_pairs_before(p, mlp_too):
            return sum(PHASE_KT[q] // 2 for q in range(p) if mlp_too or q not in (1, 3))

        def y_source(p, i):
            if p == 0:
                return view(9216 + 512 * i, 512) if i < 4 else view(512 * (i - 4), 512)
            base = {2: 4096, 4: 8192, 5: 6144, 6: 0}[p]
            return view(base + 512 * i, 512)

        def wait_acc(eng, p, b):
            if b < 3:
                eng.wait_ge(S["acc"], 7 * p + 2 * b + 2)
            else:
                wait_used(eng, last_of(f"out{p}"))

        def flat2(t, i):
            return t[:, 2 * i:2 * i + 2, :].rearrange("p k t -> p (k t)")

        def evac_value(u):
            return EVAC_UNITS[EVAC[UNITS[u][3]]].index(u) + 1

        def wait_evac(eng, u):
            eng.wait_ge(S["evac_act"] if EVAC[UNITS[u][3]] == "act" else S["evac_dve"], evac_value(u))

        def wait_used(eng, u):
            eng.wait_ge(S["used"], u + 1)

        def split_by(u):
            return LOW_OF[u][0]

        def wait_low(eng, u):
            eng.wait_ge(S["lo_" + LOW_OF[u][0]], LOW_OF[u][1])

        def unit_src(u):
            kind, w, c0, _, _ = UNITS[u]
            src = a[w]
            if kind != "B":
                return src[:, c0:c0 + UCOLS].rearrange("(k p) c -> p k c", p=P)
            return src[c0:c0 + 2 * P, :].rearrange("(k p) c -> p k c", p=P)

        def slot(t, u, kind):
            return t[:, u % RING, :].rearrange("p (k c) -> p k c", k=2 if kind == "B" else KT)

        def bank(u):
            return PS[A_OF[u] % 2]

        @block.sync
        def _(eng):
            small = (
                (ident[:, :], a["tbl"][:, T_IDENT:T_IDENT + P]),
                (rows1[0:ROWS1, :], a["rows1"]),
                (rows2[0:ROWS2, :], a["rows2"]),
                (rel_in, a["rel_bias"]),
                (onehot, a["tbl"][0:32, T_ONEHOT:T_ONEHOT + SEQ]),
            )
            for dst, src in small:
                eng.dma_start(dst, src).then_inc(S["d_small"], 16)
            eng.dma_start(x_in, a["x"].rearrange("(t p) d -> p t d", p=P)).then_inc(S["d_x"], 16)
            for u in range(NU):
                if u == 1:
                    eng.dma_start(g_lf, a["tbl"][:, T_MASKS:T_END]).then_inc(S["d_masks"], 16)
                if u == RING:
                    eng.dma_start(tables[:, :], a["tbl"][:, 0:T_CAUSAL]).then_inc(S["d_tables"], 16)
                    eng.dma_start(wg[:, :, :],
                                  a["od_w_in"][:, 3072:3080].rearrange("(k p) c -> p k c", p=P)).then_inc(S["d_wg"], 16)
                    eng.dma_start(gzb[:, :], a["gate_b"].broadcast_to([P, 8])).then_inc(S["d_wg"], 16)
                if u == at("mv"):
                    eng.wait_ge(S["y_src"], 6)
                    eng.dma_start(tables[:, 0:384], a["tbl"][:, T_CAUSAL:T_CAUSAL + 384]).then_inc(S["d_causal"], 16)
                if u == at("out5"):
                    eng.wait_ge(S["aout"], ATT_HEADS)
                    eng.dma_start(fin_gain, a["final_gain"].broadcast_to([P, D])).then_inc(S["d_gain"], 16)
                if u == at("aq"):
                    eng.wait_ge(S["warg"], HEADS)
                    eng.wait_ge(S["gbm"], 1)
                    eng.wait_ge(S["d_u"], 16)
                    src = scratch_dram
                    eng.dma_start(bias[:, :, :], bass.AP(tensor=src.tensor, offset=src.offset,
                                                         ap=[[1, P], [384, ATT_HEADS], [1, SEQ]])).then_inc(S["d_bias"], 16)
                if u >= RING:
                    wait_low(eng, u - RING)
                eng.dma_start(slot(raw, u, UNITS[u][0]), unit_src(u)).then_inc(raw_sem[u % RING], 16)
            for t, done in enumerate((S["fin_dve"], S["fin_act"])):
                eng.wait_ge(done, 2)
                eng.dma_start(out[t * P:(t + 1) * P, :], fin_t[:, t, :]).then_inc(S["d_out"], 16)
            eng.wait_ge(S["d_out"], 32)

        @block.tensor
        def _(eng):
            def mm(o, l, r, start, stop):
                return eng.matmul(o, l, r, start=start, stop=stop, skip_group_check=True)

            def a_first(u, norm):
                w_hi, w_lo, o = slot(wh, u, "A"), slot(wl, u, "A"), bank(u)

                def both(w, h, k, first=False, last=False):
                    for g in range(2):
                        c, dst = slice(g * P, (g + 1) * P), o[:, g * SEQ:(g + 1) * SEQ]
                        if FORM[UNITS[u][3]] == "F":
                            m = mm(dst, w[:, k, c], h[:, k, :], first and g == 0, last)
                        else:
                            m = mm(dst, h[:, k, c], w[:, k, :], first and g == 0, last)
                    return m

                for j, k in enumerate(x_tiles(norm)):
                    eng.wait_ge(S["hh"], KT * norm + j + 1)
                    both(w_hi, hh, k, first=j == 0)
                wait_low(eng, u)
                for k in x_tiles(norm):
                    both(w_lo, hh, k)
                for j, k in enumerate(x_tiles(norm)):
                    eng.wait_ge(S["hl"], KT * norm + j + 1)
                    m = both(w_hi, hl, k, last=j == KT - 1)
                m.then_inc(S["used"], 1)

            def a_forward(u, between):
                role, i = UNITS[u][3:]
                w_hi, w_lo, o = slot(wh, u, "A"), slot(wl, u, "A"), bank(u)
                for g in range(2):
                    if g == 1 and between is not None:
                        between()
                    for k in range(KT):
                        first, last = k == 0, k == KT - 1
                        c = slice(g * P, (g + 1) * P)
                        if FORM[role] == "F":
                            dst = o[:, g * SEQ:(g + 1) * SEQ]
                            mm(dst, w_hi[:, k, c], hh[:, k, :], first, False)
                            mm(dst, w_hi[:, k, c], hl[:, k, :], False, False)
                            m = mm(dst, w_lo[:, k, c], hh[:, k, :], False, last)
                        else:
                            dst = o[:, g * UCOLS:(g + 1) * UCOLS]
                            mm(dst, hh[:, k, c], w_hi[:, k, :], first, False)
                            mm(dst, hh[:, k, c], w_lo[:, k, :], False, False)
                            m = mm(dst, hl[:, k, c], w_hi[:, k, :], False, last)
                m.then_inc(S["used"], 1)

            def mod_sums(u):
                i = UNITS[u][4]
                part = mod_part(i)
                for g in range(2):
                    m = mm(PS[2][:, 8 + 2 * i + g:9 + 2 * i + g], part[:, g * P:(g + 1) * P], ones[:, :], True, True)
                m.then_inc(S["used"], 1)

            def b_forward(u):
                role, i = UNITS[u][3:]
                p = PHASE[role]
                w_hi, w_lo = slot(wh, u, "B"), slot(wl, u, "B")
                kt = 2 * i if p not in (1, 3) else 2 * (i % 4)
                end = i == PHASE_KT[p] // 2 - 1
                for g in range(KT):
                    c = slice(g * P, (g + 1) * P)
                    dst = acc_group(g)
                    if p == 6 and i == 0 and g % 2 == 0:
                        eng.wait_ge(S["acc_free5"], g // 2 + 1)
                    for k in range(2):
                        mm(dst, w_hi[:, k, c], yh[:, kt + k, :], i == 0 and k == 0 and g % 2 == 0, False)
                        mm(dst, w_hi[:, k, c], yl[:, kt + k, :], False, False)
                        m = mm(dst, w_lo[:, k, c], yh[:, kt + k, :], False, end and k == 1)
                    if end and g < KT - 1:
                        m.then_inc(S["acc"], 1)
                m.then_inc(S["used"], 1)

            def column_sums(stat_col, tiles, first=True, last=True):
                for sq in tiles:
                    for tt in range(TT):
                        m = mm(PS[2][:, stat_col + tt:stat_col + tt + 1], sq[:, tt * P:(tt + 1) * P], ones[:, :],
                               first and sq is tiles[0] and tt == 0, last and sq is tiles[-1])
                return m

            def all_sums(dst, sq, first=True, last=True):
                return mm(dst, ones[:, 0:1].broadcast_to([P, P]), sq, first, last)

            def spread(dst, col):
                return mm(dst, col.broadcast_to([P, P]), ident[:, :], True, True)

            def x_stats(n):
                eng.wait_ge(S["xsum"], n)
                column_sums(0, [xsq[:, x_tiles(n)[0], :]]).then_inc(S["xstat"], 1)

            def x_spread(n):
                eng.wait_ge(S["xrs"], n + 1)
                spread(PS[3][:, 0:P], rs[:, 0:1])
                spread(PS[3][:, P:2 * P], rs[:, 1:2]).then_inc(S["xbc"], 1)

            def prenorm(n):
                x_stats(n)
                x_spread(n)

            def postnorm(n):
                eng.wait_ge(S["ysum"], n + 1)
                column_sums(4, [work[:, 0, :], work[:, 1, :]], last=False)
                eng.wait_ge(S["ysq"], 4 * n + 4)
                column_sums(4, [work[:, 6, :], work[:, 7, :]], first=False).then_inc(S["ystat"], 1)
                eng.wait_ge(S["yrs"], n + 1)
                spread(PS[3][:, 2 * P:3 * P], rs[:, 2:3])
                spread(PS[3][:, 3 * P:4 * P], rs[:, 3:4]).then_inc(S["ybc"], 1)

            eng.wait_ge(S["d_small"], 16 * 5)
            eng.transpose(PS[2][:, 0:ROWS1], rows1[0:ROWS1, :], ident[0:ROWS1, 0:ROWS1])
            eng.transpose(PS[2][:, P:P + ROWS2], rows2[0:ROWS2, :], ident[0:ROWS2, 0:ROWS2])
            mm(PS[3][0:ATT_HEADS, 0:SEQ], rel_in, onehot, True, True).then_inc(S["colsT"], 1)
            eng.wait_ge(S["d_x"], 16)
            for g in range(KT):
                if g == 6:
                    eng.wait_ge(S["cols"], 2)
                    eng.wait_ge(S["u"], 1)
                    x_spread(0)
                for tt in range(TT):
                    m = eng.transpose(PS[4 + g // 2][:, (g % 2) * SEQ + tt * P:(g % 2) * SEQ + (tt + 1) * P],
                                      x_in[:, tt, g * P:(g + 1) * P], ident[:, :])
                if g % 2 == 1:
                    m.then_inc(S["xin"], 1)
            eng.wait_ge(S["const"], 2)

            def level_scores(i):
                half, lv = items[i]
                dst = PS[2 + i % 2]
                if i >= 2:
                    eng.wait_ge(S["pred"], i - 1)
                if lv != 7:
                    eng.wait_ge(S["q"], decays_to(i))
                    eng.wait_ge(S["k"], decays_to(i))
                for h in range(2):
                    for tt in range(TT):
                        if lv == 7:
                            qq, kk = g_qk[:, 2 * half + h, 0, :], g_qk[:, 2 * half + h, 1, :]
                        else:
                            qq = scr1[:, 2 + i % 2, h * SEQ:(h + 1) * SEQ]
                            kk = scr2[:, i % 2, h * SEQ:(h + 1) * SEQ]
                        if lv == 8:
                            if tt == 0:
                                m = mm(dst[:, h * P:(h + 1) * P], kk[:, 0:P], qq[:, P:2 * P], True, True)
                        else:
                            c = slice(tt * P, (tt + 1) * P)
                            m = mm(dst[:, (2 * h + tt) * P:(2 * h + tt + 1) * P], kk[:, c], qq[:, c], True, True)
                m.then_inc(S["smm"], 1)

            def gated_out():
                eng.wait_ge(S["pred"], len(items))
                for h in range(HEADS):
                    dst = PS[2 + h // 2][:, (h % 2) * SEQ:(h % 2 + 1) * SEQ]
                    v0, v1 = g_v[:, 0, h * DK:(h + 1) * DK], g_v[:, 1, h * DK:(h + 1) * DK]
                    mm(dst[:, 0:P], v0, wf[:, (2 * h) * P:(2 * h + 1) * P], True, True)
                    mm(dst[:, P:2 * P], v0, wf[:, 1024 + h * P:1024 + (h + 1) * P], True, False)
                    m = mm(dst[:, P:2 * P], v1, wf[:, (2 * h + 1) * P:(2 * h + 2) * P], False, True)
                m.then_inc(S["hout"], 1)

            def ret_scores():
                eng.wait_ge(S["rope"], 4)
                for h in range(HEADS):
                    rq, rk = r_qk[:, h, 0, :], r_qk[:, h, 1, :]
                    mm(PS[4 + h][:, 0:SEQ], rk[:, 0:P], rq, True, True)
                    m = mm(PS[4 + h][:, SEQ:SEQ + P], rk[:, P:2 * P], rq[:, P:2 * P], True, True)
                m.then_inc(S["rmm"], 1)

            def values_out(dst, v, c0, probs, last_sem):
                for g in range(2):
                    o = dst[:, g * SEQ:(g + 1) * SEQ]
                    mm(o, v[:, 0, c0 + g * P:c0 + (g + 1) * P], probs[:, 0:SEQ], True, False)
                    m = mm(o[:, P:2 * P], v[:, 1, c0 + g * P:c0 + (g + 1) * P], probs[:, SEQ:SEQ + P], False, True)
                m.then_inc(last_sem, 1)

            def head_sums(dst, sq_of, groups):
                for h in range(HEADS):
                    for tt in range(TT):
                        for g in range(groups):
                            m = mm(dst[:, 2 * h + tt:2 * h + tt + 1], sq_of(h, g)[:, tt * P:(tt + 1) * P], ones[:, :],
                                   g == 0, g == groups - 1)
                return m

            def head_spread(dst_of, cols):
                for h in range(HEADS):
                    for tt in range(TT):
                        m = spread(dst_of(h)[:, tt * P:(tt + 1) * P], cols[:, 2 * h + tt:2 * h + tt + 1])
                return m

            def gate_products():
                eng.wait_ge(S["d_wg"], 32)
                eng.wait_ge(S["h"], 3 * KT)
                for tt in range(TT):
                    for k in range(KT):
                        m = mm(PS[4][:, 8 * tt:8 * tt + 8], work[:, k, tt * P:(tt + 1) * P], wg[:, k, :],
                               k == 0, k == KT - 1)
                m.then_inc(S["gmm"], 1)

            def gate_cumsum():
                eng.wait_ge(S["gsp"], 1)
                eng.wait_ge(S["d_causal"], 16)
                o = PS[4]
                mm(o[:, 32:36], upper, glf[:, 0, :], True, True)
                mm(o[:, 36:40], ones[:, 0:1].broadcast_to([P, P]), glf[:, 0, :], True, False)
                mm(o[:, 36:40], upper, glf[:, 1, :], False, True).then_inc(S["gbm"], 1)

            def gate_rows():
                eng.wait_ge(S["g"], 1)
                for tt in range(TT):
                    m = eng.transpose(PS[7][0:HEADS, tt * P:(tt + 1) * P], gg[:, tt, :], ident[:, :])
                m.then_inc(S["gT"], 1)

            def gate_max():
                eng.wait_ge(S["M"], 1)
                for h in range(HEADS):
                    m = mm(PS[5 + h // 2][:, (h % 2) * SEQ:(h % 2 + 1) * SEQ],
                           ident[0:HEADS, h:h + 1].broadcast_to([HEADS, P]), MT, True, True)
                for tt in range(TT):
                    m = eng.transpose(PS[7][:, 256 + 4 * tt:260 + 4 * tt], MT[:, tt * P:(tt + 1) * P],
                                      ident[0:HEADS, 0:HEADS])
                m.then_inc(S["Mb"], 1)

            def ml_scores(h):
                eng.wait_ge(S["qk"], 2 if h < 2 else 4)
                if h >= 2:
                    eng.wait_ge(S["ms"], h - 1)
                q, k, o = m_qk[:, h, :], m_qk[:, HEADS + h, :], PS[2 + h % 2]
                mm(o[:, 0:SEQ], k[:, 0:P], q, True, True)
                mm(o[:, SEQ:SEQ + P], k[:, P:2 * P], q[:, P:2 * P], True, True).then_inc(S["msc"], 1)

            def ml_out(h):
                eng.wait_ge(S["ms"], h + 1)
                wait_evac(eng, last_of("mv"))
                if h == 0:
                    eng.wait_ge(S["warg"], HEADS)
                if h >= 2:
                    eng.wait_ge(S["mev"], 2 * (h - 1))
                s = m_s[:, h, :]
                mm(PS[4][:, 64 + h:65 + h], s[:, 0:P], ones[:, :], True, True)
                mm(PS[4][:, 68 + h:69 + h], s[:, P:2 * P], ones[:, :], True, False)
                mm(PS[4][:, 68 + h:69 + h], s[:, SEQ:SEQ + P], ones[:, :], False, True)
                values_out(PS[5 + h % 2], m_v, h * RET_DV, s, S["mout"])

            def ml_spread():
                eng.wait_ge(S["mc"], 1)
                head_spread(lambda h: PS[2 + h // 2][:, (h % 2) * SEQ:(h % 2 + 1) * SEQ],
                            gc[:, :]).then_inc(S["mbc"], 1)

            def att_scores(h):
                if h == 0:
                    wait_evac(eng, last_of("ak"))
                if h >= 2:
                    eng.wait_ge(S["lg"], h - 1)
                q, k, o = a_q[:, h, :], a_k[:, h, :], PS[2 + h % 2]
                mm(o[:, 0:P], q[:, 0:P], k[:, 0:P], True, True)
                mm(o[:, P:P + SEQ], q[:, P:2 * P], k, True, True).then_inc(S["asc"], 1)

            def att_turn(h):
                eng.wait_ge(S["p"], h + 1)
                if h >= 2:
                    eng.wait_ge(S["pt"], h - 1)
                pr = wf[:, 384 * (h % 2):384 * (h % 2 + 1)]
                for j in range(3):
                    m = eng.transpose(PS[4 + h % 2][:, j * P:(j + 1) * P], pr[:, j * P:(j + 1) * P], ident[:, :])
                m.then_inc(S["tr"], 1)

            def att_out(h):
                eng.wait_ge(S["pt"], h + 1)
                if h >= 2:
                    eng.wait_ge(S["aout_v"], h - 1)
                pt, o = wf[:, 768 + 384 * (h % 2):768 + 384 * (h % 2 + 1)], PS[6 + h % 2]
                mm(o[:, 0:SEQ], a_v[:, 0, h * P:(h + 1) * P], pt[:, 0:SEQ], True, False)
                mm(o[:, P:2 * P], a_v[:, 1, h * P:(h + 1) * P], pt[:, SEQ:SEQ + P], False, True).then_inc(S["aout"], 1)

            for u in range(NU):
                kind, _, _, role, i = UNITS[u]
                if role in ("up0", "mv", "up1", "aq") and i == 0:
                    n = ("up0", "mv", "up1", "aq").index(role)
                    postnorm(n)
                    if n + 1 not in LATE:
                        prenorm(n + 1)
                if kind != "C":
                    eng.wait_ge(S["hi"], SPLIT_OF[u] + 1)
                if u not in PRENORM:
                    wait_low(eng, u)
                if kind == "A":
                    if A_OF[u] >= 2:
                        wait_evac(eng, A_UNITS[A_OF[u] - 2])
                    if u in PRENORM:
                        a_first(u, PRENORM[u])
                    else:
                        a_forward(u, {at("mog", 3): ml_spread,
                                      at("up0", 1): lambda: x_spread(1), at("mv", 1): lambda: x_spread(2),
                                      at("up1", 1): lambda: x_spread(3)}.get(u))
                elif kind == "C":
                    mod_sums(u)
                else:
                    p = PHASE[role]
                    if p in (1, 3):
                        eng.wait_ge(S["yl_dve"], (p // 2) * 16 + i + 1)
                    else:
                        eng.wait_ge(S["yl_pool"], y_pairs_before(p, False) + i + 1)
                    if i == 0 and p == 4:
                        eng.wait_ge(S["aout_v"], ATT_HEADS)
                    if i == 0 and p == 5:
                        eng.wait_ge(S["acc_free4"], 4)
                    b_forward(u)

                if PRENORM.get(u) in LATE:
                    x_stats(PRENORM[u])
                for j in items_of(u):
                    level_scores(j)
                if u == at("rv"):
                    ret_scores()
                if u == at("rgate"):
                    wait_evac(eng, last_of("rv"))
                    for h in range(HEADS):
                        eng.wait_ge(S["rdec"], h + 1)
                        values_out(PS[4 + h], r_v, h * RET_DV, r_p[:, h, :], S["rout"])
                if u == at("rgate", 2):
                    eng.wait_ge(S["rsum"], 1)
                    for h in range(HEADS):
                        m = all_sums(PS[5 + h // 2][:, (h % 2) * SEQ:(h % 2 + 1) * SEQ], r_qk[:, h, 0, :])
                    m.then_inc(S["rst"], 1)
                if u == at("rgate", 3):
                    gated_out()
                if u == at("hgate"):
                    eng.wait_ge(S["hsq"], 1)
                    for h in range(HEADS):
                        m = all_sums(PS[2 + h // 2][:, (h % 2) * SEQ:(h % 2 + 1) * SEQ], g_sq[:, h * SEQ:(h + 1) * SEQ])
                    m.then_inc(S["hst"], 1)

                if u == at("mv", 1):
                    gate_products()
                if u == at("mv", 3):
                    gate_cumsum()
                if u == at("mqk"):
                    gate_rows()
                if u == at("mqk", 1):
                    gate_max()
                for h in range(HEADS):
                    if u == at("mqk", 3) + h // 2:
                        ml_scores(h)
                for h in range(HEADS):
                    if u == at("mog", h // 2):
                        ml_out(h)
                if u == at("mog", 2):
                    eng.wait_ge(S["msum"], HEADS)
                    eng.wait_ge(S["fls"], 1)
                    head_sums(PS[7], lambda h, g: m_sq[:, h, 0:SEQ], 1).then_inc(S["mst"], 1)

                for h in range(ATT_HEADS):
                    if u == a_unit(h):
                        att_scores(h)
                    if u == a_unit(h) + 3:
                        att_turn(h)
                    if u == a_unit(h) + 4:
                        att_out(h)

            for g in range(KT):
                eng.wait_ge(S["x_last"], g + 1)
                for tt in range(TT):
                    m = eng.transpose(fin_bank(tt, g // 4)[:, (g % 4) * P:(g % 4 + 1) * P],
                                      xT[:, g, tt * P:(tt + 1) * P], ident[:, :])
                if g % 4 == 3:
                    m.then_inc(S["fin_mm"], 1)

        @block.vector
        def _(eng):
            steps = [0]

            def link(ins):
                steps[0] += 1
                ins.then_inc(S["step_dve"], 1)
                eng.wait_ge(S["step_dve"], steps[0])

            def tt(o, x, y, op):
                return eng.tensor_tensor(o, x, y, op)

            def ts(o, x, c1, c2, op0, op1=ALU.bypass):
                return eng.tensor_scalar(o, x, c1, c2, op0, op1)

            def stt(o, x, c, y, op0, op1):
                return eng.scalar_tensor_tensor(out=o, in0=x, scalar=c, in1=y, op0=op0, op1=op1)

            def split(u):
                eng.wait_ge(raw_sem[u % RING], 16 * (u // RING + 1))
                eng.wait_ge(S["hi"], SPLIT_OF[u] + 1)
                if u >= RING:
                    wait_used(eng, u - RING)
                tt(wl[:, u % RING, :], raw[:, u % RING, :], wh[:, u % RING, :].bitcast(F32),
                   ALU.subtract).then_inc(S["lo_dve"], 1)

            def mod_rows(u):
                eng.wait_ge(raw_sem[u % RING], 16 * (u // RING + 1))
                wait_used(eng, u - RING)
                eng.wait_ge(S["c_act"], 1)
                w, o = slot(raw, u, "C"), mod_part(UNITS[u][4])
                link(ts(o, w[:, 0, :], cf[:, 0:1], None, ALU.mult))
                for k in range(1, KT - 1):
                    link(stt(o, w[:, k, :], cf[:, k:k + 1], o, ALU.mult, ALU.add))
                stt(o, w[:, KT - 1, :], cf[:, KT - 1:KT], o, ALU.mult, ALU.add).then_inc(S["lo_ada"], 1)

            def gain(n, g):
                if n < 4:
                    c = R_NORM + 32 * (n // 2) + 16 * (n % 2) + g
                    return col1[:, c:c + 1]
                return gs[:, g:g + 1]

            def fold(sq, order, done, n, out):
                first = pair_of(sq, order[0])
                eng.wait_ge(done, 4 * n + 1)
                for j in range(1, 4):
                    eng.wait_ge(done, 4 * n + j + 1)
                    link(tt(first, first, pair_of(sq, order[j]), ALU.add))
                tt(first[:, 0:SEQ], first[:, 0:SEQ], first[:, SEQ:2 * SEQ], ALU.add).then_inc(out, 1)

            def x_root(n):
                eng.wait_ge(S["xsd"], n + 1)
                eng.reciprocal(rs[:, 0:2], sd[:, 0:2]).then_inc(S["xrs"], 1)

            def prenorm(n):
                if n in LATE:
                    for j, g in enumerate(x_tiles(n)):
                        if j % 4 == 0:
                            eng.wait_ge(S["x_pool"], 2 * (n - 1) + j // 4 + 1)
                        if j % 4 == 2:
                            eng.wait_ge(S["x_dve"], 2 * (n - 1) + j // 4 + 1)
                        ts(work[:, g, :], xT[:, g, :], gain(n, g), None, ALU.mult).then_inc(S["h"], 1)
                    fold(xsq, x_pairs(n), S["xsq"], n - 1, S["xsum"])
                    return
                if n != 0:
                    fold(xsq, x_pairs(n), S["xsq"], n - 1, S["xsum"])
                x_root(n)
                if n == 0:
                    eng.wait_ge(S["xcopy_dve"], 2)
                eng.wait_ge(S["xbc"], n + 1)
                for j, g in enumerate(x_tiles(n)):
                    if n == 0 and g % 2 == 0 and g >= 4:
                        eng.wait_ge(S["xcopy_act"], g // 2 - 1)
                    stt(work[:, g, :], xT[:, g, :], gain(n, g), PS[3][:, 0:SEQ], ALU.mult, ALU.mult).then_inc(
                        S["h"] if n == 0 else S["h_part"], 1)
                if n == 4:
                    for j, g in enumerate(x_tiles(n)):
                        eng.wait_ge(S["h_part"], j + 1)
                        eng.wait_ge(S["hh"], KT * n + j + 1)
                        stt(hl[:, g, :], work[:, g, :], mod[:, g:g + 1], hh[:, g, :].bitcast(F32), ALU.add,
                            ALU.subtract).then_inc(S["hl"], 1)

            def pair_of(t, b):
                return t[:, 2 * b:2 * b + 2, :].rearrange("p k t -> p (k t)")

            def scale_y(n, j):
                b = X_ORDER[j]
                eng.wait_ge(S["yg"], 4 * n + j + 1)
                tt(yg[:, 2 * b:2 * b + 2, :], yg[:, 2 * b:2 * b + 2, :],
                   PS[3][:, SEQ:2 * SEQ].unsqueeze(1).broadcast_to([P, 2, SEQ]), ALU.mult).then_inc(S["t"], 1)

            def postnorm(n):
                eng.wait_ge(S["ysq"], 4 * n + 2)
                link(tt(pair_of(work, 0), pair_of(work, 0), pair_of(work, 1), ALU.add))
                eng.wait_ge(S["ysq"], 4 * n + 3)
                tt(pair_of(work, 0), pair_of(work, 0), pair_of(work, 2), ALU.add).then_inc(S["ysum"], 1)
                eng.wait_ge(S["ysd"], n + 1)
                eng.reciprocal(rs[:, 2:4], sd[:, 2:4]).then_inc(S["yrs"], 1)
                eng.wait_ge(S["ybc"], n + 1)
                scale_y(n, 0)
                scale_y(n, 1)
                scale_y(n, 2)
                for j in (1, 3):
                    if j == 3:
                        scale_y(n, 3)
                    eng.wait_ge(S["t"], 4 * n + j + 1)
                    tt(pair_of(xT, X_ORDER[j]), pair_of(xT, X_ORDER[j]), pair_of(yg, X_ORDER[j]), ALU.add).then_inc(S["x_dve"], 1)

            eng.memset(ones[:, :], 1.0).then_inc(S["const"], 1)
            eng.memset(eps[:, :], EPS).then_inc(S["const"], 1)
            link(eng.memset(u_row, -MASKED))
            eng.wait_ge(S["colsT"], 1)
            tensor = eng.tensor_copy
            tensor(col1[:, :], PS[2][:, 0:ROWS1]).then_inc(S["cols"], 1)
            tensor(col2[:, :], PS[2][:, P:P + ROWS2]).then_inc(S["cols"], 1)
            tensor(u_row[:, P - 1:P - 1 + SEQ], PS[3][0:ATT_HEADS, 0:SEQ]).then_inc(S["u"], 1)
            eng.wait_ge(S["cols"], 2)
            low = [col1[:, R_LOWER + HEADS * r:R_LOWER + HEADS * (r + 1)] for r in range(3)]
            link(tt(lbs[:, 2, :], low[0], low[1], ALU.max))
            link(tt(lbs[:, 2, :], lbs[:, 2, :], low[2], ALU.max))
            for r in range(3):
                tt(lb[:, r, :], low[r], lbs[:, 2, :], ALU.subtract).then_inc(S["low"], 1)
            for b in range(2):
                eng.wait_ge(S["xin"], b + 1)
                tensor(xT[:, 2 * b:2 * b + 2, :], PS[4 + b][:, :].rearrange("p (k t) -> p k t", k=2)).then_inc(S["xcopy_dve"], 1)
            prenorm(0)

            def rope(u):
                i, which = UNITS[u][4], 0 if UNITS[u][3] == "rq" else 1
                dst = r_qk[:, 2 * i:2 * i + 2, which, :]
                tmp = scr2[:, 2 + i % 2, :].rearrange("p (h t) -> p h t", h=2)
                ps = bank(u)[:, :].rearrange("p (h t) -> p h t", h=2)
                half = P // 2

                def both(x):
                    return x.unsqueeze(1).broadcast_to([x.shape[0], 2, SEQ])

                if i == 0 and which == 0:
                    eng.wait_ge(S["d_tables"], 16)
                link(tt(dst, ps, both(cosT), ALU.mult))
                link(tt(tmp[0:half], ps[half:P], both(sinT[half:P]), ALU.mult))
                tt(tmp[half:P], ps[0:half], both(sinT[0:half]), ALU.mult).then_inc(S["evac_dve"], 1)
                eng.wait_ge(S["evac_dve"], evac_value(u))
                tt(dst, dst, tmp, ALU.add).then_inc(S["rope"], 1)

            def conv_taps(u):
                i = UNITS[u][4]
                pair = QK_ORDER[i]
                ps = m_raw[:, i % 2, :, :]
                tt(ps, bank(u)[:, :].rearrange("p (h t) -> p h t", h=2), x_rms(2), ALU.mult).then_inc(S["evac_dve"], 1)
                eng.wait_ge(S["evac_dve"], evac_value(u))
                for j in range(4):
                    for g in range(2):
                        c = 2 * pair + g
                        w = col1[:, R_CONVW + 8 * (3 - j) + c:R_CONVW + 8 * (3 - j) + c + 1]
                        y = m_qk[:, c, :]
                        if j == 0:
                            m = ts(y, ps[:, g, :], w, col1[:, R_CONVB + c:R_CONVB + c + 1], ALU.mult, ALU.add)
                        else:
                            m = stt(y[:, j:], ps[:, g, 0:SEQ - j], w, y[:, j:], ALU.mult, ALU.add)
                    if j < 3:
                        link(m)
                m.then_inc(S["conv"], 1)

            def short_conv(u):
                i = UNITS[u][4]
                eng.wait_ge(S["evac_act"], evac_value(u - 1))
                tt(c_u, bank(u)[:, :], c_u, ALU.mult).then_inc(S["evac_dve"], 1)
                eng.wait_ge(S["evac_dve"], evac_value(u))
                for j in range(3):
                    for g in range(2):
                        kt = 2 * i + g
                        w = col2[:, R2_CONVW + 8 * (2 - j) + kt:R2_CONVW + 8 * (2 - j) + kt + 1]
                        x, y = c_u[:, g * SEQ:(g + 1) * SEQ], c_y[:, kt, :]
                        if j == 0:
                            m = ts(y, x, w, None, ALU.mult)
                        else:
                            m = stt(y[:, j:], x[:, 0:SEQ - j], w, y[:, j:], ALU.mult, ALU.add)
                    link(m)

            def level_decays(i):
                half, lv = items[i]
                if lv == 7:
                    return
                if i >= 2 and items[i - 2][1] != 7:
                    eng.wait_ge(S["q"], decays_to(i - 2))
                    eng.wait_ge(S["k"], decays_to(i - 2))
                m = LEVELS[lv] if lv < 7 else 128
                b = g_b[:, half * 512:(half + 1) * 512].rearrange("p (n w) -> p n w", w=2 * m)
                e = scr1[:, i % 2, :].rearrange("p (n w) -> p n w", w=2 * m)
                n = 256 // m

                def at_col(j, w):
                    return b[:, :, j:j + 1].broadcast_to([P, n, w])

                if m < 64:
                    tt(e[:, :, m:2 * m], b[:, :, m:2 * m], at_col(m - 1, m), ALU.subtract)
                    tt(e[:, :, 0:m], at_col(m - 1, m), b[:, :, 0:m], ALU.subtract).then_inc(S["diff"], 1)
                elif m == 64:
                    tensor(e[:, :, 64:128], b[:, :, 64:128])
                    tt(e[:, :, 0:64], at_col(63, 64), b[:, :, 0:64], ALU.subtract).then_inc(S["diff"], 1)
                else:
                    tensor(e[:, :, 128:192], b[:, :, 128:192])
                    tt(e[:, :, 192:256], b[:, :, 192:256], at_col(191, 64), ALU.add)
                    link(tt(e[:, :, 0:64], at_col(63, 64), b[:, :, 0:64], ALU.subtract))
                    tt(e[:, :, 0:64], e[:, :, 0:64], at_col(127, 64), ALU.add)
                    tt(e[:, :, 64:128], at_col(127, 64), b[:, :, 64:128], ALU.subtract).then_inc(S["diff"], 1)

            def level_queries(i):
                half, lv = items[i]
                if lv == 7:
                    return
                eng.wait_ge(S["e"], decays_to(i))
                if i >= 2:
                    eng.wait_ge(S["smm"], i - 1)
                tt(scr1[:, 2 + i % 2, :].rearrange("p (h t) -> p h t", h=2), g_qk[:, 2 * half:2 * half + 2, 0, :],
                   scr1[:, i % 2, :].rearrange("p (h t) -> p h t", h=2), ALU.mult).then_inc(S["q"], 1)

            def level_pick(i):
                half, lv = items[i]
                eng.wait_ge(S["smm"], i + 1)
                if i == 0:
                    eng.wait_ge(S["masks"], 1)
                if i >= 1:
                    eng.wait_ge(S["pred"], i)
                if lv == 8:
                    tensor(wf[:, 1024 + half * SEQ:1024 + (half + 1) * SEQ], PS[2 + i % 2][:, 0:SEQ]).then_inc(S["pred"], 1)
                else:
                    eng.copy_predicated(
                        wf[:, half * 512:(half + 1) * 512].rearrange("p (n t) -> p n t", n=4),
                        masks[:, lv, :].unsqueeze(1).broadcast_to([P, 4, P]),
                        PS[2 + i % 2][:, :].rearrange("p (n t) -> p n t", n=4)).then_inc(S["pred"], 1)

            def att_logits(h):
                eng.wait_ge(S["asc"], h + 1)
                if h == 0:
                    eng.wait_ge(S["d_bias"], 16)
                if h >= 2:
                    eng.wait_ge(S["tr"], h - 1)
                o, ps = wf[:, 384 * (h % 2):384 * (h % 2 + 1)], PS[2 + h % 2]
                stt(o[:, 0:P], ps[:, 0:P], QK_SCALE, bias[:, h, P - 1::-1], ALU.mult, ALU.add)
                stt(o[:, P:P + SEQ], ps[:, P:P + SEQ], QK_SCALE, bias[:, h, SEQ - 1::-1], ALU.mult,
                    ALU.add).then_inc(S["lg"], 1)
                eng.wait_ge(S["lg"], h + 1)
                if h >= 2:
                    eng.wait_ge(S["aexp"], h - 1)
                eng.tensor_reduce(mx[:, h % 2, 0:1], o[:, 0:P], AX_X, ALU.max)
                link(eng.tensor_reduce(mx[:, h % 2, 1:2], o[:, P:P + SEQ], AX_X, ALU.max))
                ts(mx[:, h % 2, :], mx[:, h % 2, :], -1.0, None, ALU.mult).then_inc(S["mxn"], 1)

            def att_norm(h):
                eng.wait_ge(S["aexp"], h + 1)
                o = wf[:, 384 * (h % 2):384 * (h % 2 + 1)]
                link(eng.reciprocal(sm[:, h % 2, :], sm[:, h % 2, :]))
                ts(o[:, 0:P], o[:, 0:P], sm[:, h % 2, 0:1], None, ALU.mult)
                ts(o[:, P:P + SEQ], o[:, P:P + SEQ], sm[:, h % 2, 1:2], None, ALU.mult).then_inc(S["p"], 1)

            def att_gate(h):
                eng.wait_ge(S["aout"], h + 1)
                if h == 0:
                    wait_evac(eng, last_of("ag"))
                tt(a_g[:, h, :], PS[6 + h % 2][:, 0:SEQ], a_g[:, h, :], ALU.mult).then_inc(S["aout_v"], 1)

            def hidden_low(layer, i):
                eng.wait_ge(S["yh"], y_pairs_before(2 * layer + 1, True) + i + 1)
                if i >= RING:
                    wait_used(eng, at(f"out{2 * layer + 1}", i - RING))
                tt(flat2(yl, i % RING), wf[:, 512 * (i % RING):512 * (i % RING + 1)], flat2(yh, i % RING).bitcast(F32),
                   ALU.subtract).then_inc(S["yl_dve"], 1)

            def gate_out(h):
                for g in range(2):
                    m = stt(m_og[:, 2 * h + g, :], m_og[:, 2 * h + g, :], col1[:, R_ML + g:R_ML + g + 1],
                            m_o[:, 2 * h + g, :], ALU.mult, ALU.mult)
                link(m)
                eng.wait_ge(S["mbc"], 1)
                b = PS[2 + h // 2][:, (h % 2) * SEQ:(h % 2 + 1) * SEQ].unsqueeze(1).broadcast_to([P, 2, SEQ])
                tt(m_og[:, 2 * h:2 * h + 2, :], m_og[:, 2 * h:2 * h + 2, :], b, ALU.mult).then_inc(S["y_src"], 1)

            def before(u):
                if u == last_of("out5"):
                    for b in range(4):
                        wait_acc(eng, 5, b)
                        wait_evac(eng, at("ma", b))
                        pair = o_ma[:, 2 * b:2 * b + 2, :].rearrange("p k t -> p (k t)")
                        tt(pair, PS[4 + b][:, :], pair, ALU.mult).then_inc(S["acc_free5"], 1)
                        eng.wait_ge(S["acc_free5"], b + 1)
                        eng.wait_ge(S["mcm"], b + 1)
                        tt(pair, pair, o_mc[:, 2 * b:2 * b + 2, :].rearrange("p k t -> p (k t)"), ALU.add).then_inc(S["merged"], 1)

                for j in items_of(u - 1):
                    level_pick(j)
                for j in items_of(u):
                    level_queries(j)
                if u == at("rgate"):
                    eng.wait_ge(S["rmm"], 1)
                    for h in range(HEADS):
                        o = r_p[:, h, :]
                        tt(o[:, 0:SEQ], PS[4 + h][:, 0:SEQ], ret_dec[:, h, :], ALU.mult)
                        tt(o[:, SEQ:SEQ + P], PS[4 + h][:, SEQ:SEQ + P], ret_dec[:, h, 0:P], ALU.mult).then_inc(S["rdec"], 1)
                if u == at("rgate", 2):
                    eng.wait_ge(S["rev"], 8)
                    tt(r_qk[:, :, 0, :], r_qk[:, :, 0, :], r_qk[:, :, 1, :], ALU.add).then_inc(S["rsum"], 1)
                if u == at("rgate", 3):
                    eng.wait_ge(S["rsd"], 1)
                    eng.reciprocal(r_row, r_row).then_inc(S["rrs"], 1)
                if u == at("hgate", 1):
                    eng.wait_ge(S["hsd"], 1)
                    eng.reciprocal(g_sq, g_sq).then_inc(S["hrs"], 1)

                if u == at("mv", 2):
                    eng.wait_ge(S["gmm"], 1)
                    eng.wait_ge(S["d_wg"], 32)
                    for t in range(TT):
                        m = stt(gz[:, t, :], PS[4][:, 8 * t:8 * t + 8], rs[:, t:t + 1], gzb[:, :], ALU.mult, ALU.add)
                    m.then_inc(S["gz"], 1)
                    eng.wait_ge(S["gcap"], 1)
                    ts(gz[:, :, :], gcap[:, :, :], CAP, None, ALU.mult).then_inc(S["gz"], 1)
                if u == at("mqk"):
                    eng.wait_ge(S["gbm"], 1)
                    tt(gg[:, :, :], gz[:, :, 0:4], PS[4][:, 32:40].rearrange("p (t j) -> p t j", t=2), ALU.add)
                    tensor(gB[:, :, :], PS[4][:, 32:40].rearrange("p (t j) -> p t j", t=2)).then_inc(S["g"], 1)
                if u == at("mqk", 1):
                    eng.wait_ge(S["gT"], 1)
                    link(tensor(gT, PS[7][0:HEADS, 0:SEQ]))
                    eng.tensor_tensor_scan(MT, gT, gT, 0.0, ALU.max, ALU.max).then_inc(S["M"], 1)
                for h in range(HEADS):
                    if u == at("mog", h // 2):
                        eng.wait_ge(S["msc"], h + 1)
                        eng.wait_ge(S["w"], h + 1)
                        stt(m_s[:, h, :], PS[2 + h % 2][:, 0:384], QK_SCALE, m_w[:, h, :], ALU.mult,
                            ALU.mult).then_inc(S["ms"], 1)
                    if u == at("mqk", 2 + h // 2):
                        if h == 0:
                            eng.wait_ge(S["Mb"], 1)
                            tt(gm[:, :, :], gB[:, :, :], PS[7][:, 256:264].rearrange("p (t j) -> p t j", t=2),
                               ALU.subtract).then_inc(S["fls"], 1)
                        mb = PS[5 + h // 2][:, (h % 2) * SEQ:(h % 2 + 1) * SEQ]
                        stt(m_w[:, h, 0:SEQ], mb, gg[:, 0, h:h + 1], causal, ALU.subtract, ALU.add)
                        stt(m_w[:, h, SEQ:384], mb[:, P:SEQ], gg[:, 1, h:h + 1], causal[:, 0:P], ALU.subtract,
                            ALU.add).then_inc(S["warg"], 1)
                for h in range(HEADS):
                    if u == at("mog", 1 + h // 2):
                        eng.wait_ge(S["mev"], 2 * h + 2)
                        tt(m_sq[:, h, 0:SEQ], m_sq[:, h, 0:SEQ], m_sq[:, h, SEQ:2 * SEQ], ALU.add).then_inc(S["msum"], 1)
                if u == at("mog", 2):
                    eng.wait_ge(S["mout"], 4)
                    link(tensor(gden[:, :, :], PS[4][:, 64:72].rearrange("p (t h) -> p t h", t=2)))
                    link(stt(gdi[:, :, :], gden[:, :, :], -1.0, gden[:, :, :], ALU.mult, ALU.max))
                    eng.wait_ge(S["fl"], 1)
                    link(tt(gdi[:, :, :], gdi[:, :, :], gm[:, :, :], ALU.max))
                    link(eng.reciprocal(gden[:, :, :], gdi[:, :, :]))
                if u == at("mog", 3):
                    eng.wait_ge(S["mst"], 1)
                    by_t = gc[:, :].rearrange("p (h t) -> p t h", t=2)
                    link(tt(by_t, PS[7][:, 0:8].rearrange("p (h t) -> p t h", t=2), gden[:, :, :], ALU.mult))
                    tt(by_t, by_t, gden[:, :, :], ALU.mult).then_inc(S["mvar"], 1)
                    eng.wait_ge(S["msd"], 1)
                    link(eng.reciprocal(rs[:, 0:8], sd[:, 0:8]))
                    tt(by_t, rs[:, 0:8].rearrange("p (h t) -> p t h", t=2), gden[:, :, :], ALU.mult).then_inc(S["mc"], 1)
                    eng.wait_ge(S["og"], HEADS - 1)
                    eng.wait_ge(S["mev"], 8)
                    for h in range(HEADS - 1):
                        gate_out(h)

                for h in range(ATT_HEADS):
                    if u == a_unit(h) + 5:
                        att_gate(h)
                for h in range(ATT_HEADS):
                    if u == a_unit(h) + 3:
                        att_norm(h)
                for h in range(ATT_HEADS):
                    if u == a_unit(h) + 1:
                        att_logits(h)

            for u in range(-AHEAD, NU):
                role, i = UNITS[u][3:] if u >= 0 else ("", 0)
                if role in ("up0", "mv", "up1", "aq") and i == 0:
                    n = ("up0", "mv", "up1", "aq").index(role)
                    postnorm(n)
                    prenorm(n + 1)
                before(u)
                s = u + AHEAD
                if s < NU and split_by(s) == "dve":
                    split(s)
                if s < NU and split_by(s) == "ada":
                    mod_rows(s)
                if u == -1:
                    eng.wait_ge(S["d_masks"], 16)
                    tensor(masks[:, :, :].rearrange("p l t -> p (l t)"), g_lf).then_inc(S["masks"], 1)
                    eng.wait_ge(S["lowe"], 1)
                    link(tt(lbs[:, 2, :], lb[:, 0, :], lb[:, 1, :], ALU.add))
                    link(tt(lbs[:, 2, :], lbs[:, 2, :], lb[:, 2, :], ALU.add))
                    link(eng.reciprocal(lbs[:, 3, :], lbs[:, 2, :]))
                    link(tt(lbs[:, 0, :], lb[:, 0, :], lbs[:, 3, :], ALU.mult))
                    link(ts(lbs[:, 1, :], lbs[:, 0, :], -1.0, 1.0, ALU.mult, ALU.add))
                if u < 0:
                    continue
                if PRENORM.get(u) in LATE:
                    x_root(PRENORM[u])
                    eng.wait_ge(S["xbc"], PRENORM[u] + 1)
                    link(tensor(x_row[PRENORM[u]], PS[3][:, 0:SEQ]))
                if EVAC.get(role) == "dve":
                    wait_used(eng, u)
                if role in ("rq", "rk"):
                    rope(u)
                elif role == "ada":
                    wait_used(eng, u)
                    c = slice(2 * i, 2 * i + 2)
                    tt(mod[:, c], PS[2][:, 8 + 2 * i:10 + 2 * i], col2[:, R2_BADA + 2 * i:R2_BADA + 2 * i + 2],
                       ALU.add).then_inc(S["mod"], 1)
                    if i == 7:
                        eng.wait_ge(S["mod"], 8)
                        link(stt(gs[:, :], mod[:, KT:2 * KT], 1.0, col2[:, R2_NORM:R2_NORM + KT], ALU.add, ALU.mult))
                elif role in ("up0", "up1"):
                    def halves(t):
                        return t.rearrange("p (g t) -> p g t", g=2)

                    stt(halves(wf[:, 512 * (i % RING):512 * (i % RING + 1)]), halves(bank(u)[:, :]), 0.0, x_rms(1 if role == "up0" else 3),
                        ALU.max, ALU.mult).then_inc(S["evac_dve"], 1)
                elif role == "mqk":
                    conv_taps(u)
                elif role == "mog":
                    tt(m_og[:, 2 * i:2 * i + 2, :], bank(u)[:, :].rearrange("p (h t) -> p h t", h=2), x_rms(2),
                       ALU.mult).then_inc(S["evac_dve"], 1)
                elif role == "cx":
                    short_conv(u)
                elif role == "cb":
                    tt(c_y[:, 2 * i:2 * i + 2, :].rearrange("p k t -> p (k t)"), bank(u)[:, :],
                       c_y[:, 2 * i:2 * i + 2, :].rearrange("p k t -> p (k t)"), ALU.mult).then_inc(S["evac_dve"], 1)
                elif role == "cg":
                    wait_evac(eng, u)
                    eng.wait_ge(S["evac_dve"], evac_value(u - 1))
                    pair = c_y[:, 2 * i:2 * i + 2, :].rearrange("p k t -> p (k t)")
                    tt(pair, pair, c_t, ALU.mult).then_inc(S["y_src"], 1)
                v = next((w for w in range(u - 1, -1, -1) if UNITS[w][0] != "C"), None)
                if role != "ada" and v is not None and UNITS[v][3] in ("up0", "up1"):
                    hidden_low(0 if UNITS[v][3] == "up0" else 1, UNITS[v][4])

                if u == at("hf", 1):
                    wait_evac(eng, u)
                    for h in range(HEADS):
                        m = ts(g_b[:, h * SEQ:(h + 1) * SEQ], g_qk[:, h, 1, :], lbs[:, 1, h:h + 1], lbs[:, 0, h:h + 1],
                               ALU.mult, ALU.add)
                    m.then_inc(S["f"], 1)
                    eng.wait_ge(S["f"], 1)
                    ts(g_qk[:, :, 1, :], g_b.rearrange("p (h t) -> p h t", h=HEADS), -1.0, 1.0, ALU.mult,
                       ALU.add).then_inc(S["k_hg"], 1)
                    eng.wait_ge(S["hl"], KT)
                    link(eng.memset(wf[:, 0:1024], 0.0))
                if u == at("hq"):
                    eng.wait_ge(S["lf"], 1)
                    eng.wait_ge(S["k_hg"], 1)
                    eng.wait_ge(S["d_tables"], 16)
                    for h in range(HEADS):
                        c = slice(h * SEQ, (h + 1) * SEQ)
                        m = eng.tensor_tensor_scan(g_b[:, c], reset, g_lf[:, c], 0.0, ALU.mult, ALU.add)
                    m.then_inc(S["b"], 1)
                    eng.wait_ge(S["b"], 1)
                if u == at("hq", 1):
                    wait_evac(eng, u)
                for j in items_of(u + 1):
                    level_decays(j)
                if u == at("hgate"):
                    wait_evac(eng, u - 1)
                    eng.wait_ge(S["rrs"], 1)
                    for h in range(HEADS):
                        b = r_row[:, h * SEQ:(h + 1) * SEQ].unsqueeze(1).broadcast_to([P, 2, SEQ])
                        for g in range(2):
                            m = stt(r_gate[:, 2 * h + g, :], r_gate[:, 2 * h + g, :], col1[:, R_RET + g:R_RET + g + 1],
                                    r_o[:, h, g, :], ALU.mult, ALU.mult)
                        link(m)
                        tt(r_gate[:, 2 * h:2 * h + 2, :], r_gate[:, 2 * h:2 * h + 2, :], b, ALU.mult).then_inc(S["y_src"], 1)
                if u == at("hgate", 1):
                    wait_evac(eng, u)
                    for b in range(2):
                        c = slice(512 * b, 512 * (b + 1))
                        link(stt(g_gate[:, c], g_gate[:, c], col1[:, R_HG:R_HG + 1], g_o[:, c], ALU.mult, ALU.mult))
                        if b == 0:
                            eng.wait_ge(S["hrs"], 1)
                        tt(g_o[:, c], g_gate[:, c], g_sq[:, c], ALU.mult).then_inc(S["y_src"], 1)

                if u == last_of("mog"):
                    eng.wait_ge(S["og"], HEADS)
                    gate_out(HEADS - 1)
                if u == last_of("out4"):
                    eng.wait_ge(S["yl_pool"], y_pairs_before(5, False))
                    for b in range(4):
                        wait_acc(eng, 4, b)
                        tensor(y_conv[:, 2 * b:2 * b + 2, :].rearrange("p k t -> p (k t)"), PS[4 + b][:, :]).then_inc(S["acc_free4"], 1)
                if role == "mc":
                    wait_evac(eng, u)
                    eng.wait_ge(S["acc_free4"], i + 1)
                    tt(o_mc[:, 2 * i:2 * i + 2, :], o_mc[:, 2 * i:2 * i + 2, :], y_conv[:, 2 * i:2 * i + 2, :],
                       ALU.mult).then_inc(S["mcm"], 1)

            for g in range(KT):
                if g % 2 == 0:
                    wait_acc(eng, 6, g // 2)
                stt(xT[:, g, :], acc_group(g), mod[:, 2 * KT + g:2 * KT + g + 1], xT[:, g, :], ALU.mult,
                    ALU.add).then_inc(S["x_last"], 1)
            eng.wait_ge(S["d_gain"], 16)

            def times_gain(half, t):
                eng.wait_ge(S["fin_ssq"], 2 * half + t + 1)
                c = slice(512 * half, 512 * (half + 1))
                tt(fin_t[:, t, c], fin_bank(t, half)[:, :], fin_gain[:, c], ALU.mult).then_inc(S["fin_g"], 1)

            times_gain(0, 0)
            times_gain(0, 1)
            times_gain(1, 0)
            eng.wait_ge(S["fin_ssq"], 4)
            tt(sd[:, 8:10], sd[:, 4:6], sd[:, 6:8], ALU.add).then_inc(S["fin_sum"], 1)
            times_gain(1, 1)
            eng.wait_ge(S["fin_sd"], 1)
            eng.reciprocal(rs[:, 8:10], sd[:, 10:12]).then_inc(S["fin_rs"], 1)
            eng.wait_ge(S["fin_rs"], 1)
            eng.wait_ge(S["fin_g"], 3)
            for half in range(2):
                c = slice(512 * half, 512 * (half + 1))
                ts(fin_t[:, 0, c], fin_t[:, 0, c], rs[:, 8:9], None, ALU.mult).then_inc(S["fin_dve"], 1)

        @block.scalar
        def _(eng):
            def act(o, x, f, **more):
                return eng.activation(o, x, f, **more)

            def high(u):
                eng.wait_ge(raw_sem[u % RING], 16 * (u // RING + 1))
                if u >= RING:
                    wait_used(eng, u - RING)
                eng.copy(wh[:, u % RING, :], raw[:, u % RING, :]).then_inc(S["hi"], 1)

            def root(o, stat, n):
                return act(o, stat, ACT.Sqrt, scale=1.0 / n, bias=eps[:, 0:1])

            def wait_x(n, j):
                if j % 2 == 0:
                    eng.wait_ge(S["x_pool"], 2 * (n - 1) + j // 2 + 1)
                else:
                    eng.wait_ge(S["x_dve"], 2 * (n - 1) + j // 2 + 1)

            def x_root(n):
                eng.wait_ge(S["xstat"], n)
                root(sd[:, 0:2], PS[2][:, 0:2], D).then_inc(S["xsd"], 1)

            def prenorm(n):
                if n in LATE:
                    for j, g in enumerate(x_tiles(n)):
                        if j % 2 == 0:
                            wait_x(n, j // 2)
                        c = R_NORM + 32 * (n // 2) + 16 * (n % 2) + g
                        act(hh[:, g, :], xT[:, g, :], ACT.Copy, scale=col1[:, c:c + 1]).then_inc(S["hh"], 1)
                if n == 0:
                    eng.wait_ge(S["d_x"], 16)
                    for t in range(TT):
                        act(xsq_rows[:, t, :], x_in[:, t, :], ACT.Square,
                            accum_out=sd[:, 4 + t:5 + t]).then_inc(S["x0_ssq"], 1)
                    eng.wait_ge(S["x0_ssq"], 2)
                    root(sd[:, 0:2], sd[:, 4:6], D).then_inc(S["xsd"], 1)
                    for b in (2, 3):
                        if b == 3:
                            high(0)
                        eng.wait_ge(S["xin"], b + 1)
                        eng.copy(flat2(xT, b), PS[4 + b][:, :]).then_inc(S["xcopy_act"], 1)
                    for g in range(KT):
                        eng.wait_ge(S["h"], g + 1)
                        eng.copy(hh[:, g, :], work[:, g, :]).then_inc(S["hh"], 1)
                    high(1)
                    return
                for j, b in enumerate(x_pairs(n)):
                    wait_x(n, j)
                    act(flat2(xsq, b), flat2(xT, b), ACT.Square).then_inc(S["xsq"], 1)
                if n in LATE:
                    return
                x_root(n)
                for j, g in enumerate(x_tiles(n)):
                    eng.wait_ge(S["h_part"], j + 1)
                    act(hh[:, g, :], work[:, g, :], ACT.Identity, bias=mod[:, g:g + 1]).then_inc(S["hh"], 1)

            def postnorm(n):
                for b in range(4):
                    wait_acc(eng, n, b)
                    act(work[:, 2 * b:2 * b + 2, :].rearrange("p k t -> p (k t)"), PS[4 + b][:, :],
                        ACT.Square).then_inc(S["ysq"], 1)
                for j, b in enumerate(X_ORDER):
                    if j == 2:
                        eng.wait_ge(S["ystat"], n + 1)
                        root(sd[:, 2:4], PS[2][:, 4:6], D).then_inc(S["ysd"], 1)
                    for g in (2 * b, 2 * b + 1):
                        c = R_NORM + 32 * (n // 2) + 16 * (n % 2) + 8 + g
                        m = act(yg[:, g, :], acc_group(g), ACT.Copy, scale=col1[:, c:c + 1])
                    m.then_inc(S["yg"], 1)

            def y_high(p, i):
                if p in (0, 2, 4):
                    eng.wait_ge(S["y_src"], {0: 0, 2: 6, 4: 10}[p] + i + 1)
                elif p == 5:
                    eng.wait_ge(S["aout_v"], 2 * i + 2)
                    wait_used(eng, at("out4", i))
                else:
                    eng.wait_ge(S["merged"], i + 1)
                eng.copy(flat2(yh, i), y_source(p, i)).then_inc(S["yh"], 1)

            def load_roots():
                act(sd[:, 15:16], eps[:, :], ACT.Sqrt)

            eng.wait_ge(S["const"], 2)
            load_roots()
            prenorm(0)
            eng.wait_ge(S["u"], 1)
            eng.dma_start(scratch_dram, u_row).then_inc(S["d_u"], 16)

            def before(u):
                if u == at("rgate", 1):
                    eng.wait_ge(S["rout"], 4)
                    for h in range(HEADS):
                        eng.copy(r_o[:, h, :, :].rearrange("p a b -> p (a b)"), PS[4 + h][:, :]).then_inc(S["rev"], 1)
                        act(r_qk[:, h, :, :].rearrange("p a b -> p (a b)"), PS[4 + h][:, :], ACT.Square).then_inc(S["rev"], 1)
                if u == at("rgate", 3):
                    eng.wait_ge(S["rst"], 1)
                    for b in range(2):
                        m = root(r_row[:, 512 * b:512 * (b + 1)], PS[5 + b][:, :], RET_DV)
                    m.then_inc(S["rsd"], 1)

                if u == at("mv", 2):
                    eng.wait_ge(S["gz"], 1)
                    act(gcap[:, :, :], gz[:, :, :], ACT.Tanh, scale=1.0 / CAP).then_inc(S["gcap"], 1)
                    eng.wait_ge(S["gz"], 2)
                    act(glf[:, :, :], gz[:, :, 4:8], ACT.Exp, scale=-1.0).then_inc(S["gle"], 1)
                    eng.wait_ge(S["gle"], 1)
                    act(glf[:, :, :], glf[:, :, :], ACT.Ln, bias=ones[:, 0:1]).then_inc(S["gsp"], 1)
                for h in range(HEADS):
                    if u == at("mqk", 2 + h // 2):
                        if h == 0:
                            eng.wait_ge(S["fls"], 1)
                            act(gm[:, :, :], gm[:, :, :], ACT.Exp).then_inc(S["fl"], 1)
                        eng.wait_ge(S["warg"], h + 1)
                        act(m_w[:, h, :], m_w[:, h, :], ACT.Exp, scale=-1.0).then_inc(S["w"], 1)
                    if u == at("mog", 1 + h // 2):
                        eng.wait_ge(S["mout"], h + 1)
                        eng.wait_ge(S["msc"], HEADS)
                        eng.copy(m_o[:, 2 * h:2 * h + 2, :].rearrange("p k t -> p (k t)"), PS[5 + h % 2][:, :]).then_inc(S["mev"], 1)
                        act(m_sq[:, h, :], PS[5 + h % 2][:, :], ACT.Square).then_inc(S["mev"], 1)
                if u == at("mog", 3):
                    eng.wait_ge(S["mvar"], 1)
                    root(sd[:, 0:8], gc[:, :], RET_DV).then_inc(S["msd"], 1)
                    for j in range(HEADS - 1):
                        y_high(2, j)
                if u == at("hgate", 1):
                    y_high(0, 2)
                    y_high(0, 3)

                for h in range(ATT_HEADS):
                    if u == a_unit(h) + 4:
                        eng.wait_ge(S["tr"], h + 1)
                        if h >= 2:
                            eng.wait_ge(S["aout"], h - 1)
                        eng.copy(wf[:, 768 + 384 * (h % 2):768 + 384 * (h % 2 + 1)], PS[4 + h % 2][:, 0:384]).then_inc(S["pt"], 1)
                for h in range(ATT_HEADS):
                    if u == a_unit(h) + 2:
                        eng.wait_ge(S["mxn"], h + 1)
                        o = wf[:, 384 * (h % 2):384 * (h % 2 + 1)]
                        act(o[:, 0:P], o[:, 0:P], ACT.Exp, bias=mx[:, h % 2, 0:1], accum_out=sm[:, h % 2, 0:1])
                        act(o[:, P:384], o[:, P:384], ACT.Exp, bias=mx[:, h % 2, 1:2],
                            accum_out=sm[:, h % 2, 1:2]).then_inc(S["aexp"], 1)

            for u in range(-AHEAD, NU):
                role, i = UNITS[u][3:] if u >= 0 else ("", 0)
                if role in ("up0", "mv", "up1", "aq") and i == 0:
                    n = ("up0", "mv", "up1", "aq").index(role)
                    postnorm(n)
                    prenorm(n + 1)
                if u + AHEAD in SPLIT_OF and u + AHEAD >= 2:
                    high(u + AHEAD)
                if PRENORM.get(u) in LATE:
                    x_root(PRENORM[u])
                if u == -1:
                    eng.wait_ge(S["low"], 3)
                    act(lb[:, :, :], lb[:, :, :], ACT.Exp).then_inc(S["lowe"], 1)
                before(u)
                if u < 0:
                    continue
                if EVAC.get(role) == "act":
                    wait_used(eng, u)
                ps = bank(u)[:, :] if u in A_OF else None
                pair = ps.rearrange("p (h t) -> p h t", h=2) if u in A_OF else None
                if role == "hf":
                    act(g_qk[:, 2 * i:2 * i + 2, 1, :], pair, ACT.Sigmoid).then_inc(S["evac_act"], 1)
                elif role == "hq":
                    act(g_qk[:, 2 * i:2 * i + 2, 0, :], pair, ACT.Silu).then_inc(S["evac_act"], 1)
                    if i == 1:
                        act(cf[:, :], col2[:, R2_C:R2_C + KT], ACT.Silu).then_inc(S["c_act"], 1)
                elif role == "hi":
                    eng.copy(g_v[:, :, i * UCOLS:(i + 1) * UCOLS], pair).then_inc(S["evac_act"], 1)
                elif role == "rv":
                    eng.copy(r_v[:, :, i * UCOLS:(i + 1) * UCOLS], pair).then_inc(S["evac_act"], 1)
                elif role == "hgate":
                    act(g_gate[:, 512 * i:512 * (i + 1)], ps, ACT.Silu).then_inc(S["evac_act"], 1)
                elif role == "rgate":
                    if i == 0:
                        eng.wait_ge(S["d_u"], 16)
                    act(r_gate[:, 2 * i:2 * i + 2, :], pair, ACT.Silu).then_inc(S["evac_act"], 1)
                elif role == "mv":
                    if i == 0:
                        eng.wait_ge(S["xrs"], 3)
                    for t in range(TT):
                        m = act(m_v[:, t, i * UCOLS:(i + 1) * UCOLS], pair[:, t, :], ACT.Copy, scale=rs[:, t:t + 1])
                    m.then_inc(S["evac_act"], 1)
                elif role == "mog":
                    eng.wait_ge(S["evac_dve"], evac_value(u))
                    act(m_og[:, 2 * i:2 * i + 2, :], m_og[:, 2 * i:2 * i + 2, :], ACT.Sigmoid).then_inc(S["og"], 1)
                elif role in ("aq", "ak"):
                    eng.copy((a_q if role == "aq" else a_k)[:, 2 * i:2 * i + 2, :], pair).then_inc(S["evac_act"], 1)
                elif role == "av":
                    eng.copy(a_v[:, :, i * UCOLS:(i + 1) * UCOLS], pair).then_inc(S["evac_act"], 1)
                elif role == "ag":
                    act(a_g[:, 2 * i:2 * i + 2, :], pair, ACT.Silu).then_inc(S["evac_act"], 1)
                elif role == "cc":
                    eng.wait_ge(S["y_src"], 10 + i)
                    eng.copy(c_u, ps).then_inc(S["evac_act"], 1)
                elif role == "cg":
                    if i >= 1:
                        eng.wait_ge(S["y_src"], 10 + i)
                    act(c_t, ps, ACT.Silu).then_inc(S["evac_act"], 1)
                elif role in ("mc", "ma"):
                    if i == 0:
                        eng.wait_ge(S["asc"], ATT_HEADS)
                    act((o_mc if role == "mc" else o_ma)[:, 2 * i:2 * i + 2, :], pair, ACT.Sigmoid).then_inc(S["evac_act"], 1)
                elif role in ("up0", "up1"):
                    layer = 0 if role == "up0" else 1
                    c = slice(512 * (i % RING), 512 * (i % RING + 1))
                    eng.wait_ge(S["evac_dve"], evac_value(u))
                    act(wf[:, c], wf[:, c], ACT.Square).then_inc(S["sq"], 1)
                    eng.wait_ge(S["sq"], 16 * layer + i + 1)
                    if i >= RING:
                        wait_used(eng, at(f"out{2 * layer + 1}", i - RING))
                    eng.copy(flat2(yh, i % RING), wf[:, c]).then_inc(S["yh"], 1)
                elif role == "mqk":
                    eng.wait_ge(S["conv"], i + 1)
                    c = slice(2 * QK_ORDER[i], 2 * QK_ORDER[i] + 2)
                    act(m_qk[:, c, :], m_qk[:, c, :], ACT.Silu).then_inc(S["qk"], 1)

                if u == at("hf", 1):
                    eng.wait_ge(S["f"], 1)
                    eng.wait_ge(S["masks"], 1)
                    act(g_lf, g_b, ACT.Ln).then_inc(S["lf"], 1)
                for j in items_of(u + 1):
                    if items[j][1] != 7:
                        eng.wait_ge(S["diff"], decays_to(j))
                        act(scr1[:, j % 2, :], scr1[:, j % 2, :], ACT.Exp).then_inc(S["e"], 1)
                if u == at("rgate", 3):
                    eng.wait_ge(S["hout"], 1)
                    for b in range(2):
                        eng.copy(g_o[:, 512 * b:512 * (b + 1)], PS[2 + b][:, :]).then_inc(S["hev"], 1)
                        m = act(g_sq[:, 512 * b:512 * (b + 1)], PS[2 + b][:, :], ACT.Square)
                    m.then_inc(S["hsq"], 1)
                if u == at("hgate"):
                    eng.wait_ge(S["hst"], 1)
                    for b in range(2):
                        m = root(g_sq[:, 512 * b:512 * (b + 1)], PS[2 + b][:, :], DK)
                    m.then_inc(S["hsd"], 1)
                    y_high(0, 0)
                    y_high(0, 1)
                if u == at("hgate", 1):
                    y_high(0, 4)
                    y_high(0, 5)

                if u == last_of("mog"):
                    y_high(2, HEADS - 1)
                if u in (last_of("out0") - 1, last_of("out2") - 1, last_of("out6") - 1):
                    load_roots()
                if role == "cg":
                    y_high(4, i)
                if role == "mc":
                    y_high(5, i)
                if u == last_of("out5"):
                    for j in range(4):
                        y_high(6, j)

            for half in range(2):
                eng.wait_ge(S["fin_mm"], half + 1)
                for t in range(TT):
                    act(xsq_rows[:, t, 512 * half:512 * (half + 1)], fin_bank(t, half)[:, :], ACT.Square,
                        accum_out=sd[:, 4 + 2 * half + t:5 + 2 * half + t]).then_inc(S["fin_ssq"], 1)
            eng.wait_ge(S["fin_sum"], 1)
            root(sd[:, 10:12], sd[:, 8:10], D).then_inc(S["fin_sd"], 1)
            eng.wait_ge(S["fin_rs"], 1)
            eng.wait_ge(S["fin_g"], 4)
            for half in range(2):
                c = slice(512 * half, 512 * (half + 1))
                act(fin_t[:, 1, c], fin_t[:, 1, c], ACT.Copy, scale=rs[:, 9:10]).then_inc(S["fin_act"], 1)

        @block.gpsimd
        def _(eng):
            def split(u):
                eng.wait_ge(raw_sem[u % RING], 16 * (u // RING + 1))
                eng.wait_ge(S["hi"], SPLIT_OF[u] + 1)
                if u >= RING:
                    wait_used(eng, u - RING)
                eng.tensor_tensor(wl[:, u % RING, :], raw[:, u % RING, :], wh[:, u % RING, :].bitcast(F32),
                                  ALU.subtract).then_inc(S["lo_pool"], 1)

            def prenorm(n):
                if n == 4:
                    return
                for j, g in enumerate(x_tiles(n)):
                    eng.wait_ge(S["h"], KT * n + j + 1)
                    eng.wait_ge(S["hh"], KT * n + j + 1)
                    eng.tensor_tensor(hl[:, g, :], work[:, g, :], hh[:, g, :].bitcast(F32), ALU.subtract).then_inc(S["hl"], 1)

            def postnorm(n):
                for j in (0, 2):
                    eng.wait_ge(S["t"], 4 * n + j + 1)
                    eng.tensor_tensor(flat2(xT, X_ORDER[j]), flat2(xT, X_ORDER[j]), flat2(yg, X_ORDER[j]),
                                      ALU.add).then_inc(S["x_pool"], 1)

            def y_low(p, i):
                eng.wait_ge(S["yh"], y_pairs_before(p, True) + i + 1)
                eng.tensor_tensor(flat2(yl, i), y_source(p, i), flat2(yh, i).bitcast(F32), ALU.subtract).then_inc(S["yl_pool"], 1)

            prenorm(0)
            for u in range(-AHEAD, NU):
                role, i = UNITS[u][3:] if u >= 0 else ("", 0)
                if role in ("up0", "mv", "up1", "aq") and i == 0:
                    n = ("up0", "mv", "up1", "aq").index(role)
                    postnorm(n)
                    prenorm(n + 1)
                for j in items_of(u):
                    if items[j][1] != 7:
                        half = items[j][0]
                        eng.wait_ge(S["e"], decays_to(j))
                        if j >= 2:
                            eng.wait_ge(S["smm"], j - 1)
                        eng.tensor_tensor(scr2[:, j % 2, :].rearrange("p (h t) -> p h t", h=2),
                                          g_qk[:, 2 * half:2 * half + 2, 1, :],
                                          scr1[:, j % 2, :].rearrange("p (h t) -> p h t", h=2), ALU.mult).then_inc(S["k"], 1)
                if u == last_of("out5"):
                    for j in range(4):
                        y_low(6, j)
                s = u + AHEAD
                if s < NU and split_by(s) == "pool":
                    split(s)
                if u < 0:
                    continue
                if u == at("hgate"):
                    y_low(0, 0)
                    y_low(0, 1)
                if u == at("hgate", 1):
                    for j in range(2, 6):
                        y_low(0, j)
                if u == last_of("mog"):
                    for j in range(4):
                        y_low(2, j)
                if role == "cg":
                    y_low(4, i)
                if role == "mc":
                    y_low(5, i)


def kernel(**inputs):
    from concourse import bacc
    from concourse.bass_utils import run_bass_kernel_spmd

    x = {k: np.asarray(v) for k, v in inputs.items()}
    tbl = shape_tables()

    def rows(*parts):
        return np.concatenate([np.ascontiguousarray(p).reshape(-1, P) for p in parts], 0)

    arrays = {
        "x": x["x"][0], "tbl": tbl,
        "rows1": rows(x["norm_g"], x["hg_lower_bound"], x["ev_hg_norm_g"], x["ev_ret_norm_g"], x["od_conv_w"],
                      x["od_conv_b"], x["od_ml_norm_g"]),
        "rows2": rows(x["c_2"], x["norm_g_2"], x["b_ada_2"], x["conv_w_2"]),
        "final_gain": x["final_g_2"].reshape(1, D),
        "rel_bias": x["rel_bias_2"], "gate_b": x["od_gate_b"].reshape(1, 8),
        "ev_w_in": x["ev_w_in"][0], "ev_w_out": x["ev_w_out"][0], "od_w_in": x["od_w_in"][0],
        "od_w_out": x["od_w_out"][0], "mlp_w1_0": x["mlp_w1"][0], "mlp_w1_1": x["mlp_w1"][1],
        "mlp_w2_0": x["mlp_w2"][0], "mlp_w2_1": x["mlp_w2"][1], "w_ada": x["w_ada_2"][0], "w_in": x["w_in_2"][0],
        "w_o_attn": x["w_o_attn_2"][0], "w_o_conv": x["w_o_conv_2"][0], "w_out": x["w_out_2"][0],
    }
    arrays = {f"in_{k}": np.ascontiguousarray(v) for k, v in arrays.items()}
    nc = bacc.Bacc("TRN2", target_bir_lowering=False, num_devices=1)
    aps = {k[3:]: nc.dram_tensor(k, v.shape, mybir.dt.from_np(v.dtype), kind="ExternalInput").ap()
           for k, v in arrays.items()}
    out = nc.dram_tensor("out", (SEQ, D), F32, kind="ExternalOutput").ap()
    build(nc, aps, out)
    r = run_bass_kernel_spmd(nc, [arrays], core_ids=[0])
    return r.results[0]["out"].reshape(1, SEQ, D)
```
